# Optimizing a Trainium2 kernel written in Bass

```python
import math, functools
import jax, jax.numpy as jnp
from jax import lax
import numpy as np

D_MODEL = 2048
BATCH = 1
SEQ = 512
DEPTH = 1
DEC_BATCH = 8
DEC_SEQ = 4
PAST_LEN = 4096
PAGE_SIZE = 128

N_META = 16
H_A = 4
DH_A = 128
D_A = H_A * DH_A
H_IDX = 16
D_IDX = 64
TOPK_MAX = 256
N_BUCKETS = 32
MAX_DIST = 128
Q_BLOCK = 128
H_B = 12
P_B = 64
D_B = H_B * P_B
N_B = 128
G_B = 2
CONV_W = 4
CONV_B = D_B + 2 * G_B * N_B
H_C = 6
DK_C = 128
DV_C = 128
D_C = H_C * DV_C
CONV_C = 2 * H_C * DK_C + H_C * DV_C
D_MIX = D_A + D_B + D_C
D_FF = 4 * D_MODEL
CHUNK = 64
EPS = 1e-6
ATTN_SCALE = DH_A ** -0.5
IDX_SCALE = (H_IDX * D_IDX) ** -0.5
SPLIT_SIZES = (D_A, D_A, D_A, H_IDX * D_IDX, D_IDX, H_IDX, D_B, CONV_B, H_B, CONV_C, D_C, H_C, H_C)
N_IN = sum(SPLIT_SIZES)

kernel_name = "hybrid_dsa_ssd_gdn_decode_step"

def rmsnorm(x, g):
    xf = x.astype(jnp.float32)
    xf = xf * lax.rsqrt(jnp.mean(xf * xf, axis=-1, keepdims=True) + EPS)
    return xf.astype(x.dtype) * g

def l2norm(x):
    xf = x.astype(jnp.float32)
    xf = xf * lax.rsqrt(jnp.sum(xf * xf, axis=-1, keepdims=True) + EPS)
    return xf.astype(x.dtype)

def t5_bucket(dist):
    max_exact = N_BUCKETS // 2
    d = jnp.maximum(dist, 0)
    log_ratio = jnp.log(jnp.maximum(d, 1).astype(jnp.float32) / max_exact) / math.log(MAX_DIST / max_exact)
    far = max_exact + (log_ratio * (N_BUCKETS - max_exact)).astype(jnp.int32)
    return jnp.where(d < max_exact, d, jnp.minimum(far, N_BUCKETS - 1))

def split_proj(proj):
    points = np.cumsum(np.array(SPLIT_SIZES))[:-1].tolist()
    return jnp.split(proj, points, axis=-1)

def causal_conv_silu(x, buf, w, b):
    T = x.shape[1]
    xp = jnp.concatenate([buf.astype(x.dtype), x], axis=1)
    y = xp[:, 0:T] * w[0]
    for i in range(1, CONV_W):
        y = y + xp[:, i:i + T] * w[i]
    if b is not None:
        y = y + b
    return jax.nn.silu(y), xp[:, T:]

def gather_rows(src, idx):
    return jax.vmap(lambda s, i: s[i])(src, idx)

def indexer_scores(qi, wi, ki):
    s = jax.nn.relu(jnp.einsum('bthd,bsd->bths', qi, ki).astype(jnp.float32))
    return jnp.einsum('bths,bth->bts', s, wi.astype(jnp.float32))

def sparse_attend(q, kg, vg, dist, valid, rel_bias):
    logits = jnp.einsum('bthd,btkhd->bthk', q, kg).astype(jnp.float32)
    bias = jnp.moveaxis(rel_bias[t5_bucket(dist)], -1, 2).astype(jnp.float32)
    logits = jnp.where(valid[:, :, None, :], logits + bias, -jnp.inf)
    p = jax.nn.softmax(logits, axis=-1).astype(vg.dtype)
    return jnp.einsum('bthk,btkhd->bthd', p, vg)

def dsa_prompt(q, k, v, qi, ki, wi, rel_bias, topk):
    Bsz, L = q.shape[:2]
    nblk = -(-L // Q_BLOCK)
    pad = nblk * Q_BLOCK - L

    def blocks(a):
        a = jnp.pad(a, ((0, 0), (0, pad)) + ((0, 0),) * (a.ndim - 2))
        return jnp.moveaxis(a.reshape((Bsz, nblk, Q_BLOCK) + a.shape[2:]), 1, 0)

    qpos = jnp.arange(nblk * Q_BLOCK, dtype=jnp.int32).reshape(nblk, Q_BLOCK)
    kpos = jnp.arange(L, dtype=jnp.int32)

    def one_block(args):
        qb, qib, wib, pb = args
        adm = kpos[None, None, :] <= pb[None, :, None]
        sc = jnp.where(adm, indexer_scores(qib, wib, ki), -jnp.inf)
        _, idx = lax.top_k(sc, topk)
        valid = idx <= pb[None, :, None]
        return sparse_attend(qb, gather_rows(k, idx), gather_rows(v, idx), pb[None, :, None] - idx, valid, rel_bias)

    out = lax.map(one_block, (blocks(q), blocks(qi), blocks(wi), qpos))
    out = jnp.moveaxis(out, 0, 1).reshape(Bsz, nblk * Q_BLOCK, H_A, DH_A)
    return out[:, :L]

def dsa_sample(q, k_new, v_new, qi, ki_new, wi, cache_k, cache_v, cache_kidx, layer, page_table, rel_bias, topk):
    DB, T = q.shape[:2]
    n_pages = PAST_LEN // PAGE_SIZE
    ki_past = cache_kidx[layer, page_table].reshape(DB, n_pages * PAGE_SIZE, D_IDX)
    ki_all = jnp.concatenate([ki_past.astype(ki_new.dtype), ki_new], axis=1)
    qpos = PAST_LEN + jnp.arange(T, dtype=jnp.int32)
    kpos = jnp.arange(PAST_LEN + T, dtype=jnp.int32)
    adm = kpos[None, None, :] <= qpos[None, :, None]
    sc = jnp.where(adm, indexer_scores(qi, wi, ki_all), -jnp.inf)
    _, idx = lax.top_k(sc, topk)
    valid = idx <= qpos[None, :, None]
    is_new = (idx >= PAST_LEN)[..., None, None]
    phys = gather_rows(page_table, jnp.minimum(idx, PAST_LEN - 1) // PAGE_SIZE)
    row = idx % PAGE_SIZE
    new_idx = jnp.clip(idx - PAST_LEN, 0, T - 1)
    kg = jnp.where(is_new, gather_rows(k_new, new_idx), cache_k[layer, phys, row].astype(k_new.dtype))
    vg = jnp.where(is_new, gather_rows(v_new, new_idx), cache_v[layer, phys, row].astype(v_new.dtype))
    return sparse_attend(q, kg, vg, qpos[None, :, None] - idx, valid, rel_bias)

def ssd_chunk_scan(x, dt, A, Bm, Cm, S0, chunk):
    Bsz, T = x.shape[:2]
    nc = T // chunk
    rep = H_B // G_B
    f32 = jnp.float32

    def to_chunks(a):
        return jnp.moveaxis(a.reshape((Bsz, nc, chunk) + a.shape[2:]), 1, 0)

    causal = jnp.tril(jnp.ones((chunk, chunk), dtype=bool))[None, :, :, None]

    def step(S, inp):
        xc, dtc, bc, cc = (a.astype(f32) for a in inp)
        bc = jnp.repeat(bc, rep, axis=2)
        cc = jnp.repeat(cc, rep, axis=2)
        Sf = S.astype(f32)
        cum = jnp.cumsum(dtc * A, axis=1)
        decay = jnp.exp(jnp.where(causal, cum[:, :, None, :] - cum[:, None, :, :], -jnp.inf))
        xdt = xc * dtc[..., None]
        scores = jnp.einsum('bthn,bshn->btsh', cc, bc) * decay
        y = jnp.einsum('btsh,bshp->bthp', scores, xdt) + jnp.einsum('bthn,bhpn->bthp', cc, Sf) * jnp.exp(cum)[..., None]
        w_end = jnp.exp(cum[:, -1:, :] - cum)[..., None]
        S_new = Sf * jnp.exp(cum[:, -1])[:, :, None, None] + jnp.einsum('bshn,bshp->bhpn', bc * w_end, xdt)
        return S_new.astype(S.dtype), y.astype(x.dtype)

    S, ys = lax.scan(step, S0, (to_chunks(x), to_chunks(dt), to_chunks(Bm), to_chunks(Cm)))
    return jnp.moveaxis(ys, 0, 1).reshape(x.shape), S

def mamba2_mixer(xbc_raw, z, dt_raw, conv_buf, S0, conv_w, conv_b, dt_bias, A_log, D_skip, norm_g, plan):
    Bsz, T = xbc_raw.shape[:2]
    xbc, new_buf = causal_conv_silu(xbc_raw, conv_buf, conv_w, conv_b)
    xs, Bm, Cm = jnp.split(xbc, [D_B, D_B + G_B * N_B], axis=-1)
    xh = xs.reshape(Bsz, T, H_B, P_B)
    Bm = Bm.reshape(Bsz, T, G_B, N_B)
    Cm = Cm.reshape(Bsz, T, G_B, N_B)
    dt = jax.nn.softplus((dt_raw + dt_bias).astype(jnp.float32))
    A = -jnp.exp(A_log.astype(jnp.float32))
    S = S0
    ys = []
    start = 0
    for length, chunk in plan:
        sl = slice(start, start + length)
        y_seg, S = ssd_chunk_scan(xh[:, sl], dt[:, sl], A, Bm[:, sl], Cm[:, sl], S, chunk)
        ys.append(y_seg)
        start += length
    y = jnp.concatenate(ys, axis=1) + xh * D_skip[:, None]
    y = (y * jax.nn.silu(z).reshape(Bsz, T, H_B, P_B)).reshape(Bsz, T, G_B, D_B // G_B)
    y = rmsnorm(y, norm_g.reshape(G_B, D_B // G_B))
    return y.reshape(Bsz, T, D_B), new_buf, S

def gdn_chunk_scan(q, k, v, g, beta, S0, chunk):
    Bsz, T = q.shape[:2]
    nc = T // chunk
    f32 = jnp.float32

    def to_chunks(a):
        a = jnp.moveaxis(a, 2, 1)
        return jnp.moveaxis(a.reshape((Bsz, H_C, nc, chunk) + a.shape[3:]), 2, 0)

    incl = jnp.tril(jnp.ones((chunk, chunk), dtype=bool))
    strict = jnp.tril(jnp.ones((chunk, chunk), dtype=bool), -1)
    eye = jnp.eye(chunk, dtype=f32)

    def step(S, inp):
        qc, kc, vc, gc, bc = (a.astype(f32) for a in inp)
        Sf = S.astype(f32)
        cum = jnp.cumsum(gc, axis=-1)
        decay = jnp.exp(jnp.where(incl, cum[..., :, None] - cum[..., None, :], -jnp.inf))
        kk = jnp.einsum('bhik,bhjk->bhij', kc, kc)
        lower = eye + jnp.where(strict, kk * decay, 0.0) * bc[..., :, None]
        rhs = vc * bc[..., None] - jnp.einsum('bhik,bhkv->bhiv', kc * (bc * jnp.exp(cum))[..., None], Sf)
        u = lax.linalg.triangular_solve(lower, rhs, left_side=True, lower=True, unit_diagonal=True)
        qk = jnp.einsum('bhik,bhjk->bhij', qc, kc) * decay
        o = jnp.einsum('bhij,bhjv->bhiv', qk, u) + jnp.einsum('bhik,bhkv->bhiv', qc * jnp.exp(cum)[..., None], Sf)
        last = cum[..., -1:]
        S_new = Sf * jnp.exp(last)[..., None] + jnp.einsum('bhjk,bhjv->bhkv', kc * jnp.exp(last - cum)[..., None], u)
        return S_new.astype(S.dtype), o.astype(q.dtype)

    S, os_ = lax.scan(step, S0, tuple(to_chunks(a) for a in (q, k, v, g, beta)))
    o = jnp.moveaxis(os_, 0, 2).reshape(Bsz, H_C, T, DV_C)
    return jnp.moveaxis(o, 1, 2), S

def gdn_mixer(qkv_raw, z, a_raw, b_raw, conv_buf, S0, conv_w, dt_bias, A_log, norm_g, plan):
    Bsz, T = qkv_raw.shape[:2]
    qkv, new_buf = causal_conv_silu(qkv_raw, conv_buf, conv_w, None)
    q, k, v = jnp.split(qkv, [H_C * DK_C, 2 * H_C * DK_C], axis=-1)
    q = l2norm(q.reshape(Bsz, T, H_C, DK_C)) * (DK_C ** -0.5)
    k = l2norm(k.reshape(Bsz, T, H_C, DK_C))
    v = v.reshape(Bsz, T, H_C, DV_C)
    g = -jnp.exp(A_log.astype(jnp.float32)) * jax.nn.softplus((a_raw + dt_bias).astype(jnp.float32))
    beta = jax.nn.sigmoid(b_raw)
    S = S0
    outs = []
    start = 0
    for length, chunk in plan:
        sl = slice(start, start + length)
        o_seg, S = gdn_chunk_scan(q[:, sl], k[:, sl], v[:, sl], g[:, sl], beta[:, sl], S, chunk)
        outs.append(o_seg)
        start += length
    o = jnp.concatenate(outs, axis=1)
    o = rmsnorm(o, norm_g) * jax.nn.silu(z.reshape(Bsz, T, H_C, DV_C))
    return o.reshape(Bsz, T, D_C), new_buf, S

def trunk_layer(x, lw, attn_fn, ssm_buf, ssm_S, gdn_buf, gdn_S, plan):
    (g_mix, w_in_l, qn, kn, sc_w, sc_b, s_dtb, s_alog, s_d, s_norm,
     gc_w, g_dtb, g_alog, g_norm, w_out_l, g_mlp, w_up_l, w_down_l) = lw
    Bsz, T = x.shape[:2]
    h = rmsnorm(x, g_mix)
    qa, ka, va, qi, ki, wi, zb, xbc, dtb, qkv, zc, a_raw, b_raw = split_proj(h @ w_in_l)
    q = rmsnorm(qa.reshape(Bsz, T, H_A, DH_A), qn) * ATTN_SCALE
    k = rmsnorm(ka.reshape(Bsz, T, H_A, DH_A), kn)
    v = va.reshape(Bsz, T, H_A, DH_A)
    qi = qi.reshape(Bsz, T, H_IDX, D_IDX)
    wi = wi * IDX_SCALE
    o_a = attn_fn(q, k, v, qi, ki, wi)
    o_b, ssm_buf, ssm_S = mamba2_mixer(xbc, zb, dtb, ssm_buf, ssm_S, sc_w, sc_b, s_dtb, s_alog, s_d, s_norm, plan)
    o_c, gdn_buf, gdn_S = gdn_mixer(qkv, zc, a_raw, b_raw, gdn_buf, gdn_S, gc_w, g_dtb, g_alog, g_norm, plan)
    mix = jnp.concatenate([o_a.reshape(Bsz, T, D_A), o_b, o_c], axis=-1)
    x = x + mix @ w_out_l
    hm = rmsnorm(x, g_mlp)
    x = x + jnp.square(jax.nn.relu(hm @ w_up_l)) @ w_down_l
    return x, (k, v, ki, ssm_buf, ssm_S, gdn_buf, gdn_S)

def setup_inputs(seed: int = 0) -> dict:
    key = jax.random.key(seed)
    ks = jax.random.split(key, 30)
    f32 = jnp.float32
    n_pages = PAST_LEN // PAGE_SIZE
    n_used = DEC_BATCH * n_pages
    n_pool = n_used + max(1, n_used // 4)

    def normal(k, shape, scale):
        return jax.random.normal(k, shape, f32) * scale

    def gain(k, shape):
        return 1.0 + 0.05 * jax.random.normal(k, shape, f32)

    def dt_bias(k, shape):
        dt = jnp.exp(jax.random.uniform(k, shape, f32, math.log(1e-3), math.log(1e-1)))
        return dt + jnp.log(-jnp.expm1(-dt))

    def a_log(k, shape):
        return jnp.log(jax.random.uniform(k, shape, f32, 1.0, 16.0))

    page_table = jax.random.permutation(ks[5], n_pool)[:n_used].reshape(DEC_BATCH, n_pages).astype(jnp.int32)
    return {
        "x_prompt": normal(ks[0], (BATCH, SEQ, D_MODEL), 1.0),
        "x_sample": normal(ks[1], (DEC_BATCH, DEC_SEQ, D_MODEL), 1.0),
        "cache_k": normal(ks[2], (DEPTH, n_pool, PAGE_SIZE, H_A, DH_A), 1.0),
        "cache_v": normal(ks[3], (DEPTH, n_pool, PAGE_SIZE, H_A, DH_A), 1.0),
        "cache_kidx": normal(ks[4], (DEPTH, n_pool, PAGE_SIZE, D_IDX), 1.0),
        "page_table": page_table,
        "state_ssm_conv": normal(ks[6], (DEPTH, DEC_BATCH, CONV_W - 1, CONV_B), 1.0),
        "state_ssm": normal(ks[7], (DEPTH, DEC_BATCH, H_B, P_B, N_B), 0.1),
        "state_gdn_conv": normal(ks[8], (DEPTH, DEC_BATCH, CONV_W - 1, CONV_C), 1.0),
        "state_gdn": normal(ks[9], (DEPTH, DEC_BATCH, H_C, DK_C, DV_C), 0.1),
        "meta_tokens": normal(ks[10], (N_META, D_MODEL), 1.0),
        "rel_bias": normal(ks[11], (N_BUCKETS, H_A), 0.5),
        "norm_mix": gain(ks[12], (DEPTH, D_MODEL)),
        "w_in": normal(ks[13], (DEPTH, D_MODEL, N_IN), D_MODEL ** -0.5),
        "q_norm": gain(ks[14], (DEPTH, DH_A)),
        "k_norm": gain(ks[15], (DEPTH, DH_A)),
        "ssm_conv_w": normal(ks[16], (DEPTH, CONV_W, CONV_B), CONV_W ** -0.5),
        "ssm_conv_b": normal(ks[17], (DEPTH, CONV_B), 0.02),
        "ssm_dt_bias": dt_bias(ks[18], (DEPTH, H_B)),
        "ssm_A_log": a_log(ks[19], (DEPTH, H_B)),
        "ssm_D": gain(ks[20], (DEPTH, H_B)),
        "ssm_norm": gain(ks[21], (DEPTH, D_B)),
        "gdn_conv_w": normal(ks[22], (DEPTH, CONV_W, CONV_C), CONV_W ** -0.5),
        "gdn_dt_bias": dt_bias(ks[23], (DEPTH, H_C)),
        "gdn_A_log": a_log(ks[24], (DEPTH, H_C)),
        "gdn_norm": gain(ks[25], (DEPTH, DV_C)),
        "w_out": normal(ks[26], (DEPTH, D_MIX, D_MODEL), D_MIX ** -0.5),
        "norm_mlp": gain(ks[27], (DEPTH, D_MODEL)),
        "w_up": normal(ks[28], (DEPTH, D_MODEL, D_FF), D_MODEL ** -0.5),
        "w_down": normal(ks[29], (DEPTH, D_FF, D_MODEL), D_FF ** -0.5),
    }

def reference(x_prompt, x_sample, cache_k, cache_v, cache_kidx, page_table, state_ssm_conv, state_ssm,
              state_gdn_conv, state_gdn, meta_tokens, rel_bias, norm_mix, w_in, q_norm, k_norm,
              ssm_conv_w, ssm_conv_b, ssm_dt_bias, ssm_A_log, ssm_D, ssm_norm, gdn_conv_w, gdn_dt_bias,
              gdn_A_log, gdn_norm, w_out, norm_mlp, w_up, w_down):
    dtype = x_prompt.dtype
    Bp, s_len = x_prompt.shape[:2]
    t_new = x_sample.shape[1]
    meta = jnp.broadcast_to(meta_tokens.astype(dtype)[None], (Bp, N_META, D_MODEL))
    xp = jnp.concatenate([meta, x_prompt], axis=1)
    xs = x_sample
    topk_prompt = min(TOPK_MAX, s_len // 4)
    topk_sample = min(TOPK_MAX, (PAST_LEN + t_new) // 4)
    plan_prompt = ((N_META, N_META), (s_len, CHUNK))
    plan_sample = ((t_new, t_new),)
    zero_ssm_conv = jnp.zeros((Bp, CONV_W - 1, CONV_B), dtype)
    zero_ssm = jnp.zeros((Bp, H_B, P_B, N_B), dtype)
    zero_gdn_conv = jnp.zeros((Bp, CONV_W - 1, CONV_C), dtype)
    zero_gdn = jnp.zeros((Bp, H_C, DK_C, DV_C), dtype)
    attn_prompt = functools.partial(dsa_prompt, rel_bias=rel_bias, topk=topk_prompt)
    prompt_rows = []
    sample_rows = []
    for l in range(DEPTH):
        lw = (norm_mix[l], w_in[l], q_norm[l], k_norm[l], ssm_conv_w[l], ssm_conv_b[l], ssm_dt_bias[l],
              ssm_A_log[l], ssm_D[l], ssm_norm[l], gdn_conv_w[l], gdn_dt_bias[l], gdn_A_log[l], gdn_norm[l],
              w_out[l], norm_mlp[l], w_up[l], w_down[l])
        attn_sample = functools.partial(dsa_sample, cache_k=cache_k, cache_v=cache_v, cache_kidx=cache_kidx,
                                        layer=l, page_table=page_table, rel_bias=rel_bias, topk=topk_sample)
        xp, rows_p = trunk_layer(xp, lw, attn_prompt, zero_ssm_conv, zero_ssm, zero_gdn_conv, zero_gdn, plan_prompt)
        xs, rows_s = trunk_layer(xs, lw, attn_sample, state_ssm_conv[l], state_ssm[l], state_gdn_conv[l],
                                 state_gdn[l], plan_sample)
        prompt_rows.append(rows_p)
        sample_rows.append(rows_s)
    k_p, v_p, kidx_p, ssm_conv_p, ssm_p, gdn_conv_p, gdn_p = [jnp.stack(t) for t in zip(*prompt_rows)]
    k_s, v_s, kidx_s, ssm_conv_s, ssm_s, gdn_conv_s, gdn_s = [jnp.stack(t) for t in zip(*sample_rows)]
    y_prompt = xp[:, N_META:]
    y_sample = xs
    return (y_prompt, y_sample, k_p, v_p, kidx_p, k_s, v_s, kidx_s, ssm_conv_p, ssm_p, ssm_conv_s, ssm_s,
            gdn_conv_p, gdn_p, gdn_conv_s, gdn_s)


_drawn_inputs = setup_inputs


def setup_inputs(seed=0):
    import zlib

    import numpy as np

    out = dict(_drawn_inputs(seed))
    spreads = {}
    factors = {'q_norm': 8.0, 'ssm_D': 24.151, 'gdn_norm': 3.859, 'ssm_norm': 3.064}
    for name, (base, spread) in spreads.items():
        noise = np.random.default_rng([zlib.crc32(name.encode()), seed]).standard_normal(out[name].shape)
        drawn = base * np.exp(spread * noise) if base else spread * noise
        out[name] = __import__('jax').numpy.asarray(drawn.astype(out[name].dtype))
    for name, factor in factors.items():
        out[name] = (out[name] * factor).astype(out[name].dtype)
    return out
```

```python
from contextlib import ExitStack

import numpy as np

import concourse.bass as bass
from concourse import mybir

F32 = mybir.dt.float32
U32 = mybir.dt.uint32
I32 = mybir.dt.int32
ALU = mybir.AluOpType
ACT = mybir.ActivationFunctionType
AX = mybir.AxisListType
AP = bass.AP

P = 128
D = 2048
KT = D // P
SEQ, META = 512, 16
TP = SEQ + META
DB, DT = 8, 4
TS = DB * DT
TOK = TP + TS
HALF = TOK // 2
NT = [128, 128, 128, 128, TOK - 512]
TAIL = NT[4]
TAILP = TP - 512
HA, DH = 4, 128
DA = HA * DH
HI, DI = 16, 64
HB, PB, NB = 12, 64, 128
DBm = HB * PB
HC, DK = 6, 128
DC = HC * DK
CB = DBm + 4 * NB
CC = 3 * DC
NCONV = (CB + CC) // P
PAST, PAGE, PAGES = 4096, 128, 32
TOPP, TOPS = 128, 256
NIN = 7784
FF = 8192
EPS = 1e-6
NEG = -1e30
TAKEN = -3e38
CH = 512
C_QKV, C_QI, C_KIW, C_XBC, C_DT, C_GQKV, C_ZC = 0, 1536, 2560, 3408, 4688, 4700, 7004
R_QI, R_CONV = 0, 1024
N_Q, N_K, N_V, N_KI, N_WI, N_ZB, N_DT, N_ZC, N_A, N_B = 0, 512, 1024, 1536, 1600, 1616, 2384, 2396, 3164, 3170
NTM = 3176


def chunk_plan():
    return [
        ("N", [(C_KIW, 512)], N_KI),
        ("F", [(C_QI, 512)], 0),
        ("F", [(C_QI + 512, 512)], 512),
        ("F", [(C_XBC, 512)], 1024),
        ("F", [(C_XBC + 512, 512)], 1536),
        ("F", [(C_XBC + 1024, 256), (C_GQKV, 256)], 2048),
        ("F", [(C_GQKV + 256, 512)], 2560),
        ("F", [(C_GQKV + 768, 512)], 3072),
        ("F", [(C_GQKV + 1280, 512)], 3584),
        ("F", [(C_GQKV + 1792, 512)], 4096),
        ("N", [(0, 512)], 0),
        ("N", [(512, 512)], 512),
        ("N", [(1024, 512)], 1024),
        ("N", [(C_KIW + 512, 336), (C_DT, 12)], N_KI + 512),
        ("N", [(C_ZC, 512)], N_ZC),
        ("N", [(C_ZC + 512, 268)], N_ZC + 512),
    ]


def t5_bucket_np(dist):
    d = np.maximum(dist, 0)
    ratio = np.log(np.maximum(d, 1).astype(np.float32) / np.float32(16)) / np.float32(np.log(8.0))
    far = 16 + (ratio * np.float32(16)).astype(np.int32)
    return np.where(d < 16, d, np.minimum(far, 31))


BUCKET_FROM = [int(np.argmax(t5_bucket_np(np.arange(200)) >= b)) for b in range(32)]


def constants():
    r = np.arange(P)
    block = np.where(r < TAILP, 0, 1 + (r - TAILP) // DT)
    full = np.ones((P, P), bool)
    tail = block[:, None] == block[None, :]
    upto = r[:, None] <= r[None, :]

    def levels(same, n):
        out = []
        for lev in range(n):
            b = 1 << lev
            j, i = r[:, None], r[None, :]
            out.append(same & (i // (2 * b) == j // (2 * b)) & ((i // b) % 2 == 1) & ((j // b) % 2 == 0))
        return np.concatenate([x.astype(np.float32) for x in out], axis=1)

    f = np.float32
    m = 639 - np.arange(768)
    onehot = (t5_bucket_np(m)[None, :] == np.arange(32)[:, None]).astype(f)
    members = np.zeros((P, 9), f)
    members[np.arange(TAIL), block[:TAIL]] = 1
    return {
        "c_ident": np.eye(P, dtype=f),
        "c_ones": np.ones((P, P), f),
        "c_upto": np.concatenate([(upto & full).astype(f), (upto & tail).astype(f)], axis=1),
        "c_same": np.concatenate([full.astype(f), tail.astype(f)], axis=1),
        "c_level": levels(full, 7),
        "c_level_tail": levels(tail, 4),
        "c_causal": np.where(r[:, None] >= r[None, :], 0.0, NEG).astype(f),
        "c_onehot": onehot,
        "c_members": members,
    }


def tile_rows(i):
    if i == 0:
        return [(0, META, "meta_tokens", 0), (META, P - META, "x_prompt", 0)]
    if i < 4:
        return [(0, P, "x_prompt", P * i - META)]
    return [(0, TAILP, "x_prompt", SEQ - TAILP), (TAILP, TS, "x_sample", 0)]


def two_halves(h):
    return slice(h * HALF, (h + 1) * HALF)


def load_and_norm(nc, dram, sb):
    with ExitStack() as ctx:
        sem = lambda n: ctx.enter_context(nc.semaphore(n))
        x_tok = ctx.enter_context(nc.sbuf_tensor("x_tok", [P, 5, D], F32))
        pt = [ctx.enter_context(nc.psum_tensor(f"xt_ps{n}", [P, 4, P], F32)) for n in range(4)]
        x_in = [sem(f"x_in{i}") for i in range(5)]
        pe_t, evac = sem("x_transposed"), sem("xT_ready")
        xT = sb["xT"]
        x_saved = sem("xT_saved")
        block = ctx.enter_context(nc.Block())

        @block.sync
        def _(sp):
            for i in range(5):
                for row, n, name, src in tile_rows(i):
                    a = dram[name] if name == "meta_tokens" else dram[name].rearrange("a b d -> (a b) d")
                    sp.dma_start(x_tok[row:row + n, i, :], a[src:src + n, :]).then_inc(x_in[i], 16)

            sp.wait_ge(evac, 20)
            sp.dma_start(dram["xT"], xT[:, :, :].rearrange("p k t -> p (k t)")).then_inc(x_saved, 16)
            sp.wait_ge(x_saved, 16)

        @block.tensor
        def _(pe):
            pe.wait_ge(sb["const_in"], 16 * sb["n_const"])
            for i in range(5):
                pe.wait_ge(x_in[i], 16 * len(tile_rows(i)))
                for g in range(4):
                    n = 4 * i + g
                    if n >= 4:
                        pe.wait_ge(evac, n - 3)
                    for k in range(4):
                        kk = 4 * g + k
                        last = pe.transpose(pt[n % 4][:, k, 0:NT[i]], x_tok[0:NT[i], i, kk * P:(kk + 1) * P],
                                            sb["ident"][0:NT[i], 0:NT[i]])
                    last.then_inc(pe_t, 1)

        @block.vector
        def _(dve):
            for i in range(5):
                for g in range(4):
                    n = 4 * i + g
                    dve.wait_ge(pe_t, n + 1)
                    dve.tensor_copy(xT[:, 4 * g:4 * g + 4, P * i:P * i + NT[i]],
                                    pt[n % 4][:, :, 0:NT[i]]).then_inc(evac, 1)

    norm_feature_major(nc, sb, sb["xT"], sb["g_mix"], sb["hT"], "mix")


def norm_feature_major(nc, sb, xT, gain, out, tag):
    with ExitStack() as ctx:
        sem = lambda n: ctx.enter_context(nc.semaphore(f"{tag}_{n}"))
        sq = ctx.enter_context(nc.sbuf_tensor(f"{tag}_sq", [P, 2, TOK], F32))
        rstd = ctx.enter_context(nc.sbuf_tensor(f"{tag}_rstd", [P, TOK], F32))
        ps = [ctx.enter_context(nc.psum_tensor(f"{tag}_ss{h}", [P, HALF], F32)) for h in range(2)]
        sq_ready, summed, root, rstd_ready = sem("sq_ready"), sem("summed"), sem("root"), sem("rstd_ready")
        block = ctx.enter_context(nc.Block())

        @block.scalar
        def _(act):
            for k in range(KT):
                if k >= 2:
                    act.wait_ge(summed, k - 1)
                act.activation(sq[:, k % 2, :], xT[:, k, :], ACT.Square).then_inc(sq_ready, 1)
            act.wait_ge(summed, KT)
            for h in range(2):
                act.activation(rstd[:, two_halves(h)], ps[h][:, :], ACT.Sqrt, bias=sb["eps"][:, 0:1],
                               scale=1.0 / D).then_inc(root, 1)

        @block.tensor
        def _(pe):
            for k in range(KT):
                pe.wait_ge(sq_ready, k + 1)
                for h in range(2):
                    last = pe.matmul(ps[h][:, :], sb["ones"][:, :], sq[:, k % 2, two_halves(h)],
                                     start=(k == 0), stop=(k == KT - 1))
                last.then_inc(summed, 1)

        @block.vector
        def _(dve):
            dve.wait_ge(root, 2)
            dve.reciprocal(rstd[:, :], rstd[:, :]).then_inc(rstd_ready, 1)
            dve.wait_ge(rstd_ready, 1)
            for k in range(KT):
                dve.scalar_tensor_tensor(out=out[:, k, :], in0=xT[:, k, :], scalar=gain[:, k:k + 1],
                                         in1=rstd[:, :], op0=ALU.mult, op1=ALU.mult)


def project_in(nc, dram, sb):
    plan = chunk_plan()
    hT, ring = sb["hT"], sb["ring"]
    with ExitStack() as ctx:
        sem = lambda n: ctx.enter_context(nc.semaphore(n))
        stage = ctx.enter_context(nc.sbuf_tensor("proj_stage", [P, 4, CH], F32))
        ps = [ctx.enter_context(nc.psum_tensor(f"proj_ps{n}", [P, CH], F32)) for n in range(4)]
        w_in = [[sem(f"w_in_{s}_{q}") for q in range(4)] for s in range(2)]
        product, evac = sem("product"), sem("proj_evac")
        stored = [sem(f"proj_stored{n}") for n in range(4)]
        banks = []
        for c, (kind, segs, r0) in enumerate(plan):
            width = sum(w for _, w in segs)
            if kind == "F":
                banks += [(c, P, HALF, dram["projT"][r0 + P * m:r0 + P * (m + 1), two_halves(h)])
                          for m in range(4) for h in range(2)]
            else:
                banks += [(c, NT[i], width, dram["projN"][P * i:P * i + NT[i], r0:r0 + width]) for i in range(5)]
        block = ctx.enter_context(nc.Block())

        @block.sync
        def _(sp):
            for c, (_, segs, _) in enumerate(plan):
                if c >= 2:
                    sp.wait_ge(product, sum(b[0] <= c - 2 for b in banks))
                at = 0
                for n, (col, width) in enumerate(segs):
                    for q in range(4):
                        src = dram["w_in"][0, 512 * q:512 * (q + 1), col:col + width]
                        sp.dma_start(ring[:, c % 2, 4 * q:4 * q + 4, at:at + width],
                                     src.rearrange("(k p) n -> p k n", p=P)).then_inc(w_in[c % 2][q], 16)
                    at += width

        @block.tensor
        def _(pe):
            seen, bank = [0, 0], 0

            def next_bank():
                if bank >= 4:
                    pe.wait_ge(evac, bank - 3)
                return ps[bank % 4]

            for c, (kind, segs, _) in enumerate(plan):
                w, width = ring[:, c % 2], sum(x for _, x in segs)
                seen[c % 2] += 16 * len(segs)
                for m in range(4 if kind == "F" else 5):
                    if kind == "F":
                        out = [next_bank()[:, 0:HALF]]
                        bank += 1
                        out.append(next_bank()[:, 0:HALF])
                        bank += 1
                    else:
                        out = [next_bank()[0:NT[m], 0:width]]
                        bank += 1
                    for k in range(KT):
                        if m == 0 and k % 4 == 0:
                            pe.wait_ge(w_in[c % 2][k // 4], seen[c % 2])
                        flags = dict(start=(k == 0), stop=(k == KT - 1))
                        if kind == "F":
                            for h in range(2):
                                last = pe.matmul(out[h], w[:, k, P * m:P * (m + 1)], hT[:, k, two_halves(h)], **flags)
                                if k == KT - 1:
                                    last.then_inc(product, 1)
                        else:
                            last = pe.matmul(out[0], hT[:, k, P * m:P * m + NT[m]], w[:, k, 0:width], **flags)
                            if k == KT - 1:
                                last.then_inc(product, 1)

        @block.vector
        def _(dve):
            for b, (_, rows, cols, _) in enumerate(banks):
                dve.wait_ge(product, b + 1)
                if b >= 4:
                    dve.wait_ge(stored[b % 4], 16 * (b // 4))
                dve.tensor_copy(stage[0:rows, b % 4, 0:cols], ps[b % 4][0:rows, 0:cols]).then_inc(evac, 1)

        @block.scalar
        def _(act):
            for b, (_, rows, cols, dst) in enumerate(banks):
                act.wait_ge(evac, b + 1)
                act.dma_start(dst, stage[0:rows, b % 4, 0:cols]).then_inc(stored[b % 4], 16)
            for n in range(4):
                act.wait_ge(stored[n], 16 * ((len(banks) - n + 3) // 4))


class Chain:

    def __init__(self, eng, sem):
        self.eng, self.sem, self.n = eng, sem, 0

    def __call__(self, ins):
        self.n += 1
        ins.then_inc(self.sem, 1)
        self.eng.wait_ge(self.sem, self.n)


F_B, F_C, F_Q = 6, 8, 10
T_X, T_B, T_GQ, T_GK, T_GV = 0, 6 * P, 8 * P, 14 * P, 20 * P
TM_COLS = 26 * P
RAW = 3 + TOK
XW = RAW + DB * 7
YW = XW - 3


def convolve(nc, dram, sb):
    with ExitStack() as ctx:
        sem = lambda n: ctx.enter_context(nc.semaphore(n))
        sbuf = lambda n, s: ctx.enter_context(nc.sbuf_tensor(n, s, F32))
        R = 4
        xp = sbuf("conv_x", [P, R, XW])
        y = sbuf("conv_y", [P, 2, YW])
        par, state = sbuf("conv_par", [P, NCONV, 5]), sbuf("conv_state", [P, NCONV, DB, 3])
        feat = sbuf("conv_feat", [P, R, TOK])
        last3 = sbuf("conv_last3", [P, R, 27])
        last3_t = sbuf("conv_last3_t", [27, NCONV * P])
        big = [ctx.enter_context(nc.psum_tensor(f"conv_big{n}", [P, 4, P], F32)) for n in range(2)]
        small = [ctx.enter_context(nc.psum_tensor(f"conv_small{n}", [P, P], F32)) for n in range(2)]
        l3 = [ctx.enter_context(nc.psum_tensor(f"conv_l3_{n}", [P, 4, P], F32)) for n in range(2)]
        par_in, zeroed = sem("conv_par_in"), sem("conv_zeroed")
        x_in = [sem(f"conv_x_in{n}") for n in range(R)]
        laid, first, conv, act_ready, turned = sem("laid"), sem("first_tap"), sem("conv_done"), sem("silu_ready"), sem("turned")
        big_out, small_out, l3_turned, l3_out, saved, chain = (
            sem("big_out"), sem("small_out"), sem("l3_turned"), sem("l3_out"), sem("conv_saved"), sem("conv_chain"))
        turned_f = [f for f in range(NCONV) if not F_C <= f < F_Q]
        nth = {f: n for n, f in enumerate(turned_f)}
        before = lambda f: sum(g < f for g in turned_f)
        dest = lambda f: sb["bcT"][:, f - F_B, :] if F_B <= f < F_Q else feat[:, f % R, :]
        block = ctx.enter_context(nc.Block())

        @block.sync
        def _(sp):
            sp.dma_start(par[:, :, :], dram["conv_par"]).then_inc(par_in, 16)
            sp.dma_start(state[:, :, :, :], dram["conv_state"]).then_inc(par_in, 16)
            for f in range(NCONV):
                if f >= R:
                    sp.wait_ge(conv, f - R + 1)
                    sp.wait_ge(laid, f - R + 1)
                sp.dma_start(xp[:, f % R, 3:RAW], dram["projT"][R_CONV + P * f:R_CONV + P * (f + 1), :]
                             ).then_inc(x_in[f % R], 16)
            sp.wait_ge(l3_out, NCONV // 4)
            outs = [("ssm_conv_prompt", "ssm_conv_sample", 0, CB), ("gdn_conv_prompt", "gdn_conv_sample", CB, CC)]
            for prompt, sample, at, n in outs:
                sp.dma_start(dram[prompt][0, 0], last3_t[0:3, at:at + n]).then_inc(saved, 16)
                sp.dma_start(dram[sample][0].rearrange("b j f -> (b j) f"), last3_t[3:27, at:at + n]).then_inc(saved, 16)
            sp.wait_ge(saved, 64)

        @block.gpsimd
        def _(pool):
            for n in range(R):
                last = pool.memset(xp[:, n, 0:3], 0.0)
            last.then_inc(zeroed, 1)
            pool.wait_ge(par_in, 32)
            pool.wait_ge(zeroed, 1)
            for f in range(NCONV):
                x, own = xp[:, f % R], xp[:, f % R, RAW:XW].rearrange("p (b c) -> p b c", c=7)
                new = x[:, 3 + TP:RAW].rearrange("p (b c) -> p b c", c=DT)
                pool.wait_ge(x_in[f % R], 16 * (f // R + 1))
                if f >= R:
                    pool.wait_ge(l3_turned, f - R + 1)
                pool.tensor_copy(own[:, :, 0:3], state[:, f, :, :])
                pool.tensor_copy(own[:, :, 3:7], new)
                pool.tensor_copy(last3[:, f % R, 0:3], x[:, TP:TP + 3])
                pool.tensor_copy(last3[:, f % R, 3:27].rearrange("p (b c) -> p b c", c=3), new[:, :, 1:4]
                                 ).then_inc(laid, 1)

        @block.scalar
        def _(act):
            def silu(f):
                if F_B <= f < F_Q:
                    pass
                elif f >= R:
                    act.wait_ge(turned, before(f - R + 1))
                act.wait_ge(conv, f + 1)
                act.activation(dest(f)[:, 0:TP], y[:, f % 2, 0:TP], ACT.Silu)
                own = y[:, f % 2, RAW:RAW + DB * 7 - 3]
                src = AP(tensor=own.tensor, offset=own.offset, ap=[list(own.ap[0]), [7, DB], [1, DT]])
                act.activation(dest(f)[:, TP:TOK].rearrange("p (b t) -> p b t", t=DT), src, ACT.Silu
                               ).then_inc(act_ready, 1)

            def small_copy(f):
                act.wait_ge(turned, nth[f] + 1)
                act.activation(sb["tm"][0:TAIL, 4, nth[f] * P:(nth[f] + 1) * P], small[nth[f] % 2][0:TAIL, :], ACT.Copy
                               ).then_inc(small_out, 1)

            act.wait_ge(par_in, 32)
            for f in range(NCONV + 2):
                if f < NCONV:
                    act.wait_ge(laid, f + 1)
                    if f >= 2:
                        act.wait_ge(act_ready, f - 1)
                    act.activation(y[:, f % 2, :], xp[:, f % R, 0:YW], ACT.Identity, bias=par[:, f, 4:5],
                                   scale=par[:, f, 0:1]).then_inc(first, 1)
                if 1 <= f <= NCONV:
                    silu(f - 1)
                if f >= 2 and f - 2 in nth:
                    small_copy(f - 2)

        @block.vector
        def _(dve):
            step = Chain(dve, chain)

            def big_copy(f):
                n = nth[f]
                dve.wait_ge(turned, n + 1)
                dve.tensor_copy(sb["tm"][:, 0:4, n * P:(n + 1) * P], big[n % 2][:, :, :]).then_inc(big_out, 1)

            def last3_copy(g):
                dve.wait_ge(l3_turned, 4 * g + 4)
                dve.tensor_copy(last3_t[:, 4 * g * P:4 * (g + 1) * P].rearrange("p (a b) -> p a b", a=4),
                                l3[g % 2][0:27, :, :]).then_inc(l3_out, 1)

            dve.wait_ge(par_in, 32)
            for f in range(NCONV + 2):
                if f < NCONV:
                    dve.wait_ge(first, f + 1)
                    for i in range(1, 4):
                        ins = dve.scalar_tensor_tensor(out=y[:, f % 2, :], in0=xp[:, f % R, i:i + YW],
                                                       scalar=par[:, f, i:i + 1], in1=y[:, f % 2, :],
                                                       op0=ALU.mult, op1=ALU.add)
                        if i < 3:
                            step(ins)
                    ins.then_inc(conv, 1)
                if f >= 2 and f - 2 in nth:
                    big_copy(f - 2)
                if f >= 4 and f % 4 == 0:
                    last3_copy(f // 4 - 1)

        @block.tensor
        def _(pe):
            ident = sb["ident"]

            def turn(f):
                n = nth[f]
                if n >= 2:
                    pe.wait_ge(big_out, n - 1)
                    pe.wait_ge(small_out, n - 1)
                pe.wait_ge(act_ready, f + 1)
                for i in range(4):
                    pe.transpose(big[n % 2][:, i, :], dest(f)[:, P * i:P * (i + 1)], ident[:, :])
                pe.transpose(small[n % 2][0:TAIL, :], dest(f)[:, 512:TOK], ident[:, :]).then_inc(turned, 1)

            for f in range(NCONV + 1):
                if f < NCONV:
                    pe.wait_ge(laid, f + 1)
                    if f % 4 == 0 and f >= 8:
                        pe.wait_ge(l3_out, f // 4 - 1)
                    pe.transpose(l3[f // 4 % 2][0:27, f % 4, :], last3[:, f % R, :], ident[:, :]).then_inc(l3_turned, 1)
                if f >= 1 and f - 1 in nth:
                    turn(f - 1)


def bc(ap, shape):
    return ap.broadcast_to(shape)


def gates(nc, dram, consts, sb):
    with ExitStack() as ctx:
        sem = lambda n: ctx.enter_context(nc.semaphore(n))
        sbuf = lambda n, s: ctx.enter_context(nc.sbuf_tensor(n, s, F32))
        raw, bias, alog = sbuf("g_raw", [P, 5, 24]), sbuf("g_bias", [P, 18]), sbuf("g_alog", [P, 18])
        z, u, w, lw, t = (sbuf(f"g_{n}", [P, 5, 18]) for n in "z u w lw t".split())
        rate = sbuf("g_rate", [P, 18])
        by_block = sbuf("g_by_block", [P, 9, 18])
        ps = ctx.enter_context(nc.psum_tensor("g_ps", [P, 5, 36], F32))
        pe_ps = ctx.enter_context(nc.psum_tensor("g_el", [P, 13, 18], F32))
        par_in, cleared, raw_in, chain, exp_u, ln_w, exp_b, rate_ready, g_ready, sums, cums, done = (
            sem(f"g_{n}") for n in ("par_in", "cleared", "raw_in", "chain", "exp_u", "ln_w", "exp_b", "rate_ready",
                                    "g_ready", "sums", "cums", "done"))
        za, wr, act_chain = sem("g_za"), sem("g_wr"), sem("g_act_chain")
        g, dt, beta = sb["g"], sb["dt"], sb["beta"]
        block = ctx.enter_context(nc.Block())

        @block.sync
        def _(sp):
            for dst, name, at, n in ((bias, "ssm_dt_bias", 0, 12), (bias, "gdn_dt_bias", 12, 6),
                                     (alog, "ssm_A_log", 0, 12), (alog, "gdn_A_log", 12, 6),
                                     (sb["ssm_d"], "ssm_D", 0, 12)):
                sp.dma_start(dst[:, at:at + n], dram[name][0].partition_broadcast(P)).then_inc(par_in, 16)
            sp.dma_start(sb["upto"][:, :], consts["c_upto"]).then_inc(par_in, 16)
            sp.dma_start(sb["same"][:, :], consts["c_same"]).then_inc(par_in, 16)
            sp.dma_start(sb["members"][:, :], consts["c_members"]).then_inc(par_in, 16)
            sp.wait_ge(cleared, 1)
            for i in range(5):
                rows = slice(P * i, P * i + NT[i])
                sp.dma_start(raw[0:NT[i], i, 0:12], dram["projN"][rows, N_DT:N_DT + 12]).then_inc(raw_in, 16)
                sp.dma_start(raw[0:NT[i], i, 12:24], dram["projN"][rows, N_A:N_A + 12]).then_inc(raw_in, 16)

        @block.gpsimd
        def _(pool):
            pool.memset(raw[:, :, :], 0.0).then_inc(cleared, 1)

        @block.vector
        def _(dve):
            step = Chain(dve, chain)
            dve.wait_ge(par_in, 128)
            dve.wait_ge(raw_in, 160)
            step(dve.memset(sb["cum"][:, :, :], 0.0))
            step(dve.tensor_tensor(z[:, :, :], raw[:, :, 0:18], bc(bias[:, :].unsqueeze(1), [P, 5, 18]), ALU.add))
            dve.scalar_tensor_tensor(out=w[:, :, :], in0=z[:, :, :], scalar=-1.0, in1=z[:, :, :], op0=ALU.mult,
                                     op1=ALU.max).then_inc(za, 1)
            dve.wait_ge(exp_u, 1)
            dve.tensor_scalar(w[:, :, :], u[:, :, :], 1.0, None, ALU.add).then_inc(wr, 1)
            dve.wait_ge(wr, 1)
            step(dve.tensor_scalar(t[:, :, :], w[:, :, :], -1.0, None, ALU.add))
            step(dve.tensor_scalar(sb["eq"][:, :, :], t[:, :, :], 0.0, None, ALU.is_equal))
            step(dve.tensor_tensor(t[:, :, :], t[:, :, :], sb["eq"][:, :, :], ALU.add))
            step(dve.reciprocal(t[:, :, :], t[:, :, :]))
            dve.wait_ge(ln_w, 1)
            step(dve.tensor_tensor(t[:, :, :], t[:, :, :], lw[:, :, :], ALU.mult))
            step(dve.tensor_tensor(t[:, :, :], t[:, :, :], sb["eq"][:, :, :], ALU.add))
            step(dve.tensor_tensor(t[:, :, :], t[:, :, :], u[:, :, :], ALU.mult))
            step(dve.scalar_tensor_tensor(out=t[:, :, :], in0=z[:, :, :], scalar=0.0, in1=t[:, :, :],
                                          op0=ALU.max, op1=ALU.add))
            step(dve.tensor_copy(dt[:, :, :], t[:, :, 0:12]))
            dve.wait_ge(rate_ready, 1)
            step(dve.scalar_tensor_tensor(out=g[:, :, :], in0=t[:, :, :], scalar=-1.0,
                                          in1=bc(rate[:, :].unsqueeze(1), [P, 5, 18]), op0=ALU.mult, op1=ALU.mult))
            for b in range(9):
                ins = dve.tensor_scalar(by_block[0:TAIL, b, :], g[0:TAIL, 4, :], sb["members"][0:TAIL, b:b + 1], None,
                                        ALU.mult)
            ins.then_inc(g_ready, 1)
            dve.wait_ge(exp_b, 1)
            step(dve.tensor_scalar(beta[:, :, :], beta[:, :, :], 1.0, None, ALU.add))
            step(dve.reciprocal(beta[:, :, :], beta[:, :, :]))
            dve.wait_ge(sums, 1)
            dve.tensor_copy(sb["cum"][:, 0:4, :], ps[:, 0:4, :])
            dve.tensor_copy(sb["cum"][0:TAIL, 4, :], ps[0:TAIL, 4, :]).then_inc(cums, 1)
            dve.wait_ge(cums, 1)
            dve.tensor_tensor(sb["wend"][:, :, :], sb["cum"][:, :, 18:36], sb["cum"][:, :, 0:18], ALU.subtract
                              ).then_inc(done, 1)

        @block.scalar
        def _(act):
            act.wait_ge(par_in, 128)
            act.activation(rate[:, :], alog[:, :], ACT.Exp).then_inc(rate_ready, 1)
            act.wait_ge(za, 1)
            act.activation(u[:, :, :], w[:, :, :], ACT.Exp, scale=-1.0).then_inc(exp_u, 1)
            act.activation(beta[:, :, :], raw[:, :, 18:24], ACT.Exp, scale=-1.0).then_inc(exp_b, 1)
            act.wait_ge(wr, 1)
            act.activation(lw[:, :, :], w[:, :, :], ACT.Ln).then_inc(ln_w, 1)
            act.wait_ge(sums, 1)
            act.activation(sb["el"][:, :, :], pe_ps[:, :, :], ACT.Exp)
            act.wait_ge(cums, 1)
            act.activation(sb["ecum"][:, :, :], sb["cum"][:, :, 0:18], ACT.Exp)
            act.wait_ge(done, 1)
            act.activation(sb["wend"][:, :, :], sb["wend"][:, :, :], ACT.Exp)

        @block.tensor
        def _(pe):
            pe.wait_ge(g_ready, 1)
            for i in range(5):
                m = P * (i == 4)
                n = NT[i]
                pe.matmul(ps[0:n, i, 0:18], sb["upto"][0:n, m:m + n], g[0:n, i, :], start=True, stop=True)
                pe.matmul(ps[0:n, i, 18:36], sb["same"][0:n, m:m + n], g[0:n, i, :], start=True, stop=True)
                if i < 4:
                    pe.matmul(pe_ps[:, i, :], sb["ones"][:, :], g[:, i, :], start=True, stop=True)
            pe.matmul(pe_ps[:, 4:13, :], sb["ones"][0:TAIL, :], by_block[0:TAIL, :, :], start=True, stop=True
                      ).then_inc(sums, 1)


def ssd_scan(nc, dram, sb):
    with ExitStack() as ctx:
        sem = lambda n: ctx.enter_context(nc.semaphore(f"ssd_{n}"))
        sbuf = lambda n, s: ctx.enter_context(nc.sbuf_tensor(f"ssd_{n}", s, F32))
        psum = lambda n, s: ctx.enter_context(nc.psum_tensor(f"ssd_{n}", s, F32))
        tm, bcT, y = sb["tm"], sb["bcT"], sb["y_ssd"]
        dec, gm = sbuf("dec", [P, 12, P]), sbuf("gm", [P, 2, P])
        xdt, xdtw, skip = sbuf("xdt", [P, DBm]), sbuf("xdtw", [P, DBm]), sbuf("skip", [P, DBm])
        sT = sbuf("sT", [P, DBm])
        s_nat, s_smp = sbuf("s_nat", [P, DB, 6, NB]), sbuf("s_smp", [P, DB, DBm])
        yT, b_own, el_nat = sbuf("yT", [P, 6, TAIL]), sbuf("b_own", [TAIL, 2, DB, NB]), sbuf("el_nat", [P, 6, DB])
        s_out = sbuf("s_out", [P, 6, NB])
        rows_ps = [psum(f"rows{n}", [P, 4, P]) for n in range(3)]
        g_ps = psum("g", [P, 2, P])
        y_ps = [psum(f"y{n}", [P, 384]) for n in range(2)]
        s_ps = [psum(f"s{n}", [P, 384]) for n in range(2)]
        (rows_done, g_done, inter_done, dif, dec_ready, w_ready, gm_ready, x_ready, inter_out, intra, intra_out, s_done,
         s_ready, skip_ready, chain, loaded, turned, turned_out, own_ready, yT_done, yT_out, upd, upd_out, sT_turned,
         sT_out, saved, el_ready) = (sem(n) for n in (
             "rows_done", "g_done", "inter_done", "dif", "dec_ready", "w_ready", "gm_ready", "x_ready", "inter_out",
             "intra", "intra_out", "s_done", "s_ready", "skip_ready", "chain", "loaded", "turned", "turned_out",
             "own_ready", "yT_done", "yT_out", "upd", "upd_out", "sT_turned", "sT_out", "saved", "el_ready"))
        h3 = lambda ap, h: ap.rearrange("p (h e) -> p h e", h=h)
        nat = lambda ap: ap.rearrange("(q r) p n -> (r p) q n", r=2)
        block = ctx.enter_context(nc.Block())

        @block.sync
        def _(sp):
            for b in range(DB):
                sp.dma_start(s_nat[:, b], nat(dram["state_ssm"][0, b])).then_inc(loaded, 16)
            sp.wait_ge(upd_out, 12)
            for b in range(DB):
                sp.dma_start(nat(dram["ssm_sample"][0, b]), s_nat[:, b]).then_inc(saved, 16)
            sp.wait_ge(sT_out, 2)
            sp.dma_start(nat(dram["ssm_prompt"][0, 0]), s_out[:, :, :]).then_inc(saved, 16)
            sp.wait_ge(saved, 144)

        @block.gpsimd
        def _(pool):
            for i in range(5):
                n = NT[i]
                if i:
                    pool.wait_ge(s_done, i)
                    pool.wait_ge(intra, i)
                    pool.wait_ge(intra_out, i)
                x = h3(tm[0:n, i, T_X:T_X + DBm], HB)
                pool.tensor_tensor(h3(xdt[0:n, :], HB), x, bc(sb["dt"][0:n, i, :].unsqueeze(2), [n, HB, PB]), ALU.mult
                                   ).then_inc(x_ready, 1)
                pool.tensor_tensor(h3(skip[0:n, :], HB), x, bc(sb["ssm_d"][0:n, :].unsqueeze(2), [n, HB, PB]), ALU.mult
                                   ).then_inc(skip_ready, 1)
                pool.wait_ge(x_ready, 2 * i + 1)
                pool.tensor_tensor(h3(xdtw[0:n, :], HB), h3(xdt[0:n, :], HB),
                                   bc(sb["wend"][0:n, i, 0:12].unsqueeze(2), [n, HB, PB]), ALU.mult).then_inc(x_ready, 1)
            for r in range(2):
                part = slice(PB * r, PB * (r + 1))
                src = sb["el"][part, 5:13, 0:12].rearrange("p b (q r) -> p q b r", r=2)[:, :, :, r]
                pool.tensor_copy(el_nat[part, :, :], src).then_inc(el_ready, 1)

        @block.tensor
        def _(pe):
            ident, g = sb["ident"], sb["g"]
            pe.wait_ge(loaded, 128)
            for q in range(24):
                if q >= 2:
                    pe.wait_ge(turned_out, q - 1)
                for r in range(2):
                    b, pair = divmod(2 * q + r, 6)
                    last = pe.transpose(s_ps[q % 2][:, r * P:(r + 1) * P], s_nat[:, b, pair, :], ident[:, :])
                last.then_inc(turned, 1)
            for i in range(5):
                n, m = NT[i], P * (i == 4)
                if i:
                    pe.wait_ge(dif, i)
                    pe.wait_ge(gm_ready, i)
                    pe.wait_ge(intra_out, i)
                for h in range(HB):
                    last = pe.matmul(rows_ps[h // 4][:, h % 4, 0:n], bc(g[0:n, i, h:h + 1], [n, P]),
                                     sb["upto"][0:n, m:m + n], start=True, stop=True)
                last.then_inc(rows_done, 1)
                for k in range(2):
                    last = pe.matmul(g_ps[0:n, k, 0:n], bcT[:, k, P * i:P * i + n], bcT[:, 2 + k, P * i:P * i + n],
                                     start=True, stop=True)
                last.then_inc(g_done, 1)
                pe.wait_ge(s_ready, i + 1)
                if i < 4:
                    for k in range(2):
                        last = pe.matmul(y_ps[k][0:n, :], bcT[:, 2 + k, P * i:P * i + n], sT[:, 384 * k:384 * (k + 1)],
                                         start=True, stop=True)
                    last.then_inc(inter_done, 1)
                else:
                    pe.wait_ge(dif, 5)
                    pe.wait_ge(turned_out, 24)
                    for q in range(6):
                        out = rows_ps[0][:, :, :].rearrange("p a b -> p (a b)")[:, TAIL * q:TAIL * (q + 1)]
                        pe.matmul(out[:, 0:TAILP], sT[:, P * q:P * (q + 1)], bcT[:, 2 + q // 3, 512:TP],
                                  start=True, stop=True)
                        for b in range(DB):
                            last = pe.matmul(out[:, TAILP + DT * b:TAILP + DT * (b + 1)], s_smp[:, b, P * q:P * (q + 1)],
                                             bcT[:, 2 + q // 3, TP + DT * b:TP + DT * (b + 1)], start=True, stop=True)
                    last.then_inc(yT_done, 1)
                    pe.wait_ge(yT_out, 1)
                    for q in range(6):
                        last = pe.transpose(y_ps[q // 3][0:n, P * (q % 3):P * (q % 3 + 1)], yT[:, q, :], ident[:, :])
                    last.then_inc(inter_done, 1)
                pe.wait_ge(inter_out, i + 1)
                pe.wait_ge(w_ready, i + 1)
                pe.wait_ge(x_ready, 2 * i + 2)
                for h in range(HB):
                    last = pe.matmul(y_ps[h // 6][0:n, PB * (h % 6):PB * (h % 6 + 1)], dec[0:n, h, 0:n],
                                     xdt[0:n, PB * h:PB * (h + 1)], start=True, stop=True)
                last.then_inc(intra, 1)
                rows = n if i < 4 else TAILP
                for k in range(2):
                    last = pe.matmul(s_ps[k][:, :], tm[0:rows, i, T_B + P * k:T_B + P * (k + 1)],
                                     xdtw[0:rows, 384 * k:384 * (k + 1)], start=True, stop=True)
                last.then_inc(s_done, 1)
            pe.wait_ge(own_ready, 1)
            for u in range(12):
                q, half = divmod(u, 2)
                if u >= 2:
                    pe.wait_ge(upd_out, u - 1)
                pe.matmul(rows_ps[1 + u % 2][:, :, :], xdtw[0:TAIL, P * q:P * (q + 1)],
                          b_own[:, q // 3, 4 * half:4 * half + 4, :], start=True, stop=True).then_inc(upd, 1)
            pe.wait_ge(s_ready, 6)
            for q in range(6):
                last = pe.transpose(s_ps[q // 3][:, P * (q % 3):P * (q % 3 + 1)], sT[:, P * q:P * (q + 1)], ident[:, :])
            last.then_inc(sT_turned, 1)

        @block.scalar
        def _(act):
            for q in range(24):
                act.wait_ge(turned, q + 1)
                b, pair = divmod(2 * q, 6)
                act.activation(s_smp[:, b, P * pair:P * (pair + 2)], s_ps[q % 2][:, 0:2 * P], ACT.Copy
                               ).then_inc(turned_out, 1)
            for i in range(5):
                n = NT[i]
                act.wait_ge(dif, i + 1)
                act.activation(dec[0:n, :, 0:n], dec[0:n, :, 0:n], ACT.Exp).then_inc(dec_ready, 1)
                if i == 4:
                    act.wait_ge(yT_done, 1)
                    act.activation(yT[:, :, :], rows_ps[0][:, :, :].rearrange("p a b -> p (a b)")[:, 0:6 * TAIL]
                                   .rearrange("p (q t) -> p q t", q=6), ACT.Copy).then_inc(yT_out, 1)
            for k in range(2):
                act.wait_ge(sT_turned, 1)
                act.activation(s_out[:, 3 * k:3 * k + 3, :], s_ps[k][:, :].rearrange("p (q n) -> p q n", q=3), ACT.Copy
                               ).then_inc(sT_out, 1)

        @block.vector
        def _(dve):
            step = Chain(dve, chain)
            dve.memset(sT[:, :], 0.0).then_inc(s_ready, 1)
            for i in range(5):
                n, m = NT[i], P * (i == 4)
                dve.wait_ge(rows_done, i + 1)
                if i:
                    dve.wait_ge(intra, i)
                for h in range(HB):
                    last = dve.tensor_scalar(dec[0:n, h, 0:n], rows_ps[h // 4][0:n, h % 4, 0:n],
                                             sb["cum"][0:n, i, h:h + 1], 0.0, ALU.subtract, ALU.min)
                last.then_inc(dif, 1)
                dve.wait_ge(g_done, i + 1)
                dve.tensor_tensor(gm[0:n, :, 0:n], g_ps[0:n, :, 0:n],
                                  bc(sb["upto"][0:n, m:m + n].unsqueeze(1), [n, 2, n]), ALU.mult).then_inc(gm_ready, 1)
                dve.wait_ge(inter_done, i + 1)
                dve.wait_ge(skip_ready, i + 1)
                for k in range(2):
                    last = dve.tensor_tensor(h3(y[0:n, i, 384 * k:384 * (k + 1)], 6), h3(y_ps[k][0:n, :], 6),
                                             bc(sb["ecum"][0:n, i, 6 * k:6 * k + 6].unsqueeze(2), [n, 6, PB]), ALU.mult)
                last.then_inc(inter_out, 1)
                dve.wait_ge(gm_ready, i + 1)
                dve.wait_ge(dec_ready, i + 1)
                for k in range(2):
                    last = dve.tensor_tensor(dec[0:n, 6 * k:6 * k + 6, 0:n], dec[0:n, 6 * k:6 * k + 6, 0:n],
                                             bc(gm[0:n, k, 0:n].unsqueeze(1), [n, 6, n]), ALU.mult)
                last.then_inc(w_ready, 1)
                dve.wait_ge(inter_out, i + 1)
                step(dve.tensor_tensor(y[0:n, i, :], y[0:n, i, :], skip[0:n, :], ALU.add))
                dve.wait_ge(inter_done, i + 1)
                step(dve.tensor_tensor(h3(sT[:, :], HB), h3(sT[:, :], HB),
                                       bc(sb["el"][:, i, 0:12].unsqueeze(2), [P, HB, PB]), ALU.mult))
                dve.wait_ge(intra, i + 1)
                for k in range(2):
                    last = dve.tensor_tensor(y[0:n, i, 384 * k:384 * (k + 1)], y[0:n, i, 384 * k:384 * (k + 1)],
                                             y_ps[k][0:n, :], ALU.add)
                last.then_inc(intra_out, 1)
                dve.wait_ge(s_done, i + 1)
                for k in range(2):
                    last = dve.tensor_tensor(sT[:, 384 * k:384 * (k + 1)], sT[:, 384 * k:384 * (k + 1)], s_ps[k][:, :],
                                             ALU.add)
                last.then_inc(s_ready, 1)
            for k in range(2):
                for b in range(DB):
                    last = dve.tensor_scalar(b_own[:, k, b, :], tm[0:TAIL, 4, T_B + P * k:T_B + P * (k + 1)],
                                             sb["members"][0:TAIL, b + 1:b + 2], None, ALU.mult)
            last.then_inc(own_ready, 1)
            dve.wait_ge(el_ready, 2)
            for u in range(12):
                q, half = divmod(u, 2)
                s = s_nat[:, 4 * half:4 * half + 4, q, :]
                step(dve.tensor_tensor(s, s, bc(el_nat[:, q, 4 * half:4 * half + 4].unsqueeze(2), [P, 4, NB]), ALU.mult))
                dve.wait_ge(upd, u + 1)
                dve.tensor_tensor(s, s, rows_ps[1 + u % 2][:, :, :], ALU.add).then_inc(upd_out, 1)


def gdn_prepare(nc, dram, consts, sb):
    with ExitStack() as ctx:
        sem = lambda n: ctx.enter_context(nc.semaphore(f"gp_{n}"))
        sbuf = lambda n, s: ctx.enter_context(nc.sbuf_tensor(f"gp_{n}", s, F32))
        psum = lambda n, s: ctx.enter_context(nc.psum_tensor(f"gp_{n}", s, F32))
        tm, kbq, atT, ttT = sb["tm"], sb["kbq"], sb["atT"], sb["ttT"]
        level = [sbuf("level", [P, 7 * P]), sbuf("level_tail", [P, 4 * P])]
        sq, kb = sbuf("sq", [P, 12, P]), sbuf("kb", [P, DC])
        kT, lT, mT, t, p1, dec, decU = (sbuf(n, [P, HC, P]) for n in ("kT", "lT", "mT", "t", "p1", "dec", "decU"))
        a_ps = [psum(f"a{n}", [P, 4, P]) for n in range(2)]
        b_ps = [psum(f"b{n}", [P, 4, P]) for n in range(2)]
        c_ps = [psum(f"c{n}", [P, 4, P]) for n in range(3)]
        names = ("level_in", "sq_ready", "summed", "root", "chain", "scaled", "kb_ready", "turned", "k_out", "kbq_out",
                 "rows_done", "dif", "dec_ready", "decU_ready", "products", "lt_ready", "tile_done", "m_ready", "p1_done",
                 "p1_out", "q_done", "t_ready")
        s = {n: sem(n) for n in names}
        rn = sb["rn"]
        parts = ((0, slice(0, 4)), (1, slice(4, 6)))
        nlev = lambda i: 7 if i < 4 else 4
        lev0 = lambda i: 7 * i
        block = ctx.enter_context(nc.Block())

        @block.sync
        def _(sp):
            sp.dma_start(level[0][:, :], consts["c_level"]).then_inc(s["level_in"], 16)
            sp.dma_start(level[1][:, :], consts["c_level_tail"]).then_inc(s["level_in"], 16)

        @block.scalar
        def _(act):
            for i in range(5):
                n = NT[i]
                if i:
                    act.wait_ge(s["summed"], i)
                act.activation(sq[0:n, :, :], tm[0:n, i, T_GQ:T_GV].rearrange("p (h e) -> p h e", h=12), ACT.Square
                               ).then_inc(s["sq_ready"], 1)
            act.wait_ge(s["summed"], 5)
            act.activation(rn[:, :, :], rn[:, :, :], ACT.Sqrt, bias=sb["eps"][:, 0:1]).then_inc(s["root"], 1)
            for i in range(5):
                n = NT[i]
                for h in range(HC):
                    act.wait_ge(s["turned"], 6 * i + h + 1)
                    if h == 0 and i:
                        act.wait_ge(s["products"], i)
                    act.activation(kT[:, h, 0:n], a_ps[h % 2][:, 0, 0:n], ACT.Copy).then_inc(s["k_out"], 1)
                act.wait_ge(s["dif"], i + 1)
                act.activation(dec[0:n, :, 0:n], dec[0:n, :, 0:n], ACT.Exp).then_inc(s["dec_ready"], 1)
                for lev in range(1, nlev(i)):
                    k = lev0(i) + lev
                    act.wait_ge(s["p1_done"], k + 1)
                    for bank, hs in parts:
                        last = act.activation(p1[0:n, hs, 0:n], a_ps[bank][0:n, 0:hs.stop - hs.start, 0:n], ACT.Copy)
                    last.then_inc(s["p1_out"], 1)

        @block.gpsimd
        def _(pool):
            pool.wait_ge(s["level_in"], 32)
            for i in range(5):
                n, m = NT[i], P * (i == 4)
                pool.wait_ge(s["dec_ready"], i + 1)
                pool.tensor_tensor(decU[0:n, :, 0:n], dec[0:n, :, 0:n],
                                   bc(sb["upto"][0:n, m:m + n].unsqueeze(1), [n, HC, n]), ALU.mult
                                   ).then_inc(s["decU_ready"], 1)
                pool.wait_ge(s["lt_ready"], i + 1)
                for lev in range(nlev(i)):
                    k = lev0(i) + lev
                    if k:
                        pool.wait_ge(s["p1_done"], k)
                    if lev == 1:
                        pool.wait_ge(s["t_ready"], k)
                    mask = level[i == 4][0:n, P * lev:P * lev + n]
                    pool.tensor_tensor(mT[0:n, :, 0:n], lT[0:n, :, 0:n], bc(mask.unsqueeze(1), [n, HC, n]), ALU.mult
                                       ).then_inc(s["m_ready"], 1)

        @block.tensor
        def _(pe):
            ident = sb["ident"]
            for i in range(5):
                n, m = NT[i], P * (i == 4)
                tok = slice(P * i, P * i + n)
                pe.wait_ge(s["scaled"], i + 1)
                pe.wait_ge(s["kb_ready"], i + 1)
                for h in range(HC):
                    if h >= 2:
                        pe.wait_ge(s["k_out"], 6 * i + h - 1)
                        pe.wait_ge(s["kbq_out"], 6 * i + h - 1)
                    for x, src in enumerate((tm[0:n, i, T_GK + P * h:T_GK + P * (h + 1)], kb[0:n, P * h:P * (h + 1)],
                                             tm[0:n, i, T_GQ + P * h:T_GQ + P * (h + 1)])):
                        last = pe.transpose(a_ps[h % 2][:, x, 0:n], src, ident[0:n, 0:n])
                    last.then_inc(s["turned"], 1)
                for h in range(HC):
                    last = pe.matmul(b_ps[h // 4][:, h % 4, 0:n], bc(sb["g"][0:n, i, 12 + h:13 + h], [n, P]),
                                     sb["upto"][0:n, m:m + n], start=True, stop=True)
                last.then_inc(s["rows_done"], 1)
                pe.wait_ge(s["k_out"], 6 * i + 6)
                pe.wait_ge(s["kbq_out"], 6 * i + 6)
                for h in range(HC):
                    out = c_ps[h // 2][0:n, 2 * (h % 2):2 * (h % 2) + 2, 0:n]
                    last = pe.matmul(out, kT[:, h, 0:n], kbq[:, h, :, tok], start=True, stop=True)
                last.then_inc(s["products"], 1)
                for lev in range(nlev(i)):
                    k = lev0(i) + lev
                    pe.wait_ge(s["m_ready"], k + 1)
                    if lev:
                        pe.wait_ge(s["t_ready"], k)
                    for h in range(HC):
                        rhs = t[0:n, h, 0:n] if lev else ident[0:n, 0:n]
                        last = pe.matmul(a_ps[h // 4][0:n, h % 4, 0:n], mT[0:n, h, 0:n], rhs, start=True, stop=True)
                    last.then_inc(s["p1_done"], 1)
                    if lev:
                        pe.wait_ge(s["p1_out"], p1_count(i, lev))
                        if lev < nlev(i) - 1:
                            for h in range(HC):
                                pe.matmul(b_ps[h // 4][0:n, h % 4, 0:n], ttT[0:n, h, tok], p1[0:n, h, 0:n],
                                          start=True, stop=True)
                        for h in range(HC):
                            last = pe.matmul(c_ps[h // 4][0:n, h % 4, 0:n], p1[0:n, h, 0:n], ttT[0:n, h, tok],
                                             start=True, stop=True)
                        last.then_inc(s["q_done"], 1)
                pe.wait_ge(s["t_ready"], lev0(i) + nlev(i))

        @block.vector
        def _(dve):
            step = Chain(dve, s["chain"])
            step(dve.memset(rn[:, :, :], 1.0))
            for i in range(5):
                n = NT[i]
                dve.wait_ge(s["sq_ready"], i + 1)
                dve.tensor_reduce(rn[0:n, i, :], sq[0:n, :, :], AX.X, ALU.add).then_inc(s["summed"], 1)
            dve.wait_ge(s["root"], 1)
            step(dve.reciprocal(rn[:, :, :], rn[:, :, :]))
            step(dve.tensor_scalar(rn[:, :, 0:6], rn[:, :, 0:6], float(DK) ** -0.5, None, ALU.mult))
            for i in range(5):
                n, m = NT[i], P * (i == 4)
                tok = slice(P * i, P * i + n)
                qk = tm[0:n, i, T_GQ:T_GV].rearrange("p (h e) -> p h e", h=12)
                beta = bc(sb["beta"][0:n, i, :].unsqueeze(2), [n, HC, P])
                dve.tensor_tensor(qk, qk, bc(rn[0:n, i, :].unsqueeze(2), [n, 12, P]), ALU.mult).then_inc(s["scaled"], 1)
                dve.wait_ge(s["scaled"], i + 1)
                if i:
                    dve.wait_ge(s["turned"], 6 * i)
                dve.tensor_tensor(kb[0:n, :].rearrange("p (h e) -> p h e", h=HC), qk[:, 6:12, :], beta, ALU.mult
                                  ).then_inc(s["kb_ready"], 1)
                v = tm[0:n, i, T_GV:T_GV + DC].rearrange("p (h e) -> p h e", h=HC)
                dve.tensor_tensor(v, v, beta, ALU.mult)
                for h in range(HC):
                    dve.wait_ge(s["turned"], 6 * i + h + 1)
                    dve.wait_ge(s["k_out"], 6 * i + h + 1)
                    dve.tensor_copy(kbq[:, h, :, tok], a_ps[h % 2][:, 1:3, 0:n]).then_inc(s["kbq_out"], 1)
                dve.wait_ge(s["rows_done"], i + 1)
                if i:
                    dve.wait_ge(s["decU_ready"], i)
                for h in range(HC):
                    last = dve.tensor_scalar(dec[0:n, h, 0:n], b_ps[h // 4][0:n, h % 4, 0:n],
                                             sb["cum"][0:n, i, 12 + h:13 + h], 0.0, ALU.subtract, ALU.min)
                last.then_inc(s["dif"], 1)
                dve.wait_ge(s["products"], i + 1)
                dve.wait_ge(s["dec_ready"], i + 1)
                if i:
                    dve.wait_ge(s["m_ready"], lev0(i))
                for c in range(3):
                    both = c_ps[c][0:n, :, 0:n].rearrange("p (h x) t -> p x h t", x=2)
                    last = dve.tensor_tensor(lT[0:n, 2 * c:2 * c + 2, 0:n], both[:, 0], dec[0:n, 2 * c:2 * c + 2, 0:n],
                                             ALU.mult)
                last.then_inc(s["lt_ready"], 1)
                dve.wait_ge(s["decU_ready"], i + 1)
                for c in range(3):
                    both = c_ps[c][0:n, :, 0:n].rearrange("p (h x) t -> p x h t", x=2)
                    last = dve.tensor_tensor(atT[0:n, 2 * c:2 * c + 2, tok], both[:, 1], decU[0:n, 2 * c:2 * c + 2, 0:n],
                                             ALU.mult)
                step(last)
                for lev in range(nlev(i)):
                    k = lev0(i) + lev
                    if lev == 0:
                        dve.wait_ge(s["m_ready"], k + 1)
                        eye = sb["ident"][0:n, 0:n].unsqueeze(1)
                        step(dve.tensor_tensor(ttT[0:n, :, tok], bc(eye, [n, HC, n]), mT[0:n, :, 0:n], ALU.subtract))
                        dve.wait_ge(s["p1_done"], k + 1)
                        for bank, hs in parts:
                            w = hs.stop - hs.start
                            last = dve.tensor_tensor(t[0:n, hs, 0:n], bc(eye, [n, w, n]), a_ps[bank][0:n, 0:w, 0:n],
                                                     ALU.subtract)
                    else:
                        dve.wait_ge(s["q_done"], p1_count(i, lev))
                        for bank, hs in parts:
                            w = hs.stop - hs.start
                            last = dve.tensor_tensor(ttT[0:n, hs, tok], ttT[0:n, hs, tok], c_ps[bank][0:n, 0:w, 0:n],
                                                     ALU.subtract)
                            if lev < nlev(i) - 1:
                                last = dve.tensor_tensor(t[0:n, hs, 0:n], t[0:n, hs, 0:n], b_ps[bank][0:n, 0:w, 0:n],
                                                         ALU.subtract)
                    last.then_inc(s["t_ready"], 1)
                    dve.wait_ge(s["t_ready"], k + 1)


def p1_count(i, lev):
    return 6 * i + lev


def gdn_scan(nc, dram, sb):
    with ExitStack() as ctx:
        sem = lambda n: ctx.enter_context(nc.semaphore(f"gs_{n}"))
        sbuf = lambda n, s: ctx.enter_context(nc.sbuf_tensor(f"gs_{n}", s, F32))
        psum = lambda n: [ctx.enter_context(nc.psum_tensor(f"gs_{n}{x}", [P, 512], F32)) for x in range(2)]
        tm, kbq, atT, ttT, y = sb["tm"], sb["kbq"], sb["atT"], sb["ttT"], sb["y_gdn"]
        st, st_smp = sbuf("st", [P, HC, P]), sbuf("st_smp", [P, DB, HC, P])
        r, u, wk = sbuf("r", [P, HC, P]), sbuf("u", [P, HC, P]), sbuf("wk", [P, HC, P])
        inT, u_own = sbuf("inT", [P, HC, 2, TAIL]), sbuf("u_own", [TAIL, 2, DB, P])
        a_ps, b_ps, c_ps, d_ps = psum("a"), psum("b"), psum("c"), psum("d")
        names = ("loaded", "st_ready", "wk_ready", "inter", "r_ready", "q_out", "u_done", "u_out", "o_done", "o_out",
                 "upd", "upd_out", "inT_done", "inT_out", "own_ready", "saved", "chain", "s_done")
        s = {n: sem(n) for n in names}
        parts = ((0, slice(0, 4)), (1, slice(4, 6)))
        heads = lambda ps, n, w: ps[0:n, 0:w * P].rearrange("p (h e) -> p h e", h=w)
        block = ctx.enter_context(nc.Block())

        @block.sync
        def _(sp):
            for b in range(DB):
                sp.dma_start(st_smp[:, b], dram["state_gdn"][0, b].rearrange("h k v -> k h v")).then_inc(s["loaded"], 16)
            sp.wait_ge(s["st_ready"], 6)
            sp.dma_start(dram["gdn_prompt"][0, 0].rearrange("h k v -> k h v"), st[:, :, :]).then_inc(s["saved"], 16)
            sp.wait_ge(s["upd_out"], 12)
            for b in range(DB):
                sp.dma_start(dram["gdn_sample"][0, b].rearrange("h k v -> k h v"), st_smp[:, b]).then_inc(s["saved"], 16)
            sp.wait_ge(s["saved"], 144)

        @block.gpsimd
        def _(pool):
            for i in range(5):
                n = NT[i]
                if i:
                    pool.wait_ge(s["s_done"], i)
                k = tm[0:n, i, T_GK:T_GK + DC].rearrange("p (h e) -> p h e", h=HC)
                pool.tensor_tensor(wk[0:n, :, :], k, bc(sb["wend"][0:n, i, 12:18].unsqueeze(2), [n, HC, P]), ALU.mult
                                   ).then_inc(s["wk_ready"], 1)
            pool.wait_ge(s["u_out"], 5)
            for h in range(HC):
                if h >= 2:
                    pool.wait_ge(s["upd"], 2 * (h - 1))
                pool.tensor_tensor(u_own[:, h % 2], bc(u[0:TAIL, h, :].unsqueeze(1), [TAIL, DB, P]),
                                   bc(sb["members"][0:TAIL, 1:9].unsqueeze(2), [TAIL, DB, P]), ALU.mult
                                   ).then_inc(s["own_ready"], 1)

        @block.tensor
        def _(pe):
            for i in range(5):
                n = NT[i]
                tok = slice(P * i, P * i + n)
                pe.wait_ge(s["st_ready"], i + 1)
                if i:
                    pe.wait_ge(s["o_out"], i)
                if i < 4:
                    for x, ps in ((0, a_ps), (1, b_ps)):
                        for h in range(HC):
                            last = pe.matmul(ps[h // 4][0:n, P * (h % 4):P * (h % 4 + 1)], kbq[:, h, x, tok], st[:, h, :],
                                             start=True, stop=True)
                else:
                    pe.wait_ge(s["loaded"], 128)
                    for h in range(HC):
                        out = d_ps[h // 3][:, 96 * (h % 3):96 * (h % 3 + 1)].rearrange("p (x t) -> p x t", x=2)
                        pe.matmul(out[:, :, 0:TAILP], st[:, h, :], kbq[:, h, :, 512:TP], start=True, stop=True)
                        for b in range(DB):
                            c = TAILP + DT * b
                            last = pe.matmul(out[:, :, c:c + DT], st_smp[:, b, h, :], kbq[:, h, :, 512 + c:512 + c + DT],
                                             start=True, stop=True)
                    last.then_inc(s["inT_done"], 1)
                    pe.wait_ge(s["inT_out"], 1)
                    for x, ps in ((0, a_ps), (1, b_ps)):
                        for h in range(HC):
                            last = pe.transpose(ps[h // 4][0:n, P * (h % 4):P * (h % 4 + 1)], inT[:, h, x, :],
                                                sb["ident"][:, :])
                last.then_inc(s["inter"], 1)
                pe.wait_ge(s["r_ready"], i + 1)
                for h in range(HC):
                    last = pe.matmul(c_ps[h // 4][0:n, P * (h % 4):P * (h % 4 + 1)], ttT[0:n, h, tok], r[0:n, h, :],
                                     start=True, stop=True)
                last.then_inc(s["u_done"], 1)
                pe.wait_ge(s["u_out"], i + 1)
                pe.wait_ge(s["wk_ready"], i + 1)
                rows = n if i < 4 else TAILP
                for h in range(HC):
                    last = pe.matmul(a_ps[h // 4][:, P * (h % 4):P * (h % 4 + 1)], wk[0:rows, h, :], u[0:rows, h, :],
                                     start=True, stop=True)
                last.then_inc(s["s_done"], 1)
                for h in range(HC):
                    last = pe.matmul(d_ps[h // 4][0:n, P * (h % 4):P * (h % 4 + 1)], atT[0:n, h, tok], u[0:n, h, :],
                                     start=True, stop=True)
                last.then_inc(s["o_done"], 1)
            for x in range(12):
                h, half = divmod(x, 2)
                pe.wait_ge(s["own_ready"], h + 1)
                if x >= 2:
                    pe.wait_ge(s["upd_out"], x - 1)
                pe.matmul(c_ps[x % 2][:, :], wk[0:TAIL, h, :], u_own[:, h % 2, 4 * half:4 * half + 4, :],
                          start=True, stop=True).then_inc(s["upd"], 1)

        @block.scalar
        def _(act):
            for i in range(5):
                n = NT[i]
                if i == 4:
                    act.wait_ge(s["inT_done"], 1)
                    for x in range(2):
                        last = act.activation(inT[:, 3 * x:3 * x + 3].rearrange("p h x t -> p (h x t)"),
                                              d_ps[x][:, 0:288], ACT.Copy)
                    last.then_inc(s["inT_out"], 1)
                act.wait_ge(s["u_done"], i + 1)
                if i:
                    act.wait_ge(s["o_done"], i)
                for bank, hs in parts:
                    last = act.activation(u[0:n, hs, :], heads(c_ps[bank], n, hs.stop - hs.start), ACT.Copy)
                last.then_inc(s["u_out"], 1)

        @block.vector
        def _(dve):
            step = Chain(dve, s["chain"])
            dve.memset(st[:, :, :], 0.0).then_inc(s["st_ready"], 1)
            for i in range(5):
                n = NT[i]
                ecum = sb["ecum"][0:n, i, 12:18]
                yi = y[0:n, i, :].rearrange("p (h e) -> p h e", h=HC)
                dve.wait_ge(s["inter"], i + 1)
                for bank, hs in parts:
                    w = hs.stop - hs.start
                    last = dve.tensor_tensor(r[0:n, hs, :], heads(a_ps[bank], n, w), bc(ecum[:, hs].unsqueeze(2), [n, w, P]),
                                             ALU.mult)
                step(last)
                dve.tensor_tensor(r[0:n, :, :], tm[0:n, i, T_GV:T_GV + DC].rearrange("p (h e) -> p h e", h=HC),
                                  r[0:n, :, :], ALU.subtract).then_inc(s["r_ready"], 1)
                for bank, hs in parts:
                    w = hs.stop - hs.start
                    last = dve.tensor_tensor(yi[:, hs, :], heads(b_ps[bank], n, w), bc(ecum[:, hs].unsqueeze(2), [n, w, P]),
                                             ALU.mult)
                step(last)
                step(dve.tensor_tensor(st[:, :, :], st[:, :, :], bc(sb["el"][:, i, 12:18].unsqueeze(2), [P, HC, P]),
                                       ALU.mult))
                dve.wait_ge(s["s_done"], i + 1)
                for bank, hs in parts:
                    last = dve.tensor_tensor(st[:, hs, :], st[:, hs, :], heads(a_ps[bank], P, hs.stop - hs.start), ALU.add)
                last.then_inc(s["st_ready"], 1)
                dve.wait_ge(s["o_done"], i + 1)
                for bank, hs in parts:
                    last = dve.tensor_tensor(yi[:, hs, :], yi[:, hs, :], heads(d_ps[bank], n, hs.stop - hs.start), ALU.add)
                last.then_inc(s["o_out"], 1)
            for x in range(12):
                h, half = divmod(x, 2)
                now = st_smp[:, 4 * half:4 * half + 4, h, :]
                decay = sb["el"][:, 5 + 4 * half:9 + 4 * half, 12 + h:13 + h]
                step(dve.tensor_tensor(now, now, bc(decay, [P, 4, P]), ALU.mult))
                dve.wait_ge(s["upd"], x + 1)
                dve.tensor_tensor(now, now, c_ps[x % 2][:, :].rearrange("p (b e) -> p b e", b=4), ALU.add
                                  ).then_inc(s["upd_out"], 1)


def gate_and_norm(nc, dram, sb):
    with ExitStack() as ctx:
        sem = lambda n: ctx.enter_context(nc.semaphore(f"gn_{n}"))
        sbuf = lambda n, s: ctx.enter_context(nc.sbuf_tensor(f"gn_{n}", s, F32))
        z, norm_b, norm_c = sbuf("z", [P, 5, 2 * DBm]), sbuf("norm_b", [P, DBm]), sbuf("norm_c", [P, DK])
        sq, ss, mix = sbuf("sq", [P, DC]), sbuf("ss", [P, 5, 8]), sbuf("mix", [P, 12, TOK])
        ps = [ctx.enter_context(nc.psum_tensor(f"gn_ps{n}", [P, 4, P], F32)) for n in range(4)]
        names = ("par_in", "silu", "gated", "norm_c_done", "cleared", "sq_b", "sq_c", "ss_c", "root", "inv", "normed", "turned",
                 "out", "saved", "chain")
        s = {n: sem(n) for n in names}
        z_in = [sem(f"z_in{i}") for i in range(5)]
        yb, yc = sb["y_ssd"], sb["y_gdn"]
        block = ctx.enter_context(nc.Block())

        @block.sync
        def _(sp):
            sp.dma_start(norm_b[:, :], dram["ssm_norm"][0].partition_broadcast(P)).then_inc(s["par_in"], 16)
            sp.dma_start(norm_c[:, :], dram["gdn_norm"][0].partition_broadcast(P)).then_inc(s["par_in"], 16)
            for i in range(5):
                rows = slice(P * i, P * i + NT[i])
                sp.dma_start(z[0:NT[i], i, 0:DBm], dram["projN"][rows, N_ZB:N_ZB + DBm]).then_inc(z_in[i], 16)
                sp.dma_start(z[0:NT[i], i, DBm:], dram["projN"][rows, N_ZC:N_ZC + DC]).then_inc(z_in[i], 16)
            sp.wait_ge(s["out"], 15)
            sp.dma_start(dram["mixT"][:, 4 * TOK:], mix[:, :, :].rearrange("p k t -> p (k t)")).then_inc(s["saved"], 16)
            sp.wait_ge(s["saved"], 16)

        @block.scalar
        def _(act):
            for i in range(5):
                n = NT[i]
                act.wait_ge(z_in[i], 32)
                act.activation(z[0:n, i, :], z[0:n, i, :], ACT.Silu).then_inc(s["silu"], 1)
            act.wait_ge(s["cleared"], 1)
            for i in range(5):
                n = NT[i]
                act.wait_ge(s["gated"], i + 1)
                for k in range(2):
                    if i or k:
                        act.wait_ge(s["sq_b"], 2 * i + k)
                    if i and k == 0:
                        act.wait_ge(s["ss_c"], i)
                    act.activation(sq[0:n, 0:384], yb[0:n, i, 384 * k:384 * (k + 1)], ACT.Square,
                                   accum_out=ss[0:n, i, k:k + 1]).then_inc(s["sq_b"], 1)
                act.wait_ge(s["sq_b"], 2 * i + 2)
                act.activation(sq[0:n, :], yc[0:n, i, :], ACT.Square).then_inc(s["sq_c"], 1)
            act.wait_ge(s["sq_b"], 10)
            act.wait_ge(s["ss_c"], 5)
            act.activation(ss[:, :, 0:2], ss[:, :, 0:2], ACT.Sqrt, bias=sb["eps"][:, 0:1], scale=1.0 / 384
                           ).then_inc(s["root"], 1)
            act.activation(ss[:, :, 2:8], ss[:, :, 2:8], ACT.Sqrt, bias=sb["eps"][:, 0:1], scale=1.0 / DK
                           ).then_inc(s["root"], 1)

        @block.gpsimd
        def _(pool):
            pool.wait_ge(s["par_in"], 32)
            for i in range(5):
                n = NT[i]
                pool.wait_ge(s["silu"], i + 1)
                zc = z[0:n, i, DBm:].rearrange("p (h e) -> p h e", h=HC)
                pool.tensor_tensor(zc, zc, bc(norm_c[0:n, :].unsqueeze(1), [n, HC, DK]), ALU.mult
                                   ).then_inc(s["norm_c_done"], 1)

        @block.vector
        def _(dve):
            step = Chain(dve, s["chain"])
            dve.wait_ge(s["par_in"], 32)
            dve.memset(ss[:, :, :], 1.0).then_inc(s["cleared"], 1)
            for i in range(5):
                n = NT[i]
                dve.wait_ge(s["silu"], i + 1)
                dve.tensor_tensor(yb[0:n, i, :], yb[0:n, i, :], z[0:n, i, 0:DBm], ALU.mult).then_inc(s["gated"], 1)
            dve.wait_ge(s["cleared"], 1)
            for i in range(5):
                n = NT[i]
                dve.wait_ge(s["sq_c"], i + 1)
                dve.tensor_reduce(ss[0:n, i, 2:8], sq[0:n, :].rearrange("p (h e) -> p h e", h=HC), AX.X, ALU.add
                                  ).then_inc(s["ss_c"], 1)
            dve.wait_ge(s["root"], 2)
            step(dve.reciprocal(ss[:, :, :], ss[:, :, :]))
            dve.wait_ge(s["norm_c_done"], 5)
            for i in range(6):
                if i < 5:
                    n = NT[i]
                    for k in range(2):
                        part = slice(384 * k, 384 * (k + 1))
                        dve.scalar_tensor_tensor(out=yb[0:n, i, part], in0=yb[0:n, i, part], scalar=ss[0:n, i, k:k + 1],
                                                 in1=norm_b[0:n, part], op0=ALU.mult, op1=ALU.mult)
                    y3 = yc[0:n, i, :].rearrange("p (h e) -> p h e", h=HC)
                    step(dve.tensor_tensor(y3, y3, bc(ss[0:n, i, 2:8].unsqueeze(2), [n, HC, DK]), ALU.mult))
                    dve.tensor_tensor(yc[0:n, i, :], yc[0:n, i, :], z[0:n, i, DBm:], ALU.mult).then_inc(s["normed"], 1)
                if i:
                    for g in range(3):
                        c = 3 * (i - 1) + g
                        m = NT[i - 1]
                        dve.wait_ge(s["turned"], c + 1)
                        dve.tensor_copy(mix[:, 4 * g:4 * g + 4, P * (i - 1):P * (i - 1) + m], ps[c % 4][:, :, 0:m]
                                        ).then_inc(s["out"], 1)

        @block.tensor
        def _(pe):
            for i in range(5):
                n = NT[i]
                pe.wait_ge(s["normed"], i + 1)
                for g in range(3):
                    c = 3 * i + g
                    if c >= 4:
                        pe.wait_ge(s["out"], c - 3)
                    for x in range(4):
                        f = 4 * g + x
                        src = (yb if f < 6 else yc)[0:n, i, P * (f % 6):P * (f % 6 + 1)]
                        last = pe.transpose(ps[c % 4][:, x, 0:n], src, sb["ident"][0:n, 0:n])
                    last.then_inc(s["turned"], 1)


def attention_inputs(nc, dram, consts, sb):
    with ExitStack() as ctx:
        sem = lambda n: ctx.enter_context(nc.semaphore(f"ai_{n}"))
        sbuf = lambda n, s: ctx.enter_context(nc.sbuf_tensor(f"ai_{n}", s, F32))
        psum = lambda n: ctx.enter_context(nc.psum_tensor(f"ai_{n}", [P, 4, P], F32))
        qk, qn, kn = sbuf("qk", [P, 5, 2 * DA]), sbuf("qn", [P, DH]), sbuf("kn", [P, DH])
        sq, ss = sbuf("sq", [P, 8, DH]), sbuf("ss", [P, 5, 8])
        ki2 = sbuf("ki2", [P, 5, 2, DI])
        rb, onehot, rows = sbuf("rb", [32, HA]), sbuf("onehot", [32, 768]), sbuf("rows", [P, HA, 768])
        ps = [psum(f"ps{n}") for n in range(4)]
        row_ps = [ctx.enter_context(nc.psum_tensor(f"ai_row{n}", [P, 384], F32)) for n in range(2)]
        names = ("par_in", "sq_ready", "summed", "root", "chain", "normed", "turned", "out", "saved", "row", "row_out",
                 "skewed", "bias_in", "copied", "w_scaled", "cleared", "ki_in")
        s = {n: sem(n) for n in names}
        qk_in = [sem(f"qk_in{i}") for i in range(5)]
        v_tok, wi = sb["v_tok"], sb["wi"]
        block = ctx.enter_context(nc.Block())

        @block.sync
        def _(sp):
            sp.dma_start(qn[:, :], dram["q_norm"][0].partition_broadcast(P)).then_inc(s["par_in"], 16)
            sp.dma_start(kn[:, :], dram["k_norm"][0].partition_broadcast(P)).then_inc(s["par_in"], 16)
            sp.dma_start(rb[:, :], dram["rel_bias"]).then_inc(s["par_in"], 16)
            sp.dma_start(onehot[:, :], consts["c_onehot"]).then_inc(s["par_in"], 16)
            sp.dma_start(sb["causal"][:, :], consts["c_causal"]).then_inc(s["par_in"], 16)
            for i in range(5):
                rows_ = slice(P * i, P * i + NT[i])
                sp.dma_start(qk[0:NT[i], i, :], dram["projN"][rows_, 0:2 * DA]).then_inc(qk_in[i], 16)
            for i in range(5):
                rows_ = slice(P * i, P * i + NT[i])
                for x in range(2):
                    sp.dma_start(ki2[0:NT[i], i, x, :], dram["projN"][rows_, N_KI:N_KI + DI]).then_inc(s["ki_in"], 16)
                sp.dma_start(wi[0:NT[i], i, :], dram["projN"][rows_, N_WI:N_WI + HI]).then_inc(s["ki_in"], 16)
                sp.dma_start(v_tok[0:NT[i], i, :], dram["projN"][rows_, N_V:N_V + DA]).then_inc(s["ki_in"], 16)
            sp.dma_start(sb["qiT"][:, :, :], dram["projT"][0:HI * DI, :].rearrange("(k p) t -> p k t", p=P)
                         ).then_inc(s["ki_in"], 16)
            new = dram["projN"]
            for dst, rows_, c, n in (("v_prompt", slice(0, TP), N_V, DA), ("v_sample", slice(TP, TOK), N_V, DA),
                                     ("kidx_prompt", slice(0, TP), N_KI, DI), ("kidx_sample", slice(TP, TOK), N_KI, DI)):
                out = dram[dst]
                out = out.rearrange("a b t h d -> (a b t) (h d)") if len(out.shape) == 5 else out.rearrange(
                    "a b t d -> (a b t) d")
                sp.dma_start(out, new[rows_, c:c + n]).then_inc(s["copied"], 16)
            for h in range(HA):
                sp.wait_ge(s["row_out"], 2 * h + 2)
                sp.dma_start(dram["skew"][h].rearrange("(p m) -> p m", p=P), rows[:, h, :]).then_inc(s["skewed"], 16)
            sp.wait_ge(s["skewed"], 64)
            skew = dram["skew"]
            for h in range(HA):
                src = AP(tensor=skew.tensor, offset=skew[h].offset + 127, ap=[[767, P], [1, 640]])
                sp.dma_start(sb["toe"][:, h, :], src).then_inc(s["bias_in"], 16)
            kp = dram["k_prompt"].rearrange("a b t h d -> (a b t) (h d)")
            ks = dram["k_sample"].rearrange("a b t h d -> (a b t) (h d)")
            for i in range(5):
                sp.wait_ge(s["normed"], i + 1)
                n = NT[i] if i < 4 else TAILP
                sp.dma_start(kp[P * i:P * i + n, :], qk[0:n, i, DA:]).then_inc(s["saved"], 16)
            sp.dma_start(ks, qk[TAILP:TAIL, 4, DA:]).then_inc(s["saved"], 16)
            sp.wait_ge(s["saved"], 96)
            sp.wait_ge(s["copied"], 64)
            sp.wait_ge(s["bias_in"], 64)
            sp.wait_ge(s["ki_in"], 16 * 21)

        @block.scalar
        def _(act):
            for i in range(5):
                n = NT[i]
                act.wait_ge(qk_in[i], 16)
                if i:
                    act.wait_ge(s["summed"], i)
                act.activation(sq[0:n, :, :], qk[0:n, i, :].rearrange("p (h e) -> p h e", h=8), ACT.Square
                               ).then_inc(s["sq_ready"], 1)
            act.wait_ge(s["summed"], 5)
            act.activation(ss[:, :, :], ss[:, :, :], ACT.Sqrt, bias=sb["eps"][:, 0:1], scale=1.0 / DH
                           ).then_inc(s["root"], 1)

        @block.vector
        def _(dve):
            step = Chain(dve, s["chain"])
            step(dve.memset(ss[:, :, :], 1.0))
            dve.wait_ge(s["par_in"], 80)
            step(dve.tensor_scalar(qn[:, :], qn[:, :], float(DH) ** -0.5, None, ALU.mult))
            for i in range(5):
                n = NT[i]
                dve.wait_ge(s["sq_ready"], i + 1)
                dve.tensor_reduce(ss[0:n, i, :], sq[0:n, :, :], AX.X, ALU.add).then_inc(s["summed"], 1)
            for x in range(8):
                dve.wait_ge(s["row"], x + 1)
                dve.tensor_copy(rows[:, x // 2, 384 * (x % 2):384 * (x % 2 + 1)], row_ps[x % 2][:, :]
                                ).then_inc(s["row_out"], 1)
            dve.wait_ge(s["root"], 1)
            step(dve.reciprocal(ss[:, :, :], ss[:, :, :]))
            for i in range(5):
                n = NT[i]
                qk3 = qk[0:n, i, :].rearrange("p (h e) -> p h e", h=8)
                step(dve.tensor_tensor(qk3, qk3, bc(ss[0:n, i, :].unsqueeze(2), [n, 8, DH]), ALU.mult))
                dve.tensor_tensor(qk3[:, 0:4, :], qk3[:, 0:4, :], bc(qn[0:n, :].unsqueeze(1), [n, 4, DH]), ALU.mult)
                dve.tensor_tensor(qk3[:, 4:8, :], qk3[:, 4:8, :], bc(kn[0:n, :].unsqueeze(1), [n, 4, DH]), ALU.mult
                                  ).then_inc(s["normed"], 1)
            dve.wait_ge(s["ki_in"], 16 * 21)
            for i in range(5):
                last = dve.tensor_scalar(wi[0:NT[i], i, :], wi[0:NT[i], i, :], float(HI * DI) ** -0.5, None, ALU.mult)
            last.then_inc(s["w_scaled"], 1)
            for i in range(5):
                n, tok = NT[i], slice(P * i, P * i + NT[i])
                for x, dst in enumerate((sb["qT"][:, :, tok], sb["kT"][:, :, tok], sb["kiT"][:, tok])):
                    c = 3 * i + x
                    dve.wait_ge(s["turned"], c + 1)
                    src = ps[c % 4][:, :, 0:n] if x < 2 else ps[c % 4][:, 0, 0:n]
                    dve.tensor_copy(dst, src).then_inc(s["out"], 1)

        @block.tensor
        def _(pe):
            pe.wait_ge(s["par_in"], 80)
            for x in range(8):
                if x >= 2:
                    pe.wait_ge(s["row_out"], x - 1)
                pe.matmul(row_ps[x % 2][:, :], bc(rb[:, x // 2:x // 2 + 1], [32, P]),
                          onehot[:, 384 * (x % 2):384 * (x % 2 + 1)], start=True, stop=True).then_inc(s["row"], 1)
            pe.wait_ge(s["ki_in"], 16 * 21)
            for i in range(5):
                n = NT[i]
                eye = sb["ident"][0:n, 0:n]
                pe.wait_ge(s["normed"], i + 1)
                for x in range(3):
                    c = 3 * i + x
                    if c >= 4:
                        pe.wait_ge(s["out"], c - 3)
                    if x < 2:
                        for h in range(HA):
                            last = pe.transpose(ps[c % 4][:, h, 0:n], qk[0:n, i, DA * x + DH * h:DA * x + DH * (h + 1)],
                                                eye)
                    else:
                        last = pe.transpose(ps[c % 4][:, 0, 0:n], ki2[0:n, i].rearrange("p x d -> p (x d)"), eye)
                    last.then_inc(s["turned"], 1)


def attend_prompt(nc, dram, sb):
    with ExitStack() as ctx:
        sem = lambda n: ctx.enter_context(nc.semaphore(f"ap_{n}"))
        sbuf = lambda n, s: ctx.enter_context(nc.sbuf_tensor(f"ap_{n}", s, F32))
        qT, kT, kiT, qiT, toe = (sb[n] for n in ("qT", "kT", "kiT", "qiT", "toe"))
        relu, sc = sbuf("relu", [P, 2, TP]), sbuf("sc", [P, 2, TP])
        best, bm, lg = sbuf("best", [P, 2, 8]), sbuf("bm", [P, 2, TP]), sbuf("lg", [P, 2, TP])
        mx, den = sbuf("mx", [P, 2]), sbuf("den", [P, 2])
        pT = sbuf("pT", [P, 2, 512])
        outT = sbuf("outT", [P, HA, TP])
        s_ps = [ctx.enter_context(nc.psum_tensor(f"ap_s{n}", [P, 1024], F32)) for n in range(2)]
        t_ps = [ctx.enter_context(nc.psum_tensor(f"ap_t{n}", [P, 512], F32)) for n in range(2)]
        o_ps = [ctx.enter_context(nc.psum_tensor(f"ap_o{n}", [P, 4, P], F32)) for n in range(2)]
        names = ("score", "relu_out", "acc", "chain", "mask_ready", "bm_ready", "qk", "lg_ready", "exp_ready", "p_ready",
                 "turned", "pT_out", "pv", "o_out", "saved", "lg_out")
        s = {n: sem(n) for n in names}
        rows = [P, P, P, P, TAILP]
        keys = [P * (i + 1) for i in range(4)] + [TP]
        order = [("h", 0, h) for h in range(HA)]
        for i in range(1, 5):
            order += [("i", i, h) for h in range(HI)] + [("h", i, h) for h in range(HA)]
        nth = {o: n for n, o in enumerate(order)}
        relus = lambda i, h: HI * (i - 1) + h
        blocks = lambda i: [(P * b, min(P, keys[i] - P * b)) for b in range(i + 1)]
        block = ctx.enter_context(nc.Block())

        def freed(eng, n):
            kind, i, h = order[n - 2]
            if kind == "i":
                eng.wait_ge(s["relu_out"], relus(i, h) + 1)
            else:
                eng.wait_ge(s["lg_out"], HA * i + h + 1)

        @block.tensor
        def _(pe):
            def head_out(i, h):
                c, n = HA * i + h, rows[i]
                pe.wait_ge(s["p_ready"], c + 1)
                if c >= 2:
                    pe.wait_ge(s["pT_out"], c - 1)
                for b, (k0, kn) in enumerate(blocks(i)):
                    last = pe.transpose(t_ps[c % 2][0:kn, n * b:n * (b + 1)], lg[0:n, c % 2, k0:k0 + kn],
                                        sb["ident"][0:n, 0:n])
                last.then_inc(s["turned"], 1)
                pe.wait_ge(s["pT_out"], c + 1)
                if h == 0 and i >= 2:
                    pe.wait_ge(s["o_out"], i - 1)
                for b, (k0, kn) in enumerate(blocks(i)):
                    last = pe.matmul(o_ps[i % 2][:, h, 0:n], sb["v_tok"][0:kn, b, DH * h:DH * (h + 1)],
                                     pT[0:kn, c % 2, n * b:n * (b + 1)], start=(b == 0), stop=(b == i))
                last.then_inc(s["pv"], 1)

            done = None
            for x, (kind, i, h) in enumerate(order):
                n = rows[i]
                q = slice(P * i, P * i + n)
                if x >= 2:
                    freed(pe, x)
                for k0, kn in ((0, min(512, keys[i])), (512, keys[i] - 512)):
                    if kn <= 0:
                        continue
                    if kind == "i":
                        half = slice(DI * (h % 2), DI * (h % 2 + 1))
                        last = pe.matmul(s_ps[x % 2][0:n, k0:k0 + kn], qiT[half, h // 2, q], kiT[half, k0:k0 + kn],
                                         start=True, stop=True)
                    else:
                        last = pe.matmul(s_ps[x % 2][0:n, k0:k0 + kn], qT[:, h, q], kT[:, h, k0:k0 + kn],
                                         start=True, stop=True)
                last.then_inc(s["score"], 1)
                if done:
                    head_out(*done)
                done = (i, h) if kind == "h" else None
            head_out(*done)

        @block.scalar
        def _(act):
            for i in range(5):
                n, L = rows[i], keys[i]
                if i:
                    for h in range(HI):
                        x = nth["i", i, h]
                        act.wait_ge(s["score"], x + 1)
                        if relus(i, h) >= 2:
                            act.wait_ge(s["acc"], relus(i, h) - 1)
                        act.activation(relu[0:n, h % 2, 0:L], s_ps[x % 2][0:n, 0:L], ACT.Relu).then_inc(s["relu_out"], 1)
                for h in range(HA):
                    c = HA * i + h
                    act.wait_ge(s["lg_ready"], c + 1)
                    act.activation(lg[0:n, c % 2, 0:L], lg[0:n, c % 2, 0:L], ACT.Exp, bias=mx[0:n, c % 2:c % 2 + 1],
                                   accum_out=den[0:n, c % 2:c % 2 + 1]).then_inc(s["exp_ready"], 1)
                    act.wait_ge(s["turned"], c + 1)
                    if c >= 2:
                        act.wait_ge(s["pv"], c - 1)
                    for b, (k0, kn) in enumerate(blocks(i)):
                        if kn == P and b:
                            continue
                        w = n * (i + 1) if kn == P and i < 4 else n * i if kn == P else n
                        at = 0 if kn == P else n * b
                        last = act.activation(pT[0:kn, c % 2, at:at + w], t_ps[c % 2][0:kn, at:at + w], ACT.Copy)
                    last.then_inc(s["pT_out"], 1)

        @block.gpsimd
        def _(pool):
            for i in range(5):
                n, L = rows[i], keys[i]
                pool.wait_ge(s["mask_ready"], i + 1)
                for h in range(HA):
                    c = HA * i + h
                    if c >= 2:
                        pool.wait_ge(s["lg_out"], c - 1)
                    pool.tensor_tensor(bm[0:n, c % 2, 0:L], toe[0:n, h, 512 - P * i:512 - P * i + L], sc[0:n, i % 2, 0:L],
                                       ALU.add).then_inc(s["bm_ready"], 1)

        @block.vector
        def _(dve):
            step = Chain(dve, s["chain"])

            def choose(i):
                n, L = rows[i], keys[i]
                x = sc[0:n, i % 2, 0:L]
                diag = sc[0:n, i % 2, P * i:L]
                causal = sb["causal"][0:n, 0:L - P * i]
                if i >= 2:
                    dve.wait_ge(s["bm_ready"], HA * (i - 1))
                if i == 0:
                    dve.tensor_copy(diag, causal).then_inc(s["mask_ready"], 1)
                    return
                for h in range(HI):
                    dve.wait_ge(s["relu_out"], relus(i, h) + 1)
                    if h == 0:
                        ins = dve.tensor_scalar(x, relu[0:n, 0, 0:L], sb["wi"][0:n, i, 0:1], None, ALU.mult)
                    else:
                        ins = dve.scalar_tensor_tensor(out=x, in0=relu[0:n, h % 2, 0:L], scalar=sb["wi"][0:n, i, h:h + 1],
                                                       in1=x, op0=ALU.mult, op1=ALU.add)
                    ins.then_inc(s["acc"], 1)
                    dve.wait_ge(s["acc"], relus(i, h) + 1)
                step(dve.tensor_tensor(diag, diag, causal, ALU.add))
                for r in range(TOPP // 8):
                    step(dve.max(best[0:n, r % 2, :], x))
                    step(dve.match_replace(x, best[0:n, r % 2, :], x, TAKEN))
                step(dve.tensor_scalar(x, x, TAKEN, NEG, ALU.not_equal, ALU.mult))
                dve.tensor_tensor(diag, diag, causal, ALU.add).then_inc(s["mask_ready"], 1)

            def soften(i):
                n, L = rows[i], keys[i]
                for h in range(HA):
                    c = HA * i + h
                    x = nth["h", i, h]
                    one = lg[0:n, c % 2, 0:L]
                    dve.wait_ge(s["bm_ready"], c + 1)
                    dve.wait_ge(s["score"], x + 1)
                    if c >= 2:
                        dve.wait_ge(s["turned"], c - 1)
                    dve.tensor_tensor(one, s_ps[x % 2][0:n, 0:L], bm[0:n, c % 2, 0:L], ALU.add).then_inc(s["lg_out"], 1)
                    dve.wait_ge(s["lg_out"], c + 1)
                    dve.tensor_reduce(mx[0:n, c % 2:c % 2 + 1], one, AX.X, ALU.max, negate=True).then_inc(s["lg_ready"], 1)
                    dve.wait_ge(s["exp_ready"], c + 1)
                    step(dve.reciprocal(den[0:n, c % 2:c % 2 + 1], den[0:n, c % 2:c % 2 + 1]))
                    dve.tensor_scalar(one, one, den[0:n, c % 2:c % 2 + 1], None, ALU.mult).then_inc(s["p_ready"], 1)
                dve.wait_ge(s["pv"], HA * (i + 1))
                dve.tensor_copy(outT[:, :, P * i:P * i + n], o_ps[i % 2][:, :, 0:n]).then_inc(s["o_out"], 1)

            for i in range(5):
                choose(i)
                soften(i)

        @block.sync
        def _(sp):
            sp.wait_ge(s["o_out"], 5)
            for h in range(HA):
                sp.dma_start(dram["mixT"][:, TOK * h:TOK * h + TP], outT[:, h, :]).then_inc(s["saved"], 16)
            sp.wait_ge(s["saved"], 16 * HA)


def clear_semaphores(nc, sb):
    with nc.Block() as block:
        @block.gpsimd
        def _(pool):
            pool.sem_clear(range(sb["const_in"].num, bass.NUM_HW_SEMAPHORES))


NROW = TS * HA
NSEL = TOPS + DT
SKEYS = PAST + DT
RING = 8


def sample_constants():
    r = np.arange(NROW)
    tok, h = r // HA, r % HA
    b, t = tok // DT, tok % DT
    own = (h[:, None, None] == np.arange(HA)[None, :, None]) & (b[:, None, None] == np.arange(TS)[None, None, :] // DT)
    rows = np.concatenate([(np.arange(P) % 32)[:, None], (PAST + t)[:, None], h[:, None] == np.arange(HA),
                           b[:, None] == np.arange(DB), own.reshape(NROW, NROW)], axis=1)
    j = np.arange(TS)
    toks = np.concatenate([j[:, None] == tok[None, :], np.where(np.arange(DT)[None, :] > j[:, None] % DT, NEG, 0.0),
                           np.broadcast_to(PAST + np.arange(DT), (TS, DT))], axis=1)
    return {"c_rows": rows.astype(np.float32), "c_toks": toks.astype(np.float32)}


R_MOD, R_QPOS, R_HEAD, R_BATCH, R_OWN = 0, 1, 2, 2 + HA, 2 + HA + DB
T_REP, T_CAUSAL, T_NEWPOS = 0, NROW, NROW + DT


def sample_scores(nc, dram, consts, sb):
    with ExitStack() as ctx:
        sem = lambda n: ctx.enter_context(nc.semaphore(f"ss_{n}"))
        sbuf = lambda n, s, t=F32: ctx.enter_context(nc.sbuf_tensor(f"ss_{n}", s, t))
        psum = lambda n, s: ctx.enter_context(nc.psum_tensor(f"ss_{n}", s, F32))
        GR, NG = 4, PAST // 512
        pt_i, ptf, offs = sbuf("pt_i", [P, DB * NG], I32), sbuf("ptf", [P, DB * NG]), sbuf("offs", [P, DB * NG], U32)
        raw, laid = sbuf("raw", [P, GR, 2, 4 * DI]), sbuf("laid", [P, 2, 4, 2, DI])
        qs, qbd = sbuf("qs", [P, HI, TS]), sbuf("qbd", [P, 4, 2, HI, DT])
        kn, wi = sbuf("kn", [DT, DB, DI]), sbuf("wi", [TS, HI])
        wt, w = sbuf("wt", [TS, DB, HI, DT]), sbuf("w", [P, 4, TS])
        kiT, knT, relu = sbuf("kiT", [P, 2, 512]), sbuf("knT", [P, 4, DT]), sbuf("relu", [P, 2, 512])
        t_ps, s_ps = [psum(f"t{n}", [P, 4, P]) for n in range(2)], [psum(f"s{n}", [P, 512]) for n in range(2)]
        c_ps = [psum(f"c{n}", [TS, 512]) for n in range(2)]
        names = ("par_in", "q_in", "chain", "offs_ready", "laid", "q_ready", "w_turned", "w_ready", "turned", "kiT_ready",
                 "scored", "relu_ready", "summed", "sc_out", "kn_turned")
        s = {n: sem(n) for n in names}
        keys_in = sb["gathered"][RING:]
        sc = sb["ssc"]
        units = [(g, p) for g in range(NG) for p in range(4)]
        block = ctx.enter_context(nc.Block())

        @block.sync
        def _(sp):
            for q in range(4):
                sp.dma_start(pt_i[32 * q:32 * (q + 1), :], dram["pages_q"][q].partition_broadcast(32)
                             ).then_inc(s["par_in"], 16)
            sp.dma_start(sb["c_rows"][:, :], consts["c_rows"]).then_inc(s["par_in"], 16)
            sp.dma_start(sb["c_toks"][:, :], consts["c_toks"]).then_inc(s["par_in"], 16)
            for x in range(2):
                src = dram["projT"][0:HI * DI, TP:TOK].rearrange("(h d) t -> d h t", d=DI)
                sp.dma_start(qs[64 * x:64 * (x + 1), :, :], src).then_inc(s["q_in"], 16)
            sp.dma_start(kn[:, :, :], dram["projN"][TP:TOK, N_KI:N_KI + DI].rearrange("(b s) d -> s b d", s=DT)
                         ).then_inc(s["q_in"], 16)
            sp.dma_start(wi[:, :], dram["projN"][TP:TOK, N_WI:N_WI + HI]).then_inc(s["q_in"], 16)

        @block.gpsimd
        def _(pool):
            pool.wait_ge(s["offs_ready"], 1)
            table = dram["cache_kidx"][0].rearrange("n (r x) d -> (n r) (x d)", x=4)
            for n, (g, p) in enumerate(units):
                if n >= GR:
                    pool.wait_ge(s["laid"], n - GR + 1)
                for x in range(2):
                    c = (2 * p + x) * NG + g
                    pool.indirect_dma_start(raw[:, n % GR, x, :], None, table,
                                            bass.IndirectOffsetOnAxis(ap=offs[:, c:c + 1], axis=0)
                                            ).then_inc(keys_in[n % GR], 16)

        @block.vector
        def _(dve):
            step = Chain(dve, s["chain"])
            dve.wait_ge(s["par_in"], 96)
            step(dve.tensor_copy(ptf[:, :], pt_i[:, :]))
            step(dve.tensor_scalar(ptf[:, :], ptf[:, :], 32.0, sb["c_rows"][:, R_MOD:R_MOD + 1], ALU.mult, ALU.add))
            dve.tensor_copy(offs[:, :], ptf[:, :]).then_inc(s["offs_ready"], 1)
            step(dve.memset(qbd[:, :, :, :, :], 0.0))
            dve.wait_ge(s["q_in"], 64)
            q5 = qs[:, :, :].rearrange("d h (p x t) -> d p x h t", x=2, t=DT)
            for x in range(2):
                half = slice(64 * x, 64 * (x + 1))
                for p in range(4):
                    last = dve.tensor_copy(qbd[half, p, x], q5[half, p, x])
            last.then_inc(s["q_ready"], 1)
            step(dve.tensor_scalar(wi[:, :], wi[:, :], float(HI * DI) ** -0.5, None, ALU.mult))
            eye = sb["ident"][0:TS, 0:TS].rearrange("p (b t) -> p b t", b=DB).unsqueeze(2)
            step(dve.tensor_copy(wt[:, :, :, :], bc(eye, [TS, DB, HI, DT])))
            for b in range(DB):
                last = dve.tensor_tensor(wt[:, b], wt[:, b], bc(wi[:, :].unsqueeze(2), [TS, HI, DT]), ALU.mult)
            last.then_inc(s["q_ready"], 1)
            dve.wait_ge(s["w_turned"], 1)
            dve.tensor_copy(w[:, :, :], t_ps[0][:, :, 0:TS]).then_inc(s["w_ready"], 1)
            dve.wait_ge(s["kn_turned"], 1)
            dve.tensor_copy(knT[:, :, :], t_ps[1][:, :, 0:DT]).then_inc(s["w_ready"], 1)

            def scores_out(g):
                dve.wait_ge(s["summed"], 4 * g + 4)
                dve.tensor_copy(sc[:, 512 * g:512 * (g + 1)], c_ps[g % 2][:, :]).then_inc(s["sc_out"], 1)

            for n, (g, p) in enumerate(units):
                dve.wait_ge(s["turned"], n + 1)
                if n >= 2:
                    dve.wait_ge(s["scored"], n - 1)
                dve.tensor_copy(kiT[:, n % 2, :].rearrange("p (q r) -> p q r", r=4),
                                t_ps[n % 2][:, :, :].rearrange("p r q -> p q r")).then_inc(s["kiT_ready"], 1)
                if g and p == 1:
                    scores_out(g - 1)
            scores_out(NG - 1)
            dve.wait_ge(s["summed"], len(units) + 1)
            dve.tensor_tensor(sc[:, PAST:], c_ps[0][:, 0:DT], sb["c_toks"][:, T_CAUSAL:T_CAUSAL + DT], ALU.add
                              ).then_inc(s["sc_out"], 1)

        @block.scalar
        def _(act):
            def lay(n):
                act.wait_ge(keys_in[n % GR], 32 * (n // GR + 1))
                if n >= 2:
                    act.wait_ge(s["turned"], n - 1)
                act.activation(laid[:, n % 2], raw[:, n % GR].rearrange("p x (r d) -> p r x d", r=4), ACT.Copy
                               ).then_inc(s["laid"], 1)

            lay(0)
            for n in range(len(units)):
                if n + 1 < len(units):
                    lay(n + 1)
                act.wait_ge(s["scored"], n + 1)
                if n >= 2:
                    act.wait_ge(s["summed"], n - 1)
                act.activation(relu[:, n % 2, :], s_ps[n % 2][:, :], ACT.Relu).then_inc(s["relu_ready"], 1)
            act.wait_ge(s["scored"], len(units) + 1)
            act.wait_ge(s["summed"], len(units))
            act.activation(relu[:, 0, 0:16], s_ps[0][:, 0:16], ACT.Relu).then_inc(s["relu_ready"], 1)

        @block.tensor
        def _(pe):
            eye = sb["ident"]
            pe.wait_ge(s["q_ready"], 2)
            for p in range(4):
                last = pe.transpose(t_ps[0][:, p, 0:TS], wt[:, 2 * p:2 * p + 2].rearrange("j x h t -> j (x h t)"),
                                    eye[0:TS, 0:TS])
            last.then_inc(s["w_turned"], 1)
            for p in range(4):
                last = pe.transpose(t_ps[1][:, p, 0:DT], kn[:, 2 * p:2 * p + 2].rearrange("s x d -> s (x d)"),
                                    eye[0:DT, 0:DT])
            last.then_inc(s["kn_turned"], 1)
            pe.wait_ge(s["w_ready"], 2)

            def turn(n):
                pe.wait_ge(s["laid"], n + 1)
                if n >= 2:
                    pe.wait_ge(s["kiT_ready"], n - 1)
                for r in range(4):
                    last = pe.transpose(t_ps[n % 2][:, r, :], laid[:, n % 2, r].rearrange("p x d -> p (x d)"), eye[:, :])
                last.then_inc(s["turned"], 1)

            def score(n, p):
                pe.wait_ge(s["kiT_ready"], n + 1)
                if n >= 2:
                    pe.wait_ge(s["relu_ready"], n - 1)
                pe.matmul(s_ps[n % 2][:, :], qbd[:, p].rearrange("d x h t -> d (x h t)"), kiT[:, n % 2, :],
                          start=True, stop=True).then_inc(s["scored"], 1)

            def add(n, g, p):
                pe.wait_ge(s["relu_ready"], n + 1)
                if g >= 2 and p == 0:
                    pe.wait_ge(s["sc_out"], g - 1)
                pe.matmul(c_ps[g % 2][:, :], w[:, p, :], relu[:, n % 2, :], start=(p == 0), stop=(p == 3)
                          ).then_inc(s["summed"], 1)

            turn(0)
            for n, (g, p) in enumerate(units):
                if n + 1 < len(units):
                    turn(n + 1)
                score(n, p)
                if n:
                    add(n - 1, *units[n - 1])
            add(n, *units[n])
            pe.wait_ge(s["relu_ready"], len(units))
            pe.wait_ge(s["sc_out"], NG - 1)
            for p in range(4):
                last = pe.matmul(s_ps[0][:, DT * p:DT * (p + 1)], qbd[:, p].rearrange("d x h t -> d (x h t)"),
                                 knT[:, p, :], start=True, stop=True)
            last.then_inc(s["scored"], 1)
            pe.wait_ge(s["relu_ready"], len(units) + 1)
            for p in range(4):
                last = pe.matmul(c_ps[0][:, 0:DT], w[:, p, :], relu[:, 0, DT * p:DT * (p + 1)], start=(p == 0),
                                 stop=(p == 3))
            last.then_inc(s["summed"], 1)


def sample_inputs(nc, dram, sb):
    with ExitStack() as ctx:
        sem = lambda n: ctx.enter_context(nc.semaphore(f"si_{n}"))
        sbuf = lambda n, s: ctx.enter_context(nc.sbuf_tensor(f"si_{n}", s, F32))
        gains, sq, ss = sbuf("gains", [TS, 2, DH]), sbuf("sq", [TS, 8, DH]), sbuf("ss", [TS, 8])
        ps = ctx.enter_context(nc.psum_tensor("si_ps", [P, 8, TS], F32))
        s = {n: sem(n) for n in ("in", "sq", "chain", "summed", "root", "normed", "turned", "out", "saved")}
        qkv = sb["s_qkv"]
        block = ctx.enter_context(nc.Block())

        @block.sync
        def _(sp):
            sp.dma_start(qkv[:, :], dram["projN"][TP:TOK, 0:3 * DA]).then_inc(s["in"], 16)
            for x, name in enumerate(("q_norm", "k_norm")):
                sp.dma_start(gains[:, x, :], dram[name][0].partition_broadcast(TS)).then_inc(s["in"], 16)
            sp.dma_start(sb["relh"][:, :], AP(tensor=dram["rel_bias_t"].tensor, offset=dram["rel_bias_t"].offset,
                                              ap=[[0, TS], [32, HA], [1, 32]])).then_inc(s["in"], 16)
            sp.dma_start(sb["pages"][:, :], AP(tensor=dram["page_table"].tensor, offset=dram["page_table"].offset,
                                               ap=[[PAGES, DB], [0, DT], [1, PAGES]])).then_inc(s["in"], 16)
            sp.wait_ge(s["normed"], 1)
            sp.dma_start(dram["q_rows"], qkv[:, 0:DA]).then_inc(s["saved"], 16)
            sp.wait_ge(s["saved"], 16)

        @block.scalar
        def _(act):
            act.wait_ge(s["in"], 80)
            act.activation(sq[:, :, :], qkv[:, 0:2 * DA].rearrange("p (h e) -> p h e", h=8), ACT.Square
                           ).then_inc(s["sq"], 1)
            act.wait_ge(s["summed"], 1)
            act.activation(ss[:, :], ss[:, :], ACT.Sqrt, bias=sb["eps"][0:TS, 0:1], scale=1.0 / DH
                           ).then_inc(s["root"], 1)

        @block.vector
        def _(dve):
            step = Chain(dve, s["chain"])
            dve.wait_ge(s["in"], 80)
            step(dve.tensor_scalar(gains[:, 0, :], gains[:, 0, :], float(DH) ** -0.5, None, ALU.mult))
            dve.wait_ge(s["sq"], 1)
            dve.tensor_reduce(ss[:, :], sq[:, :, :], AX.X, ALU.add).then_inc(s["summed"], 1)
            dve.wait_ge(s["root"], 1)
            step(dve.reciprocal(ss[:, :], ss[:, :]))
            qk3 = qkv[:, 0:2 * DA].rearrange("p (h e) -> p h e", h=8)
            step(dve.tensor_tensor(qk3, qk3, bc(ss[:, :].unsqueeze(2), [TS, 8, DH]), ALU.mult))
            for x in range(2):
                last = dve.tensor_tensor(qk3[:, 4 * x:4 * x + 4, :], qk3[:, 4 * x:4 * x + 4, :],
                                         bc(gains[:, x:x + 1, :], [TS, 4, DH]), ALU.mult)
            last.then_inc(s["normed"], 1)
            dve.wait_ge(s["turned"], 1)
            dve.tensor_copy(sb["s_qT"][:, :].rearrange("p (t h) -> p h t", h=HA), ps[:, 0:4, :])
            dve.tensor_copy(sb["s_kT"][:, :].rearrange("p (h t) -> p h t", h=HA), ps[:, 4:8, :])

        @block.tensor
        def _(pe):
            pe.wait_ge(s["normed"], 1)
            for x in range(8):
                last = pe.transpose(ps[:, x, :], qkv[:, DH * x:DH * (x + 1)], sb["ident"][0:TS, 0:TS])
            last.then_inc(s["turned"], 1)


def attend_sample(nc, dram, sb):
    with ExitStack() as ctx:
        sem = lambda n: ctx.enter_context(nc.semaphore(f"as_{n}"))
        sbuf = lambda n, s, t=F32: ctx.enter_context(nc.sbuf_tensor(f"as_{n}", s, t))
        psum = lambda n, s: ctx.enter_context(nc.psum_tensor(f"as_{n}", s, F32))
        best, idx = sbuf("best", [TS, 2, 8]), sbuf("idx", [TS, TOPS], U32)
        pos, dead, phys, hit = sbuf("pos", [TS, NSEL]), sbuf("dead", [TS, NSEL]), sbuf("phys", [TS, TOPS]), sbuf(
            "hit", [TS, TOPS])
        jump, offs = sbuf("jump", [TS, PAGES]), sbuf("offs", [P, 2, TS], U32)
        drop, bias, near = sbuf("drop", [P, 32]), sbuf("bias", [P, NSEL]), sbuf("near", [P, NSEL])
        dist = sbuf("dist", [P, NSEL])
        rows, qb, prod = sbuf("rows", [P, RING, DA]), sbuf("qb", [P, 4, DA]), sbuf("prod", [P, 2, DA])
        lt, own, p_t = sbuf("lt", [P, 2, NROW]), sbuf("own", [P, NROW]), sbuf("p_t", [P, 2, NROW])
        p, mx, den = sbuf("p", [P, NSEL]), sbuf("mx", [P, 1]), sbuf("den", [P, 1])
        pn, pnT = sbuf("pn", [P, DB, DT]), sbuf("pnT", [TS, NROW])
        win = sbuf("win", [P, 4, 2 * NROW - HA])
        o, oT = sbuf("o", [P, DH]), sbuf("oT", [P, HA, TS])
        off_ps, rep_ps, dead_ps, l_ps, n_ps, pT_ps, o_ps, t_ps = (psum(n, s_) for n, s_ in (
            ("off_ps", [P, 2, TS]), ("rep_ps", [P, NSEL]), ("dead_ps", [P, NSEL]), ("l_ps", [P, 2, NROW]),
            ("n_ps", [P, NROW]), ("pT_ps", [P, 3, NROW]), ("o_ps", [P, DA]), ("t_ps", [P, NROW])))
        names = ("chain", "phys_ready", "pos_ready", "off_turned", "spread", "offs_ready", "q_scored", "own_logits",
                 "multiplied", "reduced", "lt_turned", "mx_ready", "exp_ready", "p_ready", "p_turned", "pT_ready",
                 "win_zeroed", "win_ready", "pv", "o_ready", "o_turned", "oT_ready", "saved")
        s = {n: sem(n) for n in names}
        rows_in, q_in = sb["gathered"][0:RING], [sem(f"q_in{n}") for n in range(4)]
        sc, c_rows, c_toks = sb["ssc"], sb["c_rows"], sb["c_toks"]
        col = lambda at, n=1: c_rows[:, at:at + n]
        units = [(j, x) for j in range(TS) for x in range(2)]
        N = len(units)
        block = ctx.enter_context(nc.Block())

        @block.gpsimd
        def _(pool):
            pool.memset(win[:, :, :], 0.0).then_inc(s["win_zeroed"], 1)
            pool.wait_ge(s["offs_ready"], 1)
            for n in range(2 * N):
                j, x = units[n % N]
                table = dram["cache_k" if n < N else "cache_v"][0].rearrange("n r h d -> (n r) (h d)")
                if RING <= n < N + RING:
                    pool.wait_ge(s["multiplied"], n - RING + 1)
                elif n >= N + RING:
                    pool.wait_ge(s["pv"], n - N - RING + 1)
                pool.indirect_dma_start(rows[:, n % RING, :], None, table,
                                        bass.IndirectOffsetOnAxis(ap=offs[:, x, j:j + 1], axis=0)
                                        ).then_inc(rows_in[n % RING], 16)

        @block.sync
        def _(sp):
            for j in range(TS):
                if j >= 4:
                    sp.wait_ge(s["multiplied"], 2 * (j - 3))
                sp.dma_start(qb[:, j % 4, :], dram["q_rows"][j].partition_broadcast(P)).then_inc(q_in[j % 4], 16)
            sp.wait_ge(s["oT_ready"], 1)
            for h in range(HA):
                sp.dma_start(dram["mixT"][:, TOK * h + TP:TOK * (h + 1)], oT[:, h, :]).then_inc(s["saved"], 16)
            sp.wait_ge(s["saved"], 16 * HA)

        @block.vector
        def _(dve):
            step = Chain(dve, s["chain"])
            step(dve.tensor_copy(jump[:, :], sb["pages"][:, :]))
            step(dve.tensor_copy(hit[:, 0:PAGES], jump[:, :]))
            step(dve.tensor_tensor(jump[:, 1:], hit[:, 1:PAGES], hit[:, 0:PAGES - 1], ALU.subtract))
            step(dve.tensor_scalar(jump[:, 1:], jump[:, 1:], -1.0, None, ALU.add))
            step(dve.tensor_scalar(jump[:, :], jump[:, :], float(PAGE), None, ALU.mult))
            for r in range(TOPS // 8):
                step(dve.max(best[:, r % 2, :], sc[:, :]))
                step(dve.max_index(idx[:, 8 * r:8 * r + 8], best[:, r % 2, :], sc[:, :]))
                step(dve.match_replace(sc[:, :], best[:, r % 2, :], sc[:, :], TAKEN))
            step(dve.tensor_copy(pos[:, 0:TOPS], idx[:, :]))
            step(dve.tensor_copy(pos[:, TOPS:], c_toks[:, T_NEWPOS:T_NEWPOS + DT]))
            step(dve.tensor_scalar(dead[:, 0:TOPS], pos[:, 0:TOPS], float(PAST), NEG, ALU.is_ge, ALU.mult))
            dve.tensor_scalar(dead[:, TOPS:], sc[:, PAST:], TAKEN, NEG, ALU.not_equal, ALU.mult
                              ).then_inc(s["pos_ready"], 1)
            idx_f = near[0:TS, 0:TOPS]
            step(dve.tensor_scalar(idx_f, pos[:, 0:TOPS], float(PAST - 1), None, ALU.min))
            step(dve.tensor_scalar(phys[:, :], idx_f, jump[:, 0:1], None, ALU.add))
            for g in range(1, PAGES):
                step(dve.tensor_scalar(hit[:, :], idx_f, float(PAGE * g), jump[:, g:g + 1], ALU.is_ge, ALU.mult))
                step(dve.tensor_tensor(phys[:, :], phys[:, :], hit[:, :], ALU.add))
            dve.tensor_copy(hit[:, :], phys[:, :]).then_inc(s["phys_ready"], 1)
            dve.wait_ge(s["off_turned"], 1)
            dve.tensor_copy(offs[:, :, :], off_ps[:, :, :]).then_inc(s["offs_ready"], 1)
            dve.wait_ge(s["spread"], 1)
            step(dve.tensor_scalar(dist[:, :], rep_ps[:, :], col(R_QPOS), -1.0, ALU.subtract, ALU.mult))
            step(dve.tensor_scalar(bias[:, :], dead_ps[:, :], sb["relh"][:, 31:32], None, ALU.add))
            step(dve.tensor_tensor(drop[:, 1:], sb["relh"][:, 0:31], sb["relh"][:, 1:32], ALU.subtract))
            for b in range(31, 0, -1):
                step(dve.tensor_scalar(near[:, :], dist[:, :], float(BUCKET_FROM[b]), drop[:, b:b + 1], ALU.is_lt,
                                       ALU.mult))
                step(dve.tensor_tensor(bias[:, :], bias[:, :], near[:, :], ALU.add))
            for n, (j, x) in enumerate(units):
                dve.wait_ge(rows_in[n % RING], 16 * (n // RING + 1))
                dve.wait_ge(q_in[j % 4], 16 * (j // 4 + 1))
                if n >= 2:
                    dve.wait_ge(s["reduced"], n - 1)
                dve.tensor_tensor(prod[:, n % 2, :], rows[:, n % RING, :], qb[:, j % 4, :], ALU.mult
                                  ).then_inc(s["multiplied"], 1)
                dve.wait_ge(s["multiplied"], n + 1)
                dve.tensor_reduce(lt[:, x, HA * j:HA * (j + 1)], prod[:, n % 2, :].rearrange("p (h e) -> p h e", h=HA),
                                  AX.X, ALU.add).then_inc(s["reduced"], 1)
            dve.wait_ge(s["q_scored"], 1)
            step(dve.tensor_tensor(own[:, :], n_ps[:, :], col(R_OWN, NROW), ALU.mult))
            step(dve.tensor_reduce(p[:, TOPS:], own[:, :].rearrange("p (m s) -> p s m", s=DT), AX.X, ALU.add))
            step(dve.tensor_tensor(p[:, TOPS:], p[:, TOPS:], bias[:, TOPS:], ALU.add))
            dve.wait_ge(s["lt_turned"], 1)
            step(dve.tensor_tensor(p[:, 0:TOPS], l_ps[:, :, :].rearrange("p x r -> p (x r)"), bias[:, 0:TOPS], ALU.add))
            dve.tensor_reduce(mx[:, :], p[:, :], AX.X, ALU.max, negate=True).then_inc(s["mx_ready"], 1)
            dve.wait_ge(s["exp_ready"], 1)
            step(dve.reciprocal(den[:, :], den[:, :]))
            step(dve.tensor_scalar(p[:, :], p[:, :], den[:, 0:1], None, ALU.mult))
            dve.tensor_tensor(pn[:, :, :], bc(p[:, TOPS:].unsqueeze(1), [P, DB, DT]),
                              bc(col(R_BATCH, DB).unsqueeze(2), [P, DB, DT]), ALU.mult).then_inc(s["p_ready"], 1)
            dve.wait_ge(s["p_turned"], 1)
            dve.tensor_copy(p_t[:, :, :], pT_ps[:, 0:2, :])
            dve.tensor_copy(pnT[:, :], pT_ps[0:TS, 2, :]).then_inc(s["pT_ready"], 1)
            dve.wait_ge(s["pv"], N)
            step(dve.tensor_scalar(o[:, :], o_ps[:, 0:DH], col(R_HEAD), None, ALU.mult))
            for h in range(1, HA):
                ins = dve.scalar_tensor_tensor(out=o[:, :], in0=o_ps[:, DH * h:DH * (h + 1)], scalar=col(R_HEAD + h),
                                               in1=o[:, :], op0=ALU.mult, op1=ALU.add)
                if h < HA - 1:
                    step(ins)
                else:
                    ins.then_inc(s["o_ready"], 1)
            dve.wait_ge(s["o_turned"], 1)
            dve.tensor_copy(oT[:, :, :], t_ps[:, :].rearrange("p (t h) -> p h t", h=HA)).then_inc(s["oT_ready"], 1)

        @block.scalar
        def _(act):
            act.wait_ge(s["mx_ready"], 1)
            act.activation(p[:, :], p[:, :], ACT.Exp, bias=mx[:, 0:1], accum_out=den[:, 0:1]).then_inc(s["exp_ready"], 1)
            act.wait_ge(s["pT_ready"], 1)
            act.wait_ge(s["win_zeroed"], 1)
            for n, (j, x) in enumerate(units):
                if n >= 4:
                    act.wait_ge(s["pv"], n - 3)
                act.activation(win[:, n % 4, NROW - HA:NROW], p_t[:, x, HA * j:HA * (j + 1)], ACT.Copy
                               ).then_inc(s["win_ready"], 1)

        @block.tensor
        def _(pe):
            eye = sb["ident"]
            pe.matmul(n_ps[:, :], sb["s_qT"][:, :], sb["s_kT"][:, :], start=True, stop=True).then_inc(s["q_scored"], 1)
            pe.wait_ge(s["pos_ready"], 1)
            rep = c_toks[:, T_REP:T_REP + NROW]
            pe.matmul(rep_ps[:, :], rep, pos[:, :], start=True, stop=True)
            pe.matmul(dead_ps[:, :], rep, dead[:, :], start=True, stop=True).then_inc(s["spread"], 1)
            pe.wait_ge(s["phys_ready"], 1)
            for x in range(2):
                last = pe.transpose(off_ps[:, x, :], hit[:, P * x:P * (x + 1)], eye[0:TS, 0:TS])
            last.then_inc(s["off_turned"], 1)
            pe.wait_ge(s["reduced"], N)
            for x in range(2):
                last = pe.transpose(l_ps[:, x, :], lt[:, x, :], eye[:, :])
            last.then_inc(s["lt_turned"], 1)
            pe.wait_ge(s["p_ready"], 1)
            for x in range(2):
                pe.transpose(pT_ps[:, x, :], p[:, P * x:P * (x + 1)], eye[:, :])
            pe.transpose(pT_ps[0:TS, 2, :], pn[:, :, :].rearrange("p b s -> p (b s)"), eye[:, :]
                         ).then_inc(s["p_turned"], 1)
            pe.wait_ge(s["pT_ready"], 1)
            pe.matmul(o_ps[:, :], pnT[:, :], sb["s_qkv"][:, 2 * DA:], start=True, stop=False)
            for n, (j, x) in enumerate(units):
                m = N + n
                pe.wait_ge(s["win_ready"], n + 1)
                pe.wait_ge(rows_in[m % RING], 16 * (m // RING + 1))
                at = NROW - HA - HA * j
                pe.matmul(o_ps[:, :], win[:, n % 4, at:at + NROW], rows[:, m % RING, :], start=False, stop=(n == N - 1)
                          ).then_inc(s["pv"], 1)
            pe.wait_ge(s["o_ready"], 1)
            pe.transpose(t_ps[:, :], o[:, :], eye[:, :]).then_inc(s["o_turned"], 1)


BANKS = 8
GROUP = FF // 4


def output_and_mlp(nc, dram, sb):
    with ExitStack() as ctx:
        sem = lambda n: ctx.enter_context(nc.semaphore(f"om_{n}"))
        sbuf = lambda n, s: ctx.enter_context(nc.sbuf_tensor(f"om_{n}", s, F32))
        x, h, hid, ring = sbuf("x", [P, KT, TOK]), sbuf("h", [P, KT, TOK]), sbuf("hid", [P, KT, TOK]), sbuf(
            "ring", [P, 2, KT, CH])
        rstd = sbuf("rstd", [P, TOK])
        ps = [ctx.enter_context(nc.psum_tensor(f"om_ps{n}", [P, CH], F32)) for n in range(BANKS)]
        w_in = [[sem(f"w_in_{s}_{q}") for q in range(4)] for s in range(2)]
        product = [[sem(f"product{s}_{b}") for b in range(BANKS)] for s in range(2)]
        evac = [sem(f"evac{b}") for b in range(BANKS)]
        relued = [sem(f"relued{b}") for b in range(BANKS)]
        x_in, sq_ready, summed, root, rstd_ready, normed, hid_free = (
            sem(n) for n in ("x_in", "sq_ready", "summed", "root", "rstd_ready", "normed", "hid_free"))
        tm_turned, tm_out = sem("tm_turned"), sem("tm_out")
        mix_in = [sem(f"mix_in{q}") for q in range(4)]
        y_out = [sem(f"y_out{i}") for i in range(5)]
        NOUT = D // CH

        def first(turn, s=0):
            return isinstance(turn, int) and turn == 0 and s == 0

        def hidden(i, s, b):
            return hid[:, bass.ds((2 * i + s) * 4 + b // 2, 1), two_halves(b % 2)].rearrange("p o t -> p (o t)")

        def y_tok(i):
            return ring[:, i % 2, 4 * (i // 2):4 * (i // 2) + 4, :].rearrange("p k n -> p (k n)")

        block = ctx.enter_context(nc.Block())

        @block.sync
        def _(sp):
            def load(s, turn, rows, col):
                if not first(turn):
                    sp.wait_ge(product[s][BANKS - 1], turn)
                for q in range(4):
                    sp.dma_start(ring[:, s, 4 * q:4 * q + 4, :], rows(q)[:, :, bass.ds(col, CH)]).then_inc(w_in[s][q], 16)

            rows_of = lambda w, q: w[512 * q:512 * (q + 1), :].rearrange("(k p) n -> p k n", p=P)
            mix_t = dram["mixT"].rearrange("p (k t) -> p k t", k=KT)
            for q in range(4):
                sp.dma_start(hid[:, 4 * q:4 * q + 4, :], mix_t[:, 4 * q:4 * q + 4, :]).then_inc(mix_in[q], 16)
            for i in range(NOUT // 2):
                for s in range(2):
                    load(s, i, lambda q: rows_of(dram["w_out"][0], q), (2 * i + s) * CH)
            up = dram["w_up"][0].rearrange("(q k p) n -> q p k n", q=4, p=P)
            down = dram["w_down"][0].rearrange("(g q k p) n -> g q p k n", g=4, q=4, p=P)
            with sp.Fori(0, 4) as g:
                with sp.Fori(0, NOUT // 2) as i:
                    for s in range(2):
                        load(s, g * 4 + i + 2, lambda q: up[q], g * GROUP + (2 * i + s) * CH)
                with sp.Fori(0, NOUT // 2) as i:
                    for s in range(2):
                        load(s, g * 4 + i + 4, lambda q: down[bass.ds(g, 1), q].rearrange("g p k n -> (g p) k n"),
                             (2 * i + s) * CH)

        @block.tensor
        def _(pe):
            def chunk(s, turn, src, wait=None):
                for m in range(4):
                    for k in range(KT):
                        if m == 0 and k % 4 == 0:
                            pe.wait_ge(w_in[s][k // 4], 16 * turn + 16)
                        if m == 0 and wait:
                            wait(k)
                        for half in range(2):
                            b = 2 * m + half
                            if k == 0 and not first(turn, s):
                                pe.wait_ge(evac[b], 2 * turn + s)
                            ins = pe.matmul(ps[b][:, 0:HALF], ring[:, s, k, P * m:P * (m + 1)], src[:, k, two_halves(half)],
                                            start=(k == 0), stop=(k == KT - 1))
                            if k == KT - 1:
                                ins.then_inc(product[s][b], 1)

            for q in range(4):
                pe.wait_ge(mix_in[q], 16)
            for i in range(NOUT // 2):
                for s in range(2):
                    chunk(s, i, hid)
            for half in range(2):
                pe.wait_ge(evac[half], NOUT)
            for k in range(KT):
                pe.wait_ge(sq_ready, k + 1)
                for half in range(2):
                    last = pe.matmul(ps[half][:, 0:HALF], sb["ones"][:, :], h[:, k, two_halves(half)], start=(k == 0),
                                     stop=(k == KT - 1))
            last.then_inc(summed, 1)
            pe.wait_ge(root, 2)
            with pe.Fori(0, 4) as g:
                with pe.Fori(0, NOUT // 2) as i:
                    for s in range(2):
                        chunk(s, g * 4 + i + 2, h, lambda k: pe.wait_ge(normed, k + 1))
                with pe.Fori(0, NOUT // 2) as i:
                    for s in range(2):
                        for b in range(BANKS):
                            pe.wait_ge(evac[b], 8 * g + 8)
                        chunk(s, g * 4 + i + 4, hid)
            for n in range(20):
                i, c = n // 4, n % 4
                b = n % BANKS
                pe.wait_ge(evac[b], 36)
                if n >= BANKS:
                    pe.wait_ge(tm_out, n - BANKS + 1)
                if n == 0:
                    for b2 in range(BANKS):
                        pe.wait_ge(evac[b2], 36)
                for j in range(4):
                    k = 4 * c + j
                    last = pe.transpose(ps[b][0:NT[i], P * j:P * (j + 1)], x[:, k, P * i:P * i + NT[i]], sb["ident"][:, :])
                last.then_inc(tm_turned, 1)

        @block.vector
        def _(dve):
            def banks(turn, s):
                for m in range(4):
                    for half in range(2):
                        b = 2 * m + half
                        dve.wait_ge(product[s][b], turn + 1)
                        yield m, two_halves(half), ps[b][:, 0:HALF], evac[b]

            def add_to_x(i, s, turn):
                for m, toks, src, done in banks(turn, s):
                    dst = x[:, bass.ds((2 * i + s) * 4 + m, 1), toks].rearrange("p o t -> p (o t)")
                    dve.tensor_tensor(dst, dst, src, ALU.add).then_inc(done, 1)

            dve.wait_ge(x_in, 16)
            for i in range(NOUT // 2):
                for s in range(2):
                    add_to_x(i, s, i)
            dve.wait_ge(root, 2)
            dve.reciprocal(rstd[:, :], rstd[:, :]).then_inc(rstd_ready, 1)
            dve.wait_ge(rstd_ready, 1)
            for k in range(KT):
                dve.scalar_tensor_tensor(out=h[:, k, :], in0=x[:, k, :], scalar=sb["g_mlp"][:, k:k + 1],
                                         in1=rstd[:, :], op0=ALU.mult, op1=ALU.mult).then_inc(normed, 1)
            with dve.Fori(0, 4) as g:
                with dve.Fori(0, NOUT // 2) as i:
                    for s in range(2):
                        for b in range(BANKS):
                            dve.wait_ge(relued[b], 4 * g + 2 * i + s + 1)
                            dst = hidden(i, s, b)
                            dve.tensor_tensor(dst, dst, dst, ALU.mult).then_inc(evac[b], 1)
                with dve.Fori(0, NOUT // 2) as i:
                    for s in range(2):
                        add_to_x(i, s, g * 4 + i + 4)
            for n in range(20):
                i, c = n // 4, n % 4
                dve.wait_ge(tm_turned, n + 1)
                dve.tensor_copy(y_tok(i)[0:NT[i], 512 * c:512 * (c + 1)], ps[n % BANKS][0:NT[i], :]).then_inc(tm_out, 1)

        @block.scalar
        def _(act):
            act.dma_start(x[:, :, :].rearrange("p k t -> p (k t)"), dram["xT"]).then_inc(x_in, 16)
            for k in range(KT):
                for half in range(2):
                    act.wait_ge(evac[2 * (k % 4) + half], k // 4 + 1)
                act.activation(h[:, k, :], x[:, k, :], ACT.Square).then_inc(sq_ready, 1)
            act.wait_ge(summed, 1)
            for half in range(2):
                act.activation(rstd[:, two_halves(half)], ps[half][:, 0:HALF], ACT.Sqrt, bias=sb["eps"][:, 0:1],
                               scale=1.0 / D).then_inc(root, 1)
            with act.Fori(0, 4) as g:
                with act.Fori(0, NOUT // 2) as i:
                    for s in range(2):
                        for b in range(BANKS):
                            act.wait_ge(evac[b], 8 * g + 4)
                        for b in range(BANKS):
                            act.wait_ge(product[s][b], 4 * g + i + 3)
                            act.activation(hidden(i, s, b), ps[b][:, 0:HALF], ACT.Relu).then_inc(relued[b], 1)
            for i in range(5):
                act.wait_ge(tm_out, 4 * i + 4)
                yp, ys, rows = dram["y_prompt"][0], dram["y_sample"].rearrange("b t d -> (b t) d"), y_tok(i)
                if i == 0:
                    act.dma_start(yp[0:P - META, :], rows[META:, :]).then_inc(y_out[i], 16)
                elif i < 4:
                    act.dma_start(yp[P * i - META:P * (i + 1) - META, :], rows).then_inc(y_out[i], 16)
                else:
                    act.dma_start(yp[SEQ - TAILP:, :], rows[0:TAILP, :]).then_inc(y_out[i], 16)
                    act.dma_start(ys, rows[TAILP:TAIL, :]).then_inc(y_out[i], 16)
            for i in range(5):
                act.wait_ge(y_out[i], 32 if i == 4 else 16)


def build(nc, dram, consts):
    with ExitStack() as ctx:
        sbuf = lambda n, s, t=F32: ctx.enter_context(nc.sbuf_tensor(n, s, t))
        sb = {}
        for name, cols in (("ident", P), ("ones", P), ("eps", 1)):
            sb[name] = sbuf(name, [P, cols])
        sb["g_mix"], sb["g_mlp"] = sbuf("g_mix", [P, KT]), sbuf("g_mlp", [P, KT])
        sb["gathered"] = [ctx.enter_context(nc.semaphore(f"gathered{n}")) for n in range(RING + 4)]
        const_in = sb["const_in"] = ctx.enter_context(nc.semaphore("const_in"))
        sb["n_const"] = 4
        with nc.Block() as block:
            @block.sync
            def _(sp):
                sp.dma_start(sb["ident"][:, :], consts["c_ident"]).then_inc(const_in, 16)
                sp.dma_start(sb["ones"][:, :], consts["c_ones"]).then_inc(const_in, 16)
                sp.dma_start(sb["g_mix"][:, :], dram["norm_mix_t"]).then_inc(const_in, 16)
                sp.dma_start(sb["g_mlp"][:, :], dram["norm_mlp_t"]).then_inc(const_in, 16)

            @block.vector
            def _(dve):
                dve.memset(sb["eps"][:, :], EPS)

        with nc.sbuf_tensor("hT", [P, KT, TOK], F32) as hT:
            sb["hT"] = hT
            with nc.sbuf_tensor("xT", [P, KT, TOK], F32) as xT:
                sb["xT"] = xT
                load_and_norm(nc, dram, sb)
            with nc.sbuf_tensor("w_ring", [P, 2, KT, CH], F32) as ring:
                sb["ring"] = ring
                project_in(nc, dram, sb)
        with ExitStack() as sample:
            own = lambda n, s, t=F32: sample.enter_context(nc.sbuf_tensor(f"sm_{n}", s, t))
            for name, shape in (("ssc", [TS, SKEYS]), ("c_rows", [P, R_OWN + NROW]), ("c_toks", [TS, T_NEWPOS + DT]),
                                ("s_qkv", [TS, 3 * DA]), ("s_qT", [P, NROW]), ("s_kT", [P, NROW]), ("relh", [P, 32])):
                sb[name] = own(name, shape)
            sb["pages"] = own("pages", [TS, PAGES], I32)
            sample_scores(nc, dram, consts, sb)
            sample_inputs(nc, dram, sb)
            attend_sample(nc, dram, sb)
        clear_semaphores(nc, sb)
        with ExitStack() as scans:
            own = lambda n, s: scans.enter_context(nc.sbuf_tensor(n, s, F32))
            sb["tm"] = own("tm", [P, 5, TM_COLS])
            for name, shape in (("g", [P, 5, 18]), ("dt", [P, 5, 12]), ("beta", [P, 5, 6]), ("cum", [P, 5, 36]),
                                ("eq", [P, 5, 18]), ("ecum", [P, 5, 18]), ("wend", [P, 5, 18]), ("el", [P, 13, 18]),
                                ("ssm_d", [P, 12]), ("upto", [P, 2 * P]), ("same", [P, 2 * P]), ("members", [P, 9]),
                                ("y_ssd", [P, 5, DBm]), ("y_gdn", [P, 5, DC])):
                sb[name] = own(name, shape)
            with nc.sbuf_tensor("bcT", [P, 4, TOK], F32) as bcT:
                sb["bcT"] = bcT
                convolve(nc, dram, sb)
                gates(nc, dram, consts, sb)
                ssd_scan(nc, dram, sb)
            with ExitStack() as delta:
                for name, shape in (("kbq", [P, HC, 2, TOK]), ("atT", [P, HC, TOK]), ("ttT", [P, HC, TOK]), ("rn", [P, 5, 12])):
                    sb[name] = delta.enter_context(nc.sbuf_tensor(name, shape, F32))
                gdn_prepare(nc, dram, consts, sb)
                gdn_scan(nc, dram, sb)
            clear_semaphores(nc, sb)
            gate_and_norm(nc, dram, sb)
        with ExitStack() as attention:
            own = lambda n, s: attention.enter_context(nc.sbuf_tensor(n, s, F32))
            for name, shape in (("qT", [P, HA, TOK]), ("kT", [P, HA, TOK]), ("kiT", [P, TOK]), ("qiT", [P, 8, TOK]),
                                ("v_tok", [P, 5, DA]), ("wi", [P, 5, HI]), ("toe", [P, HA, 640]), ("causal", [P, P])):
                sb[name] = own(name, shape)
            attention_inputs(nc, dram, consts, sb)
            attend_prompt(nc, dram, sb)
        clear_semaphores(nc, sb)
        output_and_mlp(nc, dram, sb)


_INS = ["x_prompt", "x_sample", "cache_k", "cache_v", "cache_kidx", "page_table", "state_ssm_conv", "state_ssm",
        "state_gdn_conv", "state_gdn", "meta_tokens", "rel_bias", "norm_mix", "w_in", "q_norm", "k_norm",
        "ssm_conv_w", "ssm_conv_b", "ssm_dt_bias", "ssm_A_log", "ssm_D", "ssm_norm", "gdn_conv_w", "gdn_dt_bias",
        "gdn_A_log", "gdn_norm", "w_out", "norm_mlp", "w_up", "w_down"]
_LAID_OUT = ("norm_mix", "norm_mlp", "ssm_conv_w", "ssm_conv_b", "gdn_conv_w", "state_ssm_conv", "state_gdn_conv")
_OUTS = [
    ("y_prompt", (1, SEQ, D)), ("y_sample", (DB, DT, D)),
    ("k_prompt", (1, 1, TP, HA, DH)), ("v_prompt", (1, 1, TP, HA, DH)), ("kidx_prompt", (1, 1, TP, DI)),
    ("k_sample", (1, DB, DT, HA, DH)), ("v_sample", (1, DB, DT, HA, DH)), ("kidx_sample", (1, DB, DT, DI)),
    ("ssm_conv_prompt", (1, 1, 3, CB)), ("ssm_prompt", (1, 1, HB, PB, NB)),
    ("ssm_conv_sample", (1, DB, 3, CB)), ("ssm_sample", (1, DB, HB, PB, NB)),
    ("gdn_conv_prompt", (1, 1, 3, CC)), ("gdn_prompt", (1, 1, HC, DK, DK)),
    ("gdn_conv_sample", (1, DB, 3, CC)), ("gdn_sample", (1, DB, HC, DK, DK)),
]


def kernel(**inputs):
    import numpy as _np
    import concourse.bacc as _bacc
    from concourse import mybir as _mybir
    from concourse.bass_utils import run_bass_kernel_spmd as _run

    nc = _bacc.Bacc("TRN2", target_bir_lowering=False, num_devices=1)
    arrays, dram, consts = {}, {}, {}

    def given(name, a):
        arrays[name] = a
        return nc.dram_tensor(name, a.shape, _mybir.dt.from_np(a.dtype), kind="ExternalInput").ap()

    for name in _INS:
        if name not in _LAID_OUT:
            dram[name] = given(f"in_{name}", _np.ascontiguousarray(inputs[name]))
    for name in ("norm_mix", "norm_mlp"):
        dram[f"{name}_t"] = given(f"in_{name}_t", _np.ascontiguousarray(inputs[name].reshape(KT, P).T))
    taps = _np.concatenate([inputs["ssm_conv_w"][0], inputs["gdn_conv_w"][0]], axis=1)
    bias = _np.concatenate([inputs["ssm_conv_b"][0], _np.zeros(CC, _np.float32)])
    conv = _np.concatenate([taps, bias[None]], axis=0).reshape(5, NCONV, P).transpose(2, 1, 0)
    dram["conv_par"] = given("in_conv_par", _np.ascontiguousarray(conv))
    state = _np.concatenate([inputs["state_ssm_conv"][0], inputs["state_gdn_conv"][0]], axis=2)
    state = state.reshape(DB, 3, NCONV, P).transpose(3, 2, 0, 1)
    dram["conv_state"] = given("in_conv_state", _np.ascontiguousarray(state))
    pages = inputs["page_table"].reshape(DB, PAGES // 4, 4).transpose(2, 0, 1)
    dram["pages_q"] = given("in_pages_q", _np.ascontiguousarray(pages.reshape(4, DB * PAGES // 4)))
    dram["rel_bias_t"] = given("in_rel_bias_t", _np.ascontiguousarray(inputs["rel_bias"].T))
    for name, a in {**constants(), **sample_constants()}.items():
        consts[name] = given(name, a)
    for name, shape in _OUTS:
        dram[name] = nc.dram_tensor(f"out_{name}", shape, F32, kind="ExternalOutput").ap()
    dram["projT"] = nc.dram_tensor("projT", (R_CONV + NCONV * P, TOK), F32).ap()
    dram["projN"] = nc.dram_tensor("projN", (TOK, NTM), F32).ap()
    dram["skew"] = nc.dram_tensor("skew", (HA, P * 768), F32).ap()
    dram["q_rows"] = nc.dram_tensor("q_rows", (TS, DA), F32).ap()
    dram["xT"] = nc.dram_tensor("xT_scratch", (P, KT * TOK), F32).ap()
    dram["mixT"] = nc.dram_tensor("mixT_scratch", (P, KT * TOK), F32).ap()
    build(nc, dram, consts)
    r = _run(nc, [arrays], core_ids=[0])
    return tuple(r.results[0][f"out_{name}"] for name, _ in _OUTS)
```

```python
from contextlib import ExitStack

import numpy as np

import concourse.bass as bass
from concourse import mybir

F32 = mybir.dt.float32
U32 = mybir.dt.uint32
I32 = mybir.dt.int32
ALU = mybir.AluOpType
ACT = mybir.ActivationFunctionType
AX = mybir.AxisListType
AP = bass.AP

P = 128
D = 2048
KT = D // P
SEQ, META = 512, 16
TP = SEQ + META
DB, DT = 8, 4
TS = DB * DT
TOK = TP + TS
HALF = TOK // 2
NT = [128, 128, 128, 128, TOK - 512]
TAIL = NT[4]
TAILP = TP - 512
HA, DH = 4, 128
DA = HA * DH
HI, DI = 16, 64
HB, PB, NB = 12, 64, 128
DBm = HB * PB
HC, DK = 6, 128
DC = HC * DK
CB = DBm + 4 * NB
CC = 3 * DC
NCONV = (CB + CC) // P
PAST, PAGE, PAGES = 4096, 128, 32
TOPP, TOPS = 128, 256
NIN = 7784
FF = 8192
EPS = 1e-6
NEG = -1e30
TAKEN = -3e38
CH = 512
C_QKV, C_QI, C_KIW, C_XBC, C_DT, C_GQKV, C_ZC = 0, 1536, 2560, 3408, 4688, 4700, 7004
R_QI, R_CONV = 0, 1024
N_Q, N_K, N_V, N_KI, N_WI, N_ZB, N_DT, N_ZC, N_A, N_B = 0, 512, 1024, 1536, 1600, 1616, 2384, 2396, 3164, 3170
NTM = 3176


def chunk_plan():
    return [
        ("N", [(C_KIW, 512)], N_KI),
        ("F", [(C_QI, 512)], 0),
        ("F", [(C_QI + 512, 512)], 512),
        ("N", [(0, 512)], 0),
        ("N", [(512, 512)], 512),
        ("N", [(1024, 512)], 1024),
        ("F", [(C_XBC, 512)], 1024),
        ("F", [(C_XBC + 512, 512)], 1536),
        ("F", [(C_XBC + 1024, 256), (C_GQKV, 256)], 2048),
        ("F", [(C_GQKV + 256, 512)], 2560),
        ("F", [(C_GQKV + 768, 512)], 3072),
        ("F", [(C_GQKV + 1280, 512)], 3584),
        ("F", [(C_GQKV + 1792, 512)], 4096),
        ("N", [(C_KIW + 512, 336), (C_DT, 12)], N_KI + 512),
        ("N", [(C_ZC, 512)], N_ZC),
        ("N", [(C_ZC + 512, 268)], N_ZC + 512),
    ]


def t5_bucket_np(dist):
    d = np.maximum(dist, 0)
    ratio = np.log(np.maximum(d, 1).astype(np.float32) / np.float32(16)) / np.float32(np.log(8.0))
    far = 16 + (ratio * np.float32(16)).astype(np.int32)
    return np.where(d < 16, d, np.minimum(far, 31))


BUCKET_FROM = [int(np.argmax(t5_bucket_np(np.arange(200)) >= b)) for b in range(32)]


def constants():
    r = np.arange(P)
    block = np.where(r < TAILP, 0, 1 + (r - TAILP) // DT)
    full = np.ones((P, P), bool)
    tail = block[:, None] == block[None, :]
    upto = r[:, None] <= r[None, :]

    def levels(same, n):
        out = []
        for lev in range(n):
            b = 1 << lev
            j, i = r[:, None], r[None, :]
            out.append(same & (i // (2 * b) == j // (2 * b)) & ((i // b) % 2 == 1) & ((j // b) % 2 == 0))
        return np.concatenate([x.astype(np.float32) for x in out], axis=1)

    f = np.float32
    m = 639 - np.arange(768)
    onehot = (t5_bucket_np(m)[None, :] == np.arange(32)[:, None]).astype(f)
    members = np.zeros((P, 9), f)
    members[np.arange(TAIL), block[:TAIL]] = 1
    return {
        "c_ident": np.eye(P, dtype=f),
        "c_ones": np.ones((P, P), f),
        "c_upto": np.concatenate([(upto & full).astype(f), (upto & tail).astype(f)], axis=1),
        "c_same": np.concatenate([full.astype(f), tail.astype(f)], axis=1),
        "c_level": levels(full, 7),
        "c_level_tail": levels(tail, 4),
        "c_causal": np.where(r[:, None] >= r[None, :], 0.0, NEG).astype(f),
        "c_onehot": onehot,
        "c_members": members,
    }


def tile_rows(i):
    if i == 0:
        return [(0, META, "meta_tokens", 0), (META, P - META, "x_prompt", 0)]
    if i < 4:
        return [(0, P, "x_prompt", P * i - META)]
    return [(0, TAILP, "x_prompt", SEQ - TAILP), (TAILP, TS, "x_sample", 0)]


def two_halves(h):
    return slice(h * HALF, (h + 1) * HALF)


def load_and_norm(nc, dram, sb):
    with ExitStack() as ctx:
        sem = lambda n: ctx.enter_context(nc.semaphore(n))
        x_tok = ctx.enter_context(nc.sbuf_tensor("x_tok", [P, 5, D], F32))
        pt = [ctx.enter_context(nc.psum_tensor(f"xt_ps{n}", [P, 4, P], F32)) for n in range(4)]
        x_in = [sem(f"x_in{i}") for i in range(5)]
        pe_t, evac = sem("x_transposed"), sem("xT_ready")
        xT = sb["xT"]
        x_saved = sem("xT_saved")
        block = ctx.enter_context(nc.Block())

        @block.sync
        def _(sp):
            for i in range(5):
                for row, n, name, src in tile_rows(i):
                    a = dram[name] if name == "meta_tokens" else dram[name].rearrange("a b d -> (a b) d")
                    sp.dma_start(x_tok[row:row + n, i, :], a[src:src + n, :]).then_inc(x_in[i], 16)

            sp.wait_ge(evac, 20)
            sp.dma_start(dram["xT"], xT[:, :, :].rearrange("p k t -> p (k t)")).then_inc(x_saved, 16)
            sp.wait_ge(x_saved, 16)

        @block.tensor
        def _(pe):
            pe.wait_ge(sb["const_in"], 16 * sb["n_const"])
            for i in range(5):
                pe.wait_ge(x_in[i], 16 * len(tile_rows(i)))
                for g in range(4):
                    n = 4 * i + g
                    if n >= 4:
                        pe.wait_ge(evac, n - 3)
                    for k in range(4):
                        kk = 4 * g + k
                        last = pe.transpose(pt[n % 4][:, k, 0:NT[i]], x_tok[0:NT[i], i, kk * P:(kk + 1) * P],
                                            sb["ident"][0:NT[i], 0:NT[i]])
                    last.then_inc(pe_t, 1)

        @block.vector
        def _(dve):
            for i in range(5):
                for g in range(4):
                    n = 4 * i + g
                    dve.wait_ge(pe_t, n + 1)
                    dve.tensor_copy(xT[:, 4 * g:4 * g + 4, P * i:P * i + NT[i]],
                                    pt[n % 4][:, :, 0:NT[i]]).then_inc(evac, 1)

    norm_feature_major(nc, sb, sb["xT"], sb["g_mix"], sb["hT"], "mix")


def norm_feature_major(nc, sb, xT, gain, out, tag):
    with ExitStack() as ctx:
        sem = lambda n: ctx.enter_context(nc.semaphore(f"{tag}_{n}"))
        sq = ctx.enter_context(nc.sbuf_tensor(f"{tag}_sq", [P, 2, TOK], F32))
        rstd = ctx.enter_context(nc.sbuf_tensor(f"{tag}_rstd", [P, TOK], F32))
        ps = [ctx.enter_context(nc.psum_tensor(f"{tag}_ss{h}", [P, HALF], F32)) for h in range(2)]
        sq_ready, summed, root, rstd_ready = sem("sq_ready"), sem("summed"), sem("root"), sem("rstd_ready")
        block = ctx.enter_context(nc.Block())

        @block.scalar
        def _(act):
            for k in range(KT):
                if k >= 2:
                    act.wait_ge(summed, k - 1)
                act.activation(sq[:, k % 2, :], xT[:, k, :], ACT.Square).then_inc(sq_ready, 1)
            act.wait_ge(summed, KT)
            for h in range(2):
                act.activation(rstd[:, two_halves(h)], ps[h][:, :], ACT.Sqrt, bias=sb["eps"][:, 0:1],
                               scale=1.0 / D).then_inc(root, 1)

        @block.tensor
        def _(pe):
            for k in range(KT):
                pe.wait_ge(sq_ready, k + 1)
                for h in range(2):
                    last = pe.matmul(ps[h][:, :], sb["ones"][:, :], sq[:, k % 2, two_halves(h)],
                                     start=(k == 0), stop=(k == KT - 1))
                last.then_inc(summed, 1)

        @block.vector
        def _(dve):
            dve.wait_ge(root, 2)
            dve.reciprocal(rstd[:, :], rstd[:, :]).then_inc(rstd_ready, 1)
            dve.wait_ge(rstd_ready, 1)
            for k in range(KT):
                dve.scalar_tensor_tensor(out=out[:, k, :], in0=xT[:, k, :], scalar=gain[:, k:k + 1],
                                         in1=rstd[:, :], op0=ALU.mult, op1=ALU.mult)


def project_in(nc, dram, sb, plan, tag, side=None):
    hT, ring = sb["hT"], sb["ring"]
    with ExitStack() as ctx:
        sem = lambda n: ctx.enter_context(nc.semaphore(f"{tag}_{n}"))
        stage = ctx.enter_context(nc.sbuf_tensor(f"{tag}_stage", [P, 4, CH], F32))
        ps = [ctx.enter_context(nc.psum_tensor(f"{tag}_ps{n}", [P, CH], F32)) for n in range(4)]
        w_in = [[sem(f"w_in_{s}_{q}") for q in range(4)] for s in range(2)]
        product, evac = sem("product"), sem("evac")
        stored = [sem(f"stored{n}") for n in range(4)]
        strips = []
        for c, (kind, segs, r0) in enumerate(plan):
            width = sum(w for _, w in segs)
            if kind == "F":
                strips += [[(c, P, HALF, dram["projT"][r0 + P * m:r0 + P * (m + 1), two_halves(h)]) for h in range(2)]
                           for m in range(4)]
            else:
                strips += [[(c, NT[i], width, dram["projN"][P * i:P * i + NT[i], r0:r0 + width])] for i in range(5)]
        banks = [b for strip in strips for b in strip]
        if side:
            side.enter(ctx)
        block = ctx.enter_context(nc.Block())

        @block.sync
        def _(sp):
            def store(b):
                _, rows, cols, dst = banks[b]
                sp.wait_ge(evac, b + 1)
                sp.dma_start(dst, stage[0:rows, b % 4, 0:cols]).then_inc(stored[b % 4], 16)

            for c, (_, segs, _) in enumerate(plan):
                if c >= 2:
                    sp.wait_ge(product, sum(b[0] <= c - 2 for b in banks))
                at = 0
                for col, width in segs:
                    for q in range(4):
                        src = dram["w_in"][0, 512 * q:512 * (q + 1), col:col + width]
                        sp.dma_start(ring[:, c % 2, 4 * q:4 * q + 4, at:at + width],
                                     src.rearrange("(k p) n -> p k n", p=P)).then_inc(w_in[c % 2][q], 16)
                    at += width
                for b in range(len(banks)):
                    if banks[b][0] == c - 1:
                        store(b)
            for b in range(len(banks)):
                if banks[b][0] == len(plan) - 1:
                    store(b)
            for n in range(4):
                sp.wait_ge(stored[n], 16 * ((len(banks) - n + 3) // 4))

        @block.tensor
        def _(pe):
            seen, bank, strip = [0, 0], 0, 0
            for c, (kind, segs, _) in enumerate(plan):
                w, width = ring[:, c % 2], sum(x for _, x in segs)
                seen[c % 2] += 16 * len(segs)
                for m in range(4 if kind == "F" else 5):
                    for b in range(bank, bank + len(strips[strip])):
                        if b >= 4:
                            pe.wait_ge(evac, b - 3)
                    for k in range(KT):
                        if m == 0 and k % 4 == 0:
                            pe.wait_ge(w_in[c % 2][k // 4], seen[c % 2])
                        flags = dict(start=(k == 0), stop=(k == KT - 1))
                        if kind == "F":
                            for h in range(2):
                                last = pe.matmul(ps[(bank + h) % 4][:, 0:HALF], w[:, k, P * m:P * (m + 1)],
                                                 hT[:, k, two_halves(h)], **flags)
                                if k == KT - 1:
                                    last.then_inc(product, 1)
                        else:
                            last = pe.matmul(ps[bank % 4][0:NT[m], 0:width], hT[:, k, P * m:P * m + NT[m]],
                                             w[:, k, 0:width], **flags)
                            if k == KT - 1:
                                last.then_inc(product, 1)
                    bank += len(strips[strip])
                    if side:
                        side.tensor(pe, strip)
                    strip += 1

        @block.scalar
        def _(act):
            b = 0
            for strip in range(len(strips)):
                for _, rows, cols, _ in strips[strip]:
                    act.wait_ge(product, b + 1)
                    if b >= 4:
                        act.wait_ge(stored[b % 4], 16 * (b // 4))
                    act.activation(stage[0:rows, b % 4, 0:cols], ps[b % 4][0:rows, 0:cols], ACT.Copy).then_inc(evac, 1)
                    b += 1
                if side:
                    side.scalar(act, strip)

        if side:
            @block.vector
            def _(dve):
                side.vector(dve)

            @block.gpsimd
            def _(pool):
                side.gpsimd(pool)


class Chain:

    def __init__(self, eng, sem):
        self.eng, self.sem, self.n = eng, sem, 0

    def __call__(self, ins):
        self.n += 1
        ins.then_inc(self.sem, 1)
        self.eng.wait_ge(self.sem, self.n)


F_B, F_C, F_Q = 6, 8, 10
T_X, T_B, T_GQ, T_GK, T_GV = 0, 6 * P, 8 * P, 14 * P, 20 * P
TM_COLS = 26 * P
RAW = 3 + TOK
XW = RAW + DB * 7
YW = XW - 3


def convolve(nc, dram, sb):
    with ExitStack() as ctx:
        sem = lambda n: ctx.enter_context(nc.semaphore(n))
        sbuf = lambda n, s: ctx.enter_context(nc.sbuf_tensor(n, s, F32))
        R = 4
        xp = sbuf("conv_x", [P, R, XW])
        y = sbuf("conv_y", [P, 2, YW])
        par, state = sbuf("conv_par", [P, NCONV, 5]), sbuf("conv_state", [P, NCONV, DB, 3])
        feat = sbuf("conv_feat", [P, R, TOK])
        last3 = sbuf("conv_last3", [P, R, 27])
        last3_t = sbuf("conv_last3_t", [27, NCONV * P])
        big = [ctx.enter_context(nc.psum_tensor(f"conv_big{n}", [P, 4, P], F32)) for n in range(2)]
        small = [ctx.enter_context(nc.psum_tensor(f"conv_small{n}", [P, P], F32)) for n in range(2)]
        l3 = [ctx.enter_context(nc.psum_tensor(f"conv_l3_{n}", [P, 4, P], F32)) for n in range(2)]
        par_in, zeroed = sem("conv_par_in"), sem("conv_zeroed")
        x_in = [sem(f"conv_x_in{n}") for n in range(R)]
        laid, first, conv, act_ready, turned = sem("laid"), sem("first_tap"), sem("conv_done"), sem("silu_ready"), sem("turned")
        big_out, small_out, l3_turned, l3_out, saved, chain = (
            sem("big_out"), sem("small_out"), sem("l3_turned"), sem("l3_out"), sem("conv_saved"), sem("conv_chain"))
        turned_f = [f for f in range(NCONV) if not F_C <= f < F_Q]
        nth = {f: n for n, f in enumerate(turned_f)}
        before = lambda f: sum(g < f for g in turned_f)
        dest = lambda f: sb["bcT"][:, f - F_B, :] if F_B <= f < F_Q else feat[:, f % R, :]
        block = ctx.enter_context(nc.Block())

        @block.sync
        def _(sp):
            sp.dma_start(par[:, :, :], dram["conv_par"]).then_inc(par_in, 16)
            sp.dma_start(state[:, :, :, :], dram["conv_state"]).then_inc(par_in, 16)
            for f in range(NCONV):
                if f >= R:
                    sp.wait_ge(conv, f - R + 1)
                    sp.wait_ge(laid, f - R + 1)
                sp.dma_start(xp[:, f % R, 3:RAW], dram["projT"][R_CONV + P * f:R_CONV + P * (f + 1), :]
                             ).then_inc(x_in[f % R], 16)
            sp.wait_ge(l3_out, NCONV // 4)
            outs = [("ssm_conv_prompt", "ssm_conv_sample", 0, CB), ("gdn_conv_prompt", "gdn_conv_sample", CB, CC)]
            for prompt, sample, at, n in outs:
                sp.dma_start(dram[prompt][0, 0], last3_t[0:3, at:at + n]).then_inc(saved, 16)
                sp.dma_start(dram[sample][0].rearrange("b j f -> (b j) f"), last3_t[3:27, at:at + n]).then_inc(saved, 16)
            sp.wait_ge(saved, 64)

        @block.gpsimd
        def _(pool):
            for n in range(R):
                last = pool.memset(xp[:, n, 0:3], 0.0)
            last.then_inc(zeroed, 1)
            pool.wait_ge(par_in, 32)
            pool.wait_ge(zeroed, 1)
            for f in range(NCONV):
                x, own = xp[:, f % R], xp[:, f % R, RAW:XW].rearrange("p (b c) -> p b c", c=7)
                new = x[:, 3 + TP:RAW].rearrange("p (b c) -> p b c", c=DT)
                pool.wait_ge(x_in[f % R], 16 * (f // R + 1))
                if f >= R:
                    pool.wait_ge(l3_turned, f - R + 1)
                pool.tensor_copy(own[:, :, 0:3], state[:, f, :, :])
                pool.tensor_copy(own[:, :, 3:7], new)
                pool.tensor_copy(last3[:, f % R, 0:3], x[:, TP:TP + 3])
                pool.tensor_copy(last3[:, f % R, 3:27].rearrange("p (b c) -> p b c", c=3), new[:, :, 1:4]
                                 ).then_inc(laid, 1)

        @block.scalar
        def _(act):
            def silu(f):
                if F_B <= f < F_Q:
                    pass
                elif f >= R:
                    act.wait_ge(turned, before(f - R + 1))
                act.wait_ge(conv, f + 1)
                act.activation(dest(f)[:, 0:TP], y[:, f % 2, 0:TP], ACT.Silu)
                own = y[:, f % 2, RAW:RAW + DB * 7 - 3]
                src = AP(tensor=own.tensor, offset=own.offset, ap=[list(own.ap[0]), [7, DB], [1, DT]])
                act.activation(dest(f)[:, TP:TOK].rearrange("p (b t) -> p b t", t=DT), src, ACT.Silu
                               ).then_inc(act_ready, 1)

            def small_copy(f):
                act.wait_ge(turned, nth[f] + 1)
                act.activation(sb["tm"][0:TAIL, 4, nth[f] * P:(nth[f] + 1) * P], small[nth[f] % 2][0:TAIL, :], ACT.Copy
                               ).then_inc(small_out, 1)

            act.wait_ge(par_in, 32)
            for f in range(NCONV + 2):
                if f < NCONV:
                    act.wait_ge(laid, f + 1)
                    if f >= 2:
                        act.wait_ge(act_ready, f - 1)
                    act.activation(y[:, f % 2, :], xp[:, f % R, 0:YW], ACT.Identity, bias=par[:, f, 4:5],
                                   scale=par[:, f, 0:1]).then_inc(first, 1)
                if 1 <= f <= NCONV:
                    silu(f - 1)
                if f >= 2 and f - 2 in nth:
                    small_copy(f - 2)

        @block.vector
        def _(dve):
            step = Chain(dve, chain)

            def big_copy(f):
                n = nth[f]
                dve.wait_ge(turned, n + 1)
                dve.tensor_copy(sb["tm"][:, 0:4, n * P:(n + 1) * P], big[n % 2][:, :, :]).then_inc(big_out, 1)

            def last3_copy(g):
                dve.wait_ge(l3_turned, 4 * g + 4)
                dve.tensor_copy(last3_t[:, 4 * g * P:4 * (g + 1) * P].rearrange("p (a b) -> p a b", a=4),
                                l3[g % 2][0:27, :, :]).then_inc(l3_out, 1)

            dve.wait_ge(par_in, 32)
            for f in range(NCONV + 2):
                if f < NCONV:
                    dve.wait_ge(first, f + 1)
                    for i in range(1, 4):
                        ins = dve.scalar_tensor_tensor(out=y[:, f % 2, :], in0=xp[:, f % R, i:i + YW],
                                                       scalar=par[:, f, i:i + 1], in1=y[:, f % 2, :],
                                                       op0=ALU.mult, op1=ALU.add)
                        if i < 3:
                            step(ins)
                    ins.then_inc(conv, 1)
                if f >= 2 and f - 2 in nth:
                    big_copy(f - 2)
                if f >= 4 and f % 4 == 0:
                    last3_copy(f // 4 - 1)

        @block.tensor
        def _(pe):
            ident = sb["ident"]

            def turn(f):
                n = nth[f]
                if n >= 2:
                    pe.wait_ge(big_out, n - 1)
                    pe.wait_ge(small_out, n - 1)
                pe.wait_ge(act_ready, f + 1)
                for i in range(4):
                    pe.transpose(big[n % 2][:, i, :], dest(f)[:, P * i:P * (i + 1)], ident[:, :])
                pe.transpose(small[n % 2][0:TAIL, :], dest(f)[:, 512:TOK], ident[:, :]).then_inc(turned, 1)

            for f in range(NCONV + 1):
                if f < NCONV:
                    pe.wait_ge(laid, f + 1)
                    if f % 4 == 0 and f >= 8:
                        pe.wait_ge(l3_out, f // 4 - 1)
                    pe.transpose(l3[f // 4 % 2][0:27, f % 4, :], last3[:, f % R, :], ident[:, :]).then_inc(l3_turned, 1)
                if f >= 1 and f - 1 in nth:
                    turn(f - 1)


def bc(ap, shape):
    return ap.broadcast_to(shape)


def gates(nc, dram, consts, sb):
    with ExitStack() as ctx:
        sem = lambda n: ctx.enter_context(nc.semaphore(n))
        sbuf = lambda n, s: ctx.enter_context(nc.sbuf_tensor(n, s, F32))
        raw, bias, alog = sbuf("g_raw", [P, 5, 24]), sbuf("g_bias", [P, 18]), sbuf("g_alog", [P, 18])
        z, u, w, lw, t = (sbuf(f"g_{n}", [P, 5, 18]) for n in "z u w lw t".split())
        rate = sbuf("g_rate", [P, 18])
        by_block = sbuf("g_by_block", [P, 9, 18])
        ps = ctx.enter_context(nc.psum_tensor("g_ps", [P, 5, 36], F32))
        pe_ps = ctx.enter_context(nc.psum_tensor("g_el", [P, 13, 18], F32))
        par_in, cleared, raw_in, chain, exp_u, ln_w, exp_b, rate_ready, g_ready, sums, cums, done = (
            sem(f"g_{n}") for n in ("par_in", "cleared", "raw_in", "chain", "exp_u", "ln_w", "exp_b", "rate_ready",
                                    "g_ready", "sums", "cums", "done"))
        za, wr, act_chain = sem("g_za"), sem("g_wr"), sem("g_act_chain")
        g, dt, beta = sb["g"], sb["dt"], sb["beta"]
        block = ctx.enter_context(nc.Block())

        @block.sync
        def _(sp):
            for dst, name, at, n in ((bias, "ssm_dt_bias", 0, 12), (bias, "gdn_dt_bias", 12, 6),
                                     (alog, "ssm_A_log", 0, 12), (alog, "gdn_A_log", 12, 6),
                                     (sb["ssm_d"], "ssm_D", 0, 12)):
                sp.dma_start(dst[:, at:at + n], dram[name][0].partition_broadcast(P)).then_inc(par_in, 16)
            sp.dma_start(sb["upto"][:, :], consts["c_upto"]).then_inc(par_in, 16)
            sp.dma_start(sb["same"][:, :], consts["c_same"]).then_inc(par_in, 16)
            sp.dma_start(sb["members"][:, :], consts["c_members"]).then_inc(par_in, 16)
            sp.wait_ge(cleared, 1)
            for i in range(5):
                rows = slice(P * i, P * i + NT[i])
                sp.dma_start(raw[0:NT[i], i, 0:12], dram["projN"][rows, N_DT:N_DT + 12]).then_inc(raw_in, 16)
                sp.dma_start(raw[0:NT[i], i, 12:24], dram["projN"][rows, N_A:N_A + 12]).then_inc(raw_in, 16)

        @block.gpsimd
        def _(pool):
            pool.memset(raw[:, :, :], 0.0).then_inc(cleared, 1)

        @block.vector
        def _(dve):
            step = Chain(dve, chain)
            dve.wait_ge(par_in, 128)
            dve.wait_ge(raw_in, 160)
            step(dve.memset(sb["cum"][:, :, :], 0.0))
            step(dve.tensor_tensor(z[:, :, :], raw[:, :, 0:18], bc(bias[:, :].unsqueeze(1), [P, 5, 18]), ALU.add))
            dve.scalar_tensor_tensor(out=w[:, :, :], in0=z[:, :, :], scalar=-1.0, in1=z[:, :, :], op0=ALU.mult,
                                     op1=ALU.max).then_inc(za, 1)
            dve.wait_ge(exp_u, 1)
            dve.tensor_scalar(w[:, :, :], u[:, :, :], 1.0, None, ALU.add).then_inc(wr, 1)
            dve.wait_ge(wr, 1)
            step(dve.tensor_scalar(t[:, :, :], w[:, :, :], -1.0, None, ALU.add))
            step(dve.tensor_scalar(sb["eq"][:, :, :], t[:, :, :], 0.0, None, ALU.is_equal))
            step(dve.tensor_tensor(t[:, :, :], t[:, :, :], sb["eq"][:, :, :], ALU.add))
            step(dve.reciprocal(t[:, :, :], t[:, :, :]))
            dve.wait_ge(ln_w, 1)
            step(dve.tensor_tensor(t[:, :, :], t[:, :, :], lw[:, :, :], ALU.mult))
            step(dve.tensor_tensor(t[:, :, :], t[:, :, :], sb["eq"][:, :, :], ALU.add))
            step(dve.tensor_tensor(t[:, :, :], t[:, :, :], u[:, :, :], ALU.mult))
            step(dve.scalar_tensor_tensor(out=t[:, :, :], in0=z[:, :, :], scalar=0.0, in1=t[:, :, :],
                                          op0=ALU.max, op1=ALU.add))
            step(dve.tensor_copy(dt[:, :, :], t[:, :, 0:12]))
            dve.wait_ge(rate_ready, 1)
            step(dve.scalar_tensor_tensor(out=g[:, :, :], in0=t[:, :, :], scalar=-1.0,
                                          in1=bc(rate[:, :].unsqueeze(1), [P, 5, 18]), op0=ALU.mult, op1=ALU.mult))
            for b in range(9):
                ins = dve.tensor_scalar(by_block[0:TAIL, b, :], g[0:TAIL, 4, :], sb["members"][0:TAIL, b:b + 1], None,
                                        ALU.mult)
            ins.then_inc(g_ready, 1)
            dve.wait_ge(exp_b, 1)
            step(dve.tensor_scalar(beta[:, :, :], beta[:, :, :], 1.0, None, ALU.add))
            step(dve.reciprocal(beta[:, :, :], beta[:, :, :]))
            dve.wait_ge(sums, 1)
            dve.tensor_copy(sb["cum"][:, 0:4, :], ps[:, 0:4, :])
            dve.tensor_copy(sb["cum"][0:TAIL, 4, :], ps[0:TAIL, 4, :]).then_inc(cums, 1)
            dve.wait_ge(cums, 1)
            dve.tensor_tensor(sb["wend"][:, :, :], sb["cum"][:, :, 18:36], sb["cum"][:, :, 0:18], ALU.subtract
                              ).then_inc(done, 1)

        @block.scalar
        def _(act):
            act.wait_ge(par_in, 128)
            act.activation(rate[:, :], alog[:, :], ACT.Exp).then_inc(rate_ready, 1)
            act.wait_ge(za, 1)
            act.activation(u[:, :, :], w[:, :, :], ACT.Exp, scale=-1.0).then_inc(exp_u, 1)
            act.activation(beta[:, :, :], raw[:, :, 18:24], ACT.Exp, scale=-1.0).then_inc(exp_b, 1)
            act.wait_ge(wr, 1)
            act.activation(lw[:, :, :], w[:, :, :], ACT.Ln).then_inc(ln_w, 1)
            act.wait_ge(sums, 1)
            act.activation(sb["el"][:, :, :], pe_ps[:, :, :], ACT.Exp)
            act.wait_ge(cums, 1)
            act.activation(sb["ecum"][:, :, :], sb["cum"][:, :, 0:18], ACT.Exp)
            act.wait_ge(done, 1)
            act.activation(sb["wend"][:, :, :], sb["wend"][:, :, :], ACT.Exp)

        @block.tensor
        def _(pe):
            pe.wait_ge(g_ready, 1)
            for i in range(5):
                m = P * (i == 4)
                n = NT[i]
                pe.matmul(ps[0:n, i, 0:18], sb["upto"][0:n, m:m + n], g[0:n, i, :], start=True, stop=True)
                pe.matmul(ps[0:n, i, 18:36], sb["same"][0:n, m:m + n], g[0:n, i, :], start=True, stop=True)
                if i < 4:
                    pe.matmul(pe_ps[:, i, :], sb["ones"][:, :], g[:, i, :], start=True, stop=True)
            pe.matmul(pe_ps[:, 4:13, :], sb["ones"][0:TAIL, :], by_block[0:TAIL, :, :], start=True, stop=True
                      ).then_inc(sums, 1)


def ssd_scan(nc, dram, sb):
    with ExitStack() as ctx:
        sem = lambda n: ctx.enter_context(nc.semaphore(f"ssd_{n}"))
        sbuf = lambda n, s: ctx.enter_context(nc.sbuf_tensor(f"ssd_{n}", s, F32))
        psum = lambda n, s: ctx.enter_context(nc.psum_tensor(f"ssd_{n}", s, F32))
        tm, bcT, y = sb["tm"], sb["bcT"], sb["y_ssd"]
        dec, gm = sbuf("dec", [P, 12, P]), sbuf("gm", [P, 2, P])
        xdt, xdtw, skip = sbuf("xdt", [P, DBm]), sbuf("xdtw", [P, DBm]), sbuf("skip", [P, DBm])
        sT = sbuf("sT", [P, DBm])
        s_nat, s_smp = sbuf("s_nat", [P, DB, 6, NB]), sbuf("s_smp", [P, DB, DBm])
        yT, b_own, el_nat = sbuf("yT", [P, 6, TAIL]), sbuf("b_own", [TAIL, 2, DB, NB]), sbuf("el_nat", [P, 6, DB])
        s_out = sbuf("s_out", [P, 6, NB])
        rows_ps = [psum(f"rows{n}", [P, 4, P]) for n in range(3)]
        g_ps = psum("g", [P, 2, P])
        y_ps = [psum(f"y{n}", [P, 384]) for n in range(2)]
        s_ps = [psum(f"s{n}", [P, 384]) for n in range(2)]
        (rows_done, g_done, inter_done, dif, dec_ready, w_ready, gm_ready, x_ready, inter_out, intra, intra_out, s_done,
         s_ready, skip_ready, chain, loaded, turned, turned_out, own_ready, yT_done, yT_out, upd, upd_out, sT_turned,
         sT_out, saved, el_ready) = (sem(n) for n in (
             "rows_done", "g_done", "inter_done", "dif", "dec_ready", "w_ready", "gm_ready", "x_ready", "inter_out",
             "intra", "intra_out", "s_done", "s_ready", "skip_ready", "chain", "loaded", "turned", "turned_out",
             "own_ready", "yT_done", "yT_out", "upd", "upd_out", "sT_turned", "sT_out", "saved", "el_ready"))
        h3 = lambda ap, h: ap.rearrange("p (h e) -> p h e", h=h)
        nat = lambda ap: ap.rearrange("(q r) p n -> (r p) q n", r=2)
        block = ctx.enter_context(nc.Block())

        @block.sync
        def _(sp):
            for b in range(DB):
                sp.dma_start(s_nat[:, b], nat(dram["state_ssm"][0, b])).then_inc(loaded, 16)
            sp.wait_ge(upd_out, 12)
            for b in range(DB):
                sp.dma_start(nat(dram["ssm_sample"][0, b]), s_nat[:, b]).then_inc(saved, 16)
            sp.wait_ge(sT_out, 2)
            sp.dma_start(nat(dram["ssm_prompt"][0, 0]), s_out[:, :, :]).then_inc(saved, 16)
            sp.wait_ge(saved, 144)

        @block.gpsimd
        def _(pool):
            for i in range(5):
                n = NT[i]
                if i:
                    pool.wait_ge(s_done, i)
                    pool.wait_ge(intra, i)
                    pool.wait_ge(intra_out, i)
                x = h3(tm[0:n, i, T_X:T_X + DBm], HB)
                pool.tensor_tensor(h3(xdt[0:n, :], HB), x, bc(sb["dt"][0:n, i, :].unsqueeze(2), [n, HB, PB]), ALU.mult
                                   ).then_inc(x_ready, 1)
                pool.tensor_tensor(h3(skip[0:n, :], HB), x, bc(sb["ssm_d"][0:n, :].unsqueeze(2), [n, HB, PB]), ALU.mult
                                   ).then_inc(skip_ready, 1)
                pool.wait_ge(x_ready, 2 * i + 1)
                pool.tensor_tensor(h3(xdtw[0:n, :], HB), h3(xdt[0:n, :], HB),
                                   bc(sb["wend"][0:n, i, 0:12].unsqueeze(2), [n, HB, PB]), ALU.mult).then_inc(x_ready, 1)
            for r in range(2):
                part = slice(PB * r, PB * (r + 1))
                src = sb["el"][part, 5:13, 0:12].rearrange("p b (q r) -> p q b r", r=2)[:, :, :, r]
                pool.tensor_copy(el_nat[part, :, :], src).then_inc(el_ready, 1)

        @block.tensor
        def _(pe):
            ident, g = sb["ident"], sb["g"]
            pe.wait_ge(loaded, 128)
            for q in range(24):
                if q >= 2:
                    pe.wait_ge(turned_out, q - 1)
                for r in range(2):
                    b, pair = divmod(2 * q + r, 6)
                    last = pe.transpose(s_ps[q % 2][:, r * P:(r + 1) * P], s_nat[:, b, pair, :], ident[:, :])
                last.then_inc(turned, 1)
            for i in range(5):
                n, m = NT[i], P * (i == 4)
                if i:
                    pe.wait_ge(dif, i)
                    pe.wait_ge(gm_ready, i)
                    pe.wait_ge(intra_out, i)
                for h in range(HB):
                    last = pe.matmul(rows_ps[h // 4][:, h % 4, 0:n], bc(g[0:n, i, h:h + 1], [n, P]),
                                     sb["upto"][0:n, m:m + n], start=True, stop=True)
                last.then_inc(rows_done, 1)
                for k in range(2):
                    last = pe.matmul(g_ps[0:n, k, 0:n], bcT[:, k, P * i:P * i + n], bcT[:, 2 + k, P * i:P * i + n],
                                     start=True, stop=True)
                last.then_inc(g_done, 1)
                pe.wait_ge(s_ready, i + 1)
                if i < 4:
                    for k in range(2):
                        last = pe.matmul(y_ps[k][0:n, :], bcT[:, 2 + k, P * i:P * i + n], sT[:, 384 * k:384 * (k + 1)],
                                         start=True, stop=True)
                    last.then_inc(inter_done, 1)
                else:
                    pe.wait_ge(dif, 5)
                    pe.wait_ge(turned_out, 24)
                    for q in range(6):
                        out = rows_ps[0][:, :, :].rearrange("p a b -> p (a b)")[:, TAIL * q:TAIL * (q + 1)]
                        pe.matmul(out[:, 0:TAILP], sT[:, P * q:P * (q + 1)], bcT[:, 2 + q // 3, 512:TP],
                                  start=True, stop=True)
                        for b in range(DB):
                            last = pe.matmul(out[:, TAILP + DT * b:TAILP + DT * (b + 1)], s_smp[:, b, P * q:P * (q + 1)],
                                             bcT[:, 2 + q // 3, TP + DT * b:TP + DT * (b + 1)], start=True, stop=True)
                    last.then_inc(yT_done, 1)
                    pe.wait_ge(yT_out, 1)
                    for q in range(6):
                        last = pe.transpose(y_ps[q // 3][0:n, P * (q % 3):P * (q % 3 + 1)], yT[:, q, :], ident[:, :])
                    last.then_inc(inter_done, 1)
                pe.wait_ge(inter_out, i + 1)
                pe.wait_ge(w_ready, i + 1)
                pe.wait_ge(x_ready, 2 * i + 2)
                for h in range(HB):
                    last = pe.matmul(y_ps[h // 6][0:n, PB * (h % 6):PB * (h % 6 + 1)], dec[0:n, h, 0:n],
                                     xdt[0:n, PB * h:PB * (h + 1)], start=True, stop=True)
                last.then_inc(intra, 1)
                rows = n if i < 4 else TAILP
                for k in range(2):
                    last = pe.matmul(s_ps[k][:, :], tm[0:rows, i, T_B + P * k:T_B + P * (k + 1)],
                                     xdtw[0:rows, 384 * k:384 * (k + 1)], start=True, stop=True)
                last.then_inc(s_done, 1)
            pe.wait_ge(own_ready, 1)
            for u in range(12):
                q, half = divmod(u, 2)
                if u >= 2:
                    pe.wait_ge(upd_out, u - 1)
                pe.matmul(rows_ps[1 + u % 2][:, :, :], xdtw[0:TAIL, P * q:P * (q + 1)],
                          b_own[:, q // 3, 4 * half:4 * half + 4, :], start=True, stop=True).then_inc(upd, 1)
            pe.wait_ge(s_ready, 6)
            for q in range(6):
                last = pe.transpose(s_ps[q // 3][:, P * (q % 3):P * (q % 3 + 1)], sT[:, P * q:P * (q + 1)], ident[:, :])
            last.then_inc(sT_turned, 1)

        @block.scalar
        def _(act):
            for q in range(24):
                act.wait_ge(turned, q + 1)
                b, pair = divmod(2 * q, 6)
                act.activation(s_smp[:, b, P * pair:P * (pair + 2)], s_ps[q % 2][:, 0:2 * P], ACT.Copy
                               ).then_inc(turned_out, 1)
            for i in range(5):
                n = NT[i]
                act.wait_ge(dif, i + 1)
                act.activation(dec[0:n, :, 0:n], dec[0:n, :, 0:n], ACT.Exp).then_inc(dec_ready, 1)
                if i == 4:
                    act.wait_ge(yT_done, 1)
                    act.activation(yT[:, :, :], rows_ps[0][:, :, :].rearrange("p a b -> p (a b)")[:, 0:6 * TAIL]
                                   .rearrange("p (q t) -> p q t", q=6), ACT.Copy).then_inc(yT_out, 1)
            for k in range(2):
                act.wait_ge(sT_turned, 1)
                act.activation(s_out[:, 3 * k:3 * k + 3, :], s_ps[k][:, :].rearrange("p (q n) -> p q n", q=3), ACT.Copy
                               ).then_inc(sT_out, 1)

        @block.vector
        def _(dve):
            step = Chain(dve, chain)
            dve.memset(sT[:, :], 0.0).then_inc(s_ready, 1)
            for i in range(5):
                n, m = NT[i], P * (i == 4)
                dve.wait_ge(rows_done, i + 1)
                if i:
                    dve.wait_ge(intra, i)
                for h in range(HB):
                    last = dve.tensor_scalar(dec[0:n, h, 0:n], rows_ps[h // 4][0:n, h % 4, 0:n],
                                             sb["cum"][0:n, i, h:h + 1], 0.0, ALU.subtract, ALU.min)
                last.then_inc(dif, 1)
                dve.wait_ge(g_done, i + 1)
                dve.tensor_tensor(gm[0:n, :, 0:n], g_ps[0:n, :, 0:n],
                                  bc(sb["upto"][0:n, m:m + n].unsqueeze(1), [n, 2, n]), ALU.mult).then_inc(gm_ready, 1)
                dve.wait_ge(inter_done, i + 1)
                dve.wait_ge(skip_ready, i + 1)
                for k in range(2):
                    last = dve.tensor_tensor(h3(y[0:n, i, 384 * k:384 * (k + 1)], 6), h3(y_ps[k][0:n, :], 6),
                                             bc(sb["ecum"][0:n, i, 6 * k:6 * k + 6].unsqueeze(2), [n, 6, PB]), ALU.mult)
                last.then_inc(inter_out, 1)
                dve.wait_ge(gm_ready, i + 1)
                dve.wait_ge(dec_ready, i + 1)
                for k in range(2):
                    last = dve.tensor_tensor(dec[0:n, 6 * k:6 * k + 6, 0:n], dec[0:n, 6 * k:6 * k + 6, 0:n],
                                             bc(gm[0:n, k, 0:n].unsqueeze(1), [n, 6, n]), ALU.mult)
                last.then_inc(w_ready, 1)
                dve.wait_ge(inter_out, i + 1)
                step(dve.tensor_tensor(y[0:n, i, :], y[0:n, i, :], skip[0:n, :], ALU.add))
                dve.wait_ge(inter_done, i + 1)
                step(dve.tensor_tensor(h3(sT[:, :], HB), h3(sT[:, :], HB),
                                       bc(sb["el"][:, i, 0:12].unsqueeze(2), [P, HB, PB]), ALU.mult))
                dve.wait_ge(intra, i + 1)
                for k in range(2):
                    last = dve.tensor_tensor(y[0:n, i, 384 * k:384 * (k + 1)], y[0:n, i, 384 * k:384 * (k + 1)],
                                             y_ps[k][0:n, :], ALU.add)
                last.then_inc(intra_out, 1)
                dve.wait_ge(s_done, i + 1)
                for k in range(2):
                    last = dve.tensor_tensor(sT[:, 384 * k:384 * (k + 1)], sT[:, 384 * k:384 * (k + 1)], s_ps[k][:, :],
                                             ALU.add)
                last.then_inc(s_ready, 1)
            for k in range(2):
                for b in range(DB):
                    last = dve.tensor_scalar(b_own[:, k, b, :], tm[0:TAIL, 4, T_B + P * k:T_B + P * (k + 1)],
                                             sb["members"][0:TAIL, b + 1:b + 2], None, ALU.mult)
            last.then_inc(own_ready, 1)
            dve.wait_ge(el_ready, 2)
            for u in range(12):
                q, half = divmod(u, 2)
                s = s_nat[:, 4 * half:4 * half + 4, q, :]
                step(dve.tensor_tensor(s, s, bc(el_nat[:, q, 4 * half:4 * half + 4].unsqueeze(2), [P, 4, NB]), ALU.mult))
                dve.wait_ge(upd, u + 1)
                dve.tensor_tensor(s, s, rows_ps[1 + u % 2][:, :, :], ALU.add).then_inc(upd_out, 1)


def gdn_prepare(nc, dram, consts, sb):
    with ExitStack() as ctx:
        sem = lambda n: ctx.enter_context(nc.semaphore(f"gp_{n}"))
        sbuf = lambda n, s: ctx.enter_context(nc.sbuf_tensor(f"gp_{n}", s, F32))
        psum = lambda n, s: ctx.enter_context(nc.psum_tensor(f"gp_{n}", s, F32))
        tm, kbq, atT, ttT = sb["tm"], sb["kbq"], sb["atT"], sb["ttT"]
        level = [sbuf("level", [P, 7 * P]), sbuf("level_tail", [P, 4 * P])]
        sq, kb = sbuf("sq", [P, 12, P]), sbuf("kb", [P, DC])
        kT, lT, mT, t, p1, dec, decU = (sbuf(n, [P, HC, P]) for n in ("kT", "lT", "mT", "t", "p1", "dec", "decU"))
        a_ps = [psum(f"a{n}", [P, 4, P]) for n in range(2)]
        b_ps = [psum(f"b{n}", [P, 4, P]) for n in range(2)]
        c_ps = [psum(f"c{n}", [P, 4, P]) for n in range(3)]
        names = ("level_in", "sq_ready", "summed", "root", "chain", "scaled", "kb_ready", "turned", "k_out", "kbq_out",
                 "rows_done", "dif", "dec_ready", "decU_ready", "products", "lt_ready", "m_ready")
        s = {n: sem(n) for n in names}
        sets = ((0, slice(0, 3)), (1, slice(3, 6)))
        p1_done, p1_out, q_done, t_ready = ([sem(f"{n}{x}") for x, _ in sets] for n in ("p1_done", "p1_out", "q_done",
                                                                                       "t_ready"))
        rn = sb["rn"]
        parts = ((0, slice(0, 4)), (1, slice(4, 6)))
        nlev = lambda i: 7 if i < 4 else 4
        lev0 = lambda i: 7 * i
        block = ctx.enter_context(nc.Block())

        @block.sync
        def _(sp):
            sp.dma_start(level[0][:, :], consts["c_level"]).then_inc(s["level_in"], 16)
            sp.dma_start(level[1][:, :], consts["c_level_tail"]).then_inc(s["level_in"], 16)

        @block.scalar
        def _(act):
            for i in range(5):
                n = NT[i]
                if i:
                    act.wait_ge(s["summed"], i)
                act.activation(sq[0:n, :, :], tm[0:n, i, T_GQ:T_GV].rearrange("p (h e) -> p h e", h=12), ACT.Square
                               ).then_inc(s["sq_ready"], 1)
            act.wait_ge(s["summed"], 5)
            act.activation(rn[:, :, :], rn[:, :, :], ACT.Sqrt, bias=sb["eps"][:, 0:1]).then_inc(s["root"], 1)
            for i in range(5):
                n = NT[i]
                for h in range(HC):
                    act.wait_ge(s["turned"], 6 * i + h + 1)
                    if h == 0 and i:
                        act.wait_ge(s["products"], i)
                    act.activation(kT[:, h, 0:n], a_ps[h % 2][:, 0, 0:n], ACT.Copy).then_inc(s["k_out"], 1)
                act.wait_ge(s["dif"], i + 1)
                act.activation(dec[0:n, :, 0:n], dec[0:n, :, 0:n], ACT.Exp).then_inc(s["dec_ready"], 1)
                for lev in range(1, nlev(i)):
                    k = lev0(i) + lev
                    for x, hs in sets:
                        act.wait_ge(p1_done[x], k + 1)
                        act.activation(p1[0:n, hs, 0:n], a_ps[x][0:n, 0:3, 0:n], ACT.Copy).then_inc(p1_out[x], 1)

        @block.gpsimd
        def _(pool):
            pool.wait_ge(s["level_in"], 32)
            for i in range(5):
                n, m = NT[i], P * (i == 4)
                pool.wait_ge(s["dec_ready"], i + 1)
                pool.tensor_tensor(decU[0:n, :, 0:n], dec[0:n, :, 0:n],
                                   bc(sb["upto"][0:n, m:m + n].unsqueeze(1), [n, HC, n]), ALU.mult
                                   ).then_inc(s["decU_ready"], 1)
                pool.wait_ge(s["lt_ready"], i + 1)
                for lev in range(nlev(i)):
                    k = lev0(i) + lev
                    for x, _ in sets:
                        if k:
                            pool.wait_ge(p1_done[x], k)
                        if lev == 1:
                            pool.wait_ge(t_ready[x], k)
                    mask = level[i == 4][0:n, P * lev:P * lev + n]
                    pool.tensor_tensor(mT[0:n, :, 0:n], lT[0:n, :, 0:n], bc(mask.unsqueeze(1), [n, HC, n]), ALU.mult
                                       ).then_inc(s["m_ready"], 1)

        @block.tensor
        def _(pe):
            ident = sb["ident"]
            for i in range(5):
                n, m = NT[i], P * (i == 4)
                tok = slice(P * i, P * i + n)
                pe.wait_ge(s["scaled"], i + 1)
                pe.wait_ge(s["kb_ready"], i + 1)
                for h in range(HC):
                    if h >= 2:
                        pe.wait_ge(s["k_out"], 6 * i + h - 1)
                        pe.wait_ge(s["kbq_out"], 6 * i + h - 1)
                    for x, src in enumerate((tm[0:n, i, T_GK + P * h:T_GK + P * (h + 1)], kb[0:n, P * h:P * (h + 1)],
                                             tm[0:n, i, T_GQ + P * h:T_GQ + P * (h + 1)])):
                        last = pe.transpose(a_ps[h % 2][:, x, 0:n], src, ident[0:n, 0:n])
                    last.then_inc(s["turned"], 1)
                for h in range(HC):
                    last = pe.matmul(b_ps[h // 4][:, h % 4, 0:n], bc(sb["g"][0:n, i, 12 + h:13 + h], [n, P]),
                                     sb["upto"][0:n, m:m + n], start=True, stop=True)
                last.then_inc(s["rows_done"], 1)
                pe.wait_ge(s["k_out"], 6 * i + 6)
                pe.wait_ge(s["kbq_out"], 6 * i + 6)
                for h in range(HC):
                    out = c_ps[h // 2][0:n, 2 * (h % 2):2 * (h % 2) + 2, 0:n]
                    last = pe.matmul(out, kT[:, h, 0:n], kbq[:, h, :, tok], start=True, stop=True)
                last.then_inc(s["products"], 1)
                for lev in range(nlev(i)):
                    k = lev0(i) + lev
                    pe.wait_ge(s["m_ready"], k + 1)
                    for x, hs in sets:
                        if lev:
                            pe.wait_ge(t_ready[x], k)
                        for h in range(hs.start, hs.stop):
                            rhs = t[0:n, h, 0:n] if lev else ident[0:n, 0:n]
                            last = pe.matmul(a_ps[x][0:n, h % 3, 0:n], mT[0:n, h, 0:n], rhs, start=True, stop=True)
                        last.then_inc(p1_done[x], 1)
                    for x, hs in sets if lev else ():
                        pe.wait_ge(p1_out[x], p1_count(i, lev))
                        if lev < nlev(i) - 1:
                            for h in range(hs.start, hs.stop):
                                pe.matmul(b_ps[x][0:n, h % 3, 0:n], ttT[0:n, h, tok], p1[0:n, h, 0:n],
                                          start=True, stop=True)
                        for h in range(hs.start, hs.stop):
                            last = pe.matmul(c_ps[x][0:n, h % 3, 0:n], p1[0:n, h, 0:n], ttT[0:n, h, tok],
                                             start=True, stop=True)
                        last.then_inc(q_done[x], 1)
                for x, _ in sets:
                    pe.wait_ge(t_ready[x], lev0(i) + nlev(i))

        @block.vector
        def _(dve):
            step = Chain(dve, s["chain"])
            step(dve.memset(rn[:, :, :], 1.0))
            for i in range(5):
                n = NT[i]
                dve.wait_ge(s["sq_ready"], i + 1)
                dve.tensor_reduce(rn[0:n, i, :], sq[0:n, :, :], AX.X, ALU.add).then_inc(s["summed"], 1)
            dve.wait_ge(s["root"], 1)
            step(dve.reciprocal(rn[:, :, :], rn[:, :, :]))
            step(dve.tensor_scalar(rn[:, :, 0:6], rn[:, :, 0:6], float(DK) ** -0.5, None, ALU.mult))
            for i in range(5):
                n, m = NT[i], P * (i == 4)
                tok = slice(P * i, P * i + n)
                qk = tm[0:n, i, T_GQ:T_GV].rearrange("p (h e) -> p h e", h=12)
                beta = bc(sb["beta"][0:n, i, :].unsqueeze(2), [n, HC, P])
                dve.tensor_tensor(qk, qk, bc(rn[0:n, i, :].unsqueeze(2), [n, 12, P]), ALU.mult).then_inc(s["scaled"], 1)
                dve.wait_ge(s["scaled"], i + 1)
                if i:
                    dve.wait_ge(s["turned"], 6 * i)
                dve.tensor_tensor(kb[0:n, :].rearrange("p (h e) -> p h e", h=HC), qk[:, 6:12, :], beta, ALU.mult
                                  ).then_inc(s["kb_ready"], 1)
                v = tm[0:n, i, T_GV:T_GV + DC].rearrange("p (h e) -> p h e", h=HC)
                dve.tensor_tensor(v, v, beta, ALU.mult)
                for h in range(HC):
                    dve.wait_ge(s["turned"], 6 * i + h + 1)
                    dve.wait_ge(s["k_out"], 6 * i + h + 1)
                    dve.tensor_copy(kbq[:, h, :, tok], a_ps[h % 2][:, 1:3, 0:n]).then_inc(s["kbq_out"], 1)
                dve.wait_ge(s["rows_done"], i + 1)
                if i:
                    dve.wait_ge(s["decU_ready"], i)
                for h in range(HC):
                    last = dve.tensor_scalar(dec[0:n, h, 0:n], b_ps[h // 4][0:n, h % 4, 0:n],
                                             sb["cum"][0:n, i, 12 + h:13 + h], 0.0, ALU.subtract, ALU.min)
                last.then_inc(s["dif"], 1)
                dve.wait_ge(s["products"], i + 1)
                dve.wait_ge(s["dec_ready"], i + 1)
                if i:
                    dve.wait_ge(s["m_ready"], lev0(i))
                for c in range(3):
                    both = c_ps[c][0:n, :, 0:n].rearrange("p (h x) t -> p x h t", x=2)
                    last = dve.tensor_tensor(lT[0:n, 2 * c:2 * c + 2, 0:n], both[:, 0], dec[0:n, 2 * c:2 * c + 2, 0:n],
                                             ALU.mult)
                last.then_inc(s["lt_ready"], 1)
                dve.wait_ge(s["decU_ready"], i + 1)
                for c in range(3):
                    both = c_ps[c][0:n, :, 0:n].rearrange("p (h x) t -> p x h t", x=2)
                    last = dve.tensor_tensor(atT[0:n, 2 * c:2 * c + 2, tok], both[:, 1], decU[0:n, 2 * c:2 * c + 2, 0:n],
                                             ALU.mult)
                step(last)
                for lev in range(nlev(i)):
                    k = lev0(i) + lev
                    if lev == 0:
                        dve.wait_ge(s["m_ready"], k + 1)
                        eye = sb["ident"][0:n, 0:n].unsqueeze(1)
                        step(dve.tensor_tensor(ttT[0:n, :, tok], bc(eye, [n, HC, n]), mT[0:n, :, 0:n], ALU.subtract))
                        for x, hs in sets:
                            dve.wait_ge(p1_done[x], k + 1)
                            dve.tensor_tensor(t[0:n, hs, 0:n], bc(eye, [n, 3, n]), a_ps[x][0:n, 0:3, 0:n], ALU.subtract
                                              ).then_inc(t_ready[x], 1)
                        continue
                    for x, hs in sets:
                        dve.wait_ge(t_ready[x], k)
                        dve.wait_ge(q_done[x], p1_count(i, lev))
                        last = dve.tensor_tensor(ttT[0:n, hs, tok], ttT[0:n, hs, tok], c_ps[x][0:n, 0:3, 0:n],
                                                 ALU.subtract)
                        if lev < nlev(i) - 1:
                            last = dve.tensor_tensor(t[0:n, hs, 0:n], t[0:n, hs, 0:n], b_ps[x][0:n, 0:3, 0:n],
                                                     ALU.subtract)
                        last.then_inc(t_ready[x], 1)


def p1_count(i, lev):
    return 6 * i + lev


def gdn_scan(nc, dram, sb):
    with ExitStack() as ctx:
        sem = lambda n: ctx.enter_context(nc.semaphore(f"gs_{n}"))
        sbuf = lambda n, s: ctx.enter_context(nc.sbuf_tensor(f"gs_{n}", s, F32))
        psum = lambda n: [ctx.enter_context(nc.psum_tensor(f"gs_{n}{x}", [P, 512], F32)) for x in range(2)]
        tm, kbq, atT, ttT, y = sb["tm"], sb["kbq"], sb["atT"], sb["ttT"], sb["y_gdn"]
        st, st_smp = sbuf("st", [P, HC, P]), sbuf("st_smp", [P, DB, HC, P])
        r, u, wk = sbuf("r", [P, HC, P]), sbuf("u", [P, HC, P]), sbuf("wk", [P, HC, P])
        inT, u_own = sbuf("inT", [P, HC, 2, TAIL]), sbuf("u_own", [TAIL, 2, DB, P])
        a_ps, b_ps, c_ps, d_ps = psum("a"), psum("b"), psum("c"), psum("d")
        names = ("loaded", "st_ready", "wk_ready", "inter", "r_ready", "q_out", "u_done", "u_out", "o_done", "o_out",
                 "upd", "upd_out", "inT_done", "inT_out", "own_ready", "saved", "chain", "s_done")
        s = {n: sem(n) for n in names}
        parts = ((0, slice(0, 4)), (1, slice(4, 6)))
        heads = lambda ps, n, w: ps[0:n, 0:w * P].rearrange("p (h e) -> p h e", h=w)
        block = ctx.enter_context(nc.Block())

        @block.sync
        def _(sp):
            for b in range(DB):
                sp.dma_start(st_smp[:, b], dram["state_gdn"][0, b].rearrange("h k v -> k h v")).then_inc(s["loaded"], 16)
            sp.wait_ge(s["st_ready"], 6)
            sp.dma_start(dram["gdn_prompt"][0, 0].rearrange("h k v -> k h v"), st[:, :, :]).then_inc(s["saved"], 16)
            sp.wait_ge(s["upd_out"], 12)
            for b in range(DB):
                sp.dma_start(dram["gdn_sample"][0, b].rearrange("h k v -> k h v"), st_smp[:, b]).then_inc(s["saved"], 16)
            sp.wait_ge(s["saved"], 144)

        @block.gpsimd
        def _(pool):
            for i in range(5):
                n = NT[i]
                if i:
                    pool.wait_ge(s["s_done"], i)
                k = tm[0:n, i, T_GK:T_GK + DC].rearrange("p (h e) -> p h e", h=HC)
                pool.tensor_tensor(wk[0:n, :, :], k, bc(sb["wend"][0:n, i, 12:18].unsqueeze(2), [n, HC, P]), ALU.mult
                                   ).then_inc(s["wk_ready"], 1)
            pool.wait_ge(s["u_out"], 5)
            for h in range(HC):
                if h >= 2:
                    pool.wait_ge(s["upd"], 2 * (h - 1))
                pool.tensor_tensor(u_own[:, h % 2], bc(u[0:TAIL, h, :].unsqueeze(1), [TAIL, DB, P]),
                                   bc(sb["members"][0:TAIL, 1:9].unsqueeze(2), [TAIL, DB, P]), ALU.mult
                                   ).then_inc(s["own_ready"], 1)

        @block.tensor
        def _(pe):
            for i in range(5):
                n = NT[i]
                tok = slice(P * i, P * i + n)
                pe.wait_ge(s["st_ready"], i + 1)
                if i:
                    pe.wait_ge(s["o_out"], i)
                if i < 4:
                    for x, ps in ((0, a_ps), (1, b_ps)):
                        for h in range(HC):
                            last = pe.matmul(ps[h // 4][0:n, P * (h % 4):P * (h % 4 + 1)], kbq[:, h, x, tok], st[:, h, :],
                                             start=True, stop=True)
                else:
                    pe.wait_ge(s["loaded"], 128)
                    for h in range(HC):
                        out = d_ps[h // 3][:, 96 * (h % 3):96 * (h % 3 + 1)].rearrange("p (x t) -> p x t", x=2)
                        pe.matmul(out[:, :, 0:TAILP], st[:, h, :], kbq[:, h, :, 512:TP], start=True, stop=True)
                        for b in range(DB):
                            c = TAILP + DT * b
                            last = pe.matmul(out[:, :, c:c + DT], st_smp[:, b, h, :], kbq[:, h, :, 512 + c:512 + c + DT],
                                             start=True, stop=True)
                    last.then_inc(s["inT_done"], 1)
                    pe.wait_ge(s["inT_out"], 1)
                    for x, ps in ((0, a_ps), (1, b_ps)):
                        for h in range(HC):
                            last = pe.transpose(ps[h // 4][0:n, P * (h % 4):P * (h % 4 + 1)], inT[:, h, x, :],
                                                sb["ident"][:, :])
                last.then_inc(s["inter"], 1)
                pe.wait_ge(s["r_ready"], i + 1)
                for h in range(HC):
                    last = pe.matmul(c_ps[h // 4][0:n, P * (h % 4):P * (h % 4 + 1)], ttT[0:n, h, tok], r[0:n, h, :],
                                     start=True, stop=True)
                last.then_inc(s["u_done"], 1)
                pe.wait_ge(s["u_out"], i + 1)
                pe.wait_ge(s["wk_ready"], i + 1)
                rows = n if i < 4 else TAILP
                for h in range(HC):
                    last = pe.matmul(a_ps[h // 4][:, P * (h % 4):P * (h % 4 + 1)], wk[0:rows, h, :], u[0:rows, h, :],
                                     start=True, stop=True)
                last.then_inc(s["s_done"], 1)
                for h in range(HC):
                    last = pe.matmul(d_ps[h // 4][0:n, P * (h % 4):P * (h % 4 + 1)], atT[0:n, h, tok], u[0:n, h, :],
                                     start=True, stop=True)
                last.then_inc(s["o_done"], 1)
            for x in range(12):
                h, half = divmod(x, 2)
                pe.wait_ge(s["own_ready"], h + 1)
                if x >= 2:
                    pe.wait_ge(s["upd_out"], x - 1)
                pe.matmul(c_ps[x % 2][:, :], wk[0:TAIL, h, :], u_own[:, h % 2, 4 * half:4 * half + 4, :],
                          start=True, stop=True).then_inc(s["upd"], 1)

        @block.scalar
        def _(act):
            for i in range(5):
                n = NT[i]
                if i == 4:
                    act.wait_ge(s["inT_done"], 1)
                    for x in range(2):
                        last = act.activation(inT[:, 3 * x:3 * x + 3].rearrange("p h x t -> p (h x t)"),
                                              d_ps[x][:, 0:288], ACT.Copy)
                    last.then_inc(s["inT_out"], 1)
                act.wait_ge(s["u_done"], i + 1)
                if i:
                    act.wait_ge(s["o_done"], i)
                for bank, hs in parts:
                    last = act.activation(u[0:n, hs, :], heads(c_ps[bank], n, hs.stop - hs.start), ACT.Copy)
                last.then_inc(s["u_out"], 1)

        @block.vector
        def _(dve):
            step = Chain(dve, s["chain"])
            dve.memset(st[:, :, :], 0.0).then_inc(s["st_ready"], 1)
            for i in range(5):
                n = NT[i]
                ecum = sb["ecum"][0:n, i, 12:18]
                yi = y[0:n, i, :].rearrange("p (h e) -> p h e", h=HC)
                dve.wait_ge(s["inter"], i + 1)
                for bank, hs in parts:
                    w = hs.stop - hs.start
                    last = dve.tensor_tensor(r[0:n, hs, :], heads(a_ps[bank], n, w), bc(ecum[:, hs].unsqueeze(2), [n, w, P]),
                                             ALU.mult)
                step(last)
                dve.tensor_tensor(r[0:n, :, :], tm[0:n, i, T_GV:T_GV + DC].rearrange("p (h e) -> p h e", h=HC),
                                  r[0:n, :, :], ALU.subtract).then_inc(s["r_ready"], 1)
                for bank, hs in parts:
                    w = hs.stop - hs.start
                    last = dve.tensor_tensor(yi[:, hs, :], heads(b_ps[bank], n, w), bc(ecum[:, hs].unsqueeze(2), [n, w, P]),
                                             ALU.mult)
                step(last)
                step(dve.tensor_tensor(st[:, :, :], st[:, :, :], bc(sb["el"][:, i, 12:18].unsqueeze(2), [P, HC, P]),
                                       ALU.mult))
                dve.wait_ge(s["s_done"], i + 1)
                for bank, hs in parts:
                    last = dve.tensor_tensor(st[:, hs, :], st[:, hs, :], heads(a_ps[bank], P, hs.stop - hs.start), ALU.add)
                last.then_inc(s["st_ready"], 1)
                dve.wait_ge(s["o_done"], i + 1)
                for bank, hs in parts:
                    last = dve.tensor_tensor(yi[:, hs, :], yi[:, hs, :], heads(d_ps[bank], n, hs.stop - hs.start), ALU.add)
                last.then_inc(s["o_out"], 1)
            for x in range(12):
                h, half = divmod(x, 2)
                now = st_smp[:, 4 * half:4 * half + 4, h, :]
                decay = sb["el"][:, 5 + 4 * half:9 + 4 * half, 12 + h:13 + h]
                step(dve.tensor_tensor(now, now, bc(decay, [P, 4, P]), ALU.mult))
                dve.wait_ge(s["upd"], x + 1)
                dve.tensor_tensor(now, now, c_ps[x % 2][:, :].rearrange("p (b e) -> p b e", b=4), ALU.add
                                  ).then_inc(s["upd_out"], 1)


def gate_and_norm(nc, dram, sb):
    with ExitStack() as ctx:
        sem = lambda n: ctx.enter_context(nc.semaphore(f"gn_{n}"))
        sbuf = lambda n, s: ctx.enter_context(nc.sbuf_tensor(f"gn_{n}", s, F32))
        z, norm_b, norm_c = sbuf("z", [P, 5, 2 * DBm]), sbuf("norm_b", [P, DBm]), sbuf("norm_c", [P, DK])
        sq, ss, mix = sbuf("sq", [P, DC]), sbuf("ss", [P, 5, 8]), sbuf("mix", [P, 12, TOK])
        ps = [ctx.enter_context(nc.psum_tensor(f"gn_ps{n}", [P, 4, P], F32)) for n in range(4)]
        names = ("par_in", "silu", "gated", "norm_c_done", "cleared", "sq_b", "sq_c", "ss_c", "root", "inv", "normed", "turned",
                 "out", "saved", "chain")
        s = {n: sem(n) for n in names}
        z_in = [sem(f"z_in{i}") for i in range(5)]
        yb, yc = sb["y_ssd"], sb["y_gdn"]
        block = ctx.enter_context(nc.Block())

        @block.sync
        def _(sp):
            sp.dma_start(norm_b[:, :], dram["ssm_norm"][0].partition_broadcast(P)).then_inc(s["par_in"], 16)
            sp.dma_start(norm_c[:, :], dram["gdn_norm"][0].partition_broadcast(P)).then_inc(s["par_in"], 16)
            for i in range(5):
                rows = slice(P * i, P * i + NT[i])
                sp.dma_start(z[0:NT[i], i, 0:DBm], dram["projN"][rows, N_ZB:N_ZB + DBm]).then_inc(z_in[i], 16)
                sp.dma_start(z[0:NT[i], i, DBm:], dram["projN"][rows, N_ZC:N_ZC + DC]).then_inc(z_in[i], 16)
            sp.wait_ge(s["out"], 15)
            sp.dma_start(dram["mixT"][:, 4 * TOK:], mix[:, :, :].rearrange("p k t -> p (k t)")).then_inc(s["saved"], 16)
            sp.wait_ge(s["saved"], 16)

        @block.scalar
        def _(act):
            for i in range(5):
                n = NT[i]
                act.wait_ge(z_in[i], 32)
                act.activation(z[0:n, i, :], z[0:n, i, :], ACT.Silu).then_inc(s["silu"], 1)
            act.wait_ge(s["cleared"], 1)
            for i in range(5):
                n = NT[i]
                act.wait_ge(s["gated"], i + 1)
                for k in range(2):
                    if i or k:
                        act.wait_ge(s["sq_b"], 2 * i + k)
                    if i and k == 0:
                        act.wait_ge(s["ss_c"], i)
                    act.activation(sq[0:n, 0:384], yb[0:n, i, 384 * k:384 * (k + 1)], ACT.Square,
                                   accum_out=ss[0:n, i, k:k + 1]).then_inc(s["sq_b"], 1)
                act.wait_ge(s["sq_b"], 2 * i + 2)
                act.activation(sq[0:n, :], yc[0:n, i, :], ACT.Square).then_inc(s["sq_c"], 1)
            act.wait_ge(s["sq_b"], 10)
            act.wait_ge(s["ss_c"], 5)
            act.activation(ss[:, :, 0:2], ss[:, :, 0:2], ACT.Sqrt, bias=sb["eps"][:, 0:1], scale=1.0 / 384
                           ).then_inc(s["root"], 1)
            act.activation(ss[:, :, 2:8], ss[:, :, 2:8], ACT.Sqrt, bias=sb["eps"][:, 0:1], scale=1.0 / DK
                           ).then_inc(s["root"], 1)

        @block.gpsimd
        def _(pool):
            pool.wait_ge(s["par_in"], 32)
            for i in range(5):
                n = NT[i]
                pool.wait_ge(s["silu"], i + 1)
                zc = z[0:n, i, DBm:].rearrange("p (h e) -> p h e", h=HC)
                pool.tensor_tensor(zc, zc, bc(norm_c[0:n, :].unsqueeze(1), [n, HC, DK]), ALU.mult
                                   ).then_inc(s["norm_c_done"], 1)

        @block.vector
        def _(dve):
            step = Chain(dve, s["chain"])
            dve.wait_ge(s["par_in"], 32)
            dve.memset(ss[:, :, :], 1.0).then_inc(s["cleared"], 1)
            for i in range(5):
                n = NT[i]
                dve.wait_ge(s["silu"], i + 1)
                dve.tensor_tensor(yb[0:n, i, :], yb[0:n, i, :], z[0:n, i, 0:DBm], ALU.mult).then_inc(s["gated"], 1)
            dve.wait_ge(s["cleared"], 1)
            for i in range(5):
                n = NT[i]
                dve.wait_ge(s["sq_c"], i + 1)
                dve.tensor_reduce(ss[0:n, i, 2:8], sq[0:n, :].rearrange("p (h e) -> p h e", h=HC), AX.X, ALU.add
                                  ).then_inc(s["ss_c"], 1)
            dve.wait_ge(s["root"], 2)
            step(dve.reciprocal(ss[:, :, :], ss[:, :, :]))
            dve.wait_ge(s["norm_c_done"], 5)
            for i in range(6):
                if i < 5:
                    n = NT[i]
                    for k in range(2):
                        part = slice(384 * k, 384 * (k + 1))
                        dve.scalar_tensor_tensor(out=yb[0:n, i, part], in0=yb[0:n, i, part], scalar=ss[0:n, i, k:k + 1],
                                                 in1=norm_b[0:n, part], op0=ALU.mult, op1=ALU.mult)
                    y3 = yc[0:n, i, :].rearrange("p (h e) -> p h e", h=HC)
                    step(dve.tensor_tensor(y3, y3, bc(ss[0:n, i, 2:8].unsqueeze(2), [n, HC, DK]), ALU.mult))
                    dve.tensor_tensor(yc[0:n, i, :], yc[0:n, i, :], z[0:n, i, DBm:], ALU.mult).then_inc(s["normed"], 1)
                if i:
                    for g in range(3):
                        c = 3 * (i - 1) + g
                        m = NT[i - 1]
                        dve.wait_ge(s["turned"], c + 1)
                        dve.tensor_copy(mix[:, 4 * g:4 * g + 4, P * (i - 1):P * (i - 1) + m], ps[c % 4][:, :, 0:m]
                                        ).then_inc(s["out"], 1)

        @block.tensor
        def _(pe):
            for i in range(5):
                n = NT[i]
                pe.wait_ge(s["normed"], i + 1)
                for g in range(3):
                    c = 3 * i + g
                    if c >= 4:
                        pe.wait_ge(s["out"], c - 3)
                    for x in range(4):
                        f = 4 * g + x
                        src = (yb if f < 6 else yc)[0:n, i, P * (f % 6):P * (f % 6 + 1)]
                        last = pe.transpose(ps[c % 4][:, x, 0:n], src, sb["ident"][0:n, 0:n])
                    last.then_inc(s["turned"], 1)


def attention_inputs(nc, dram, consts, sb):
    with ExitStack() as ctx:
        sem = lambda n: ctx.enter_context(nc.semaphore(f"ai_{n}"))
        sbuf = lambda n, s: ctx.enter_context(nc.sbuf_tensor(f"ai_{n}", s, F32))
        psum = lambda n: ctx.enter_context(nc.psum_tensor(f"ai_{n}", [P, 4, P], F32))
        qk, qn, kn = sbuf("qk", [P, 5, 2 * DA]), sbuf("qn", [P, DH]), sbuf("kn", [P, DH])
        sq, ss = sbuf("sq", [P, 8, DH]), sbuf("ss", [P, 5, 8])
        ki2 = sbuf("ki2", [P, 5, 2, DI])
        rb, onehot, rows = sbuf("rb", [32, HA]), sbuf("onehot", [32, 768]), sbuf("rows", [P, HA, 768])
        ps = [psum(f"ps{n}") for n in range(4)]
        row_ps = [ctx.enter_context(nc.psum_tensor(f"ai_row{n}", [P, 384], F32)) for n in range(2)]
        names = ("par_in", "sq_ready", "summed", "root", "chain", "normed", "turned", "out", "saved", "row", "row_out",
                 "skewed", "bias_in", "copied", "w_scaled", "cleared", "ki_in")
        s = {n: sem(n) for n in names}
        qk_in = [sem(f"qk_in{i}") for i in range(5)]
        v_tok, wi = sb["v_tok"], sb["wi"]
        block = ctx.enter_context(nc.Block())

        @block.sync
        def _(sp):
            sp.dma_start(qn[:, :], dram["q_norm"][0].partition_broadcast(P)).then_inc(s["par_in"], 16)
            sp.dma_start(kn[:, :], dram["k_norm"][0].partition_broadcast(P)).then_inc(s["par_in"], 16)
            sp.dma_start(rb[:, :], dram["rel_bias"]).then_inc(s["par_in"], 16)
            sp.dma_start(onehot[:, :], consts["c_onehot"]).then_inc(s["par_in"], 16)
            sp.dma_start(sb["causal"][:, :], consts["c_causal"]).then_inc(s["par_in"], 16)
            for i in range(5):
                rows_ = slice(P * i, P * i + NT[i])
                sp.dma_start(qk[0:NT[i], i, :], dram["projN"][rows_, 0:2 * DA]).then_inc(qk_in[i], 16)
            for i in range(5):
                rows_ = slice(P * i, P * i + NT[i])
                for x in range(2):
                    sp.dma_start(ki2[0:NT[i], i, x, :], dram["projN"][rows_, N_KI:N_KI + DI]).then_inc(s["ki_in"], 16)
                sp.dma_start(wi[0:NT[i], i, :], dram["projN"][rows_, N_WI:N_WI + HI]).then_inc(s["ki_in"], 16)
                sp.dma_start(v_tok[0:NT[i], i, :], dram["projN"][rows_, N_V:N_V + DA]).then_inc(s["ki_in"], 16)
            sp.dma_start(sb["qiT"][:, :, :], dram["projT"][0:HI * DI, :].rearrange("(k p) t -> p k t", p=P)
                         ).then_inc(s["ki_in"], 16)
            new = dram["projN"]
            for dst, rows_, c, n in (("v_prompt", slice(0, TP), N_V, DA), ("v_sample", slice(TP, TOK), N_V, DA),
                                     ("kidx_prompt", slice(0, TP), N_KI, DI), ("kidx_sample", slice(TP, TOK), N_KI, DI)):
                out = dram[dst]
                out = out.rearrange("a b t h d -> (a b t) (h d)") if len(out.shape) == 5 else out.rearrange(
                    "a b t d -> (a b t) d")
                sp.dma_start(out, new[rows_, c:c + n]).then_inc(s["copied"], 16)
            for h in range(HA):
                sp.wait_ge(s["row_out"], 2 * h + 2)
                sp.dma_start(dram["skew"][h].rearrange("(p m) -> p m", p=P), rows[:, h, :]).then_inc(s["skewed"], 16)
            sp.wait_ge(s["skewed"], 64)
            skew = dram["skew"]
            for h in range(HA):
                src = AP(tensor=skew.tensor, offset=skew[h].offset + 127, ap=[[767, P], [1, 640]])
                sp.dma_start(sb["toe"][:, h, :], src).then_inc(s["bias_in"], 16)
            kp = dram["k_prompt"].rearrange("a b t h d -> (a b t) (h d)")
            ks = dram["k_sample"].rearrange("a b t h d -> (a b t) (h d)")
            for i in range(5):
                sp.wait_ge(s["normed"], i + 1)
                n = NT[i] if i < 4 else TAILP
                sp.dma_start(kp[P * i:P * i + n, :], qk[0:n, i, DA:]).then_inc(s["saved"], 16)
            sp.dma_start(ks, qk[TAILP:TAIL, 4, DA:]).then_inc(s["saved"], 16)
            sp.wait_ge(s["saved"], 96)
            sp.wait_ge(s["copied"], 64)
            sp.wait_ge(s["bias_in"], 64)
            sp.wait_ge(s["ki_in"], 16 * 21)

        @block.scalar
        def _(act):
            for i in range(5):
                n = NT[i]
                act.wait_ge(qk_in[i], 16)
                if i:
                    act.wait_ge(s["summed"], i)
                act.activation(sq[0:n, :, :], qk[0:n, i, :].rearrange("p (h e) -> p h e", h=8), ACT.Square
                               ).then_inc(s["sq_ready"], 1)
            act.wait_ge(s["summed"], 5)
            act.activation(ss[:, :, :], ss[:, :, :], ACT.Sqrt, bias=sb["eps"][:, 0:1], scale=1.0 / DH
                           ).then_inc(s["root"], 1)

        @block.vector
        def _(dve):
            step = Chain(dve, s["chain"])
            step(dve.memset(ss[:, :, :], 1.0))
            dve.wait_ge(s["par_in"], 80)
            step(dve.tensor_scalar(qn[:, :], qn[:, :], float(DH) ** -0.5, None, ALU.mult))
            for i in range(5):
                n = NT[i]
                dve.wait_ge(s["sq_ready"], i + 1)
                dve.tensor_reduce(ss[0:n, i, :], sq[0:n, :, :], AX.X, ALU.add).then_inc(s["summed"], 1)
            for x in range(8):
                dve.wait_ge(s["row"], x + 1)
                dve.tensor_copy(rows[:, x // 2, 384 * (x % 2):384 * (x % 2 + 1)], row_ps[x % 2][:, :]
                                ).then_inc(s["row_out"], 1)
            dve.wait_ge(s["root"], 1)
            step(dve.reciprocal(ss[:, :, :], ss[:, :, :]))
            for i in range(5):
                n = NT[i]
                qk3 = qk[0:n, i, :].rearrange("p (h e) -> p h e", h=8)
                step(dve.tensor_tensor(qk3, qk3, bc(ss[0:n, i, :].unsqueeze(2), [n, 8, DH]), ALU.mult))
                dve.tensor_tensor(qk3[:, 0:4, :], qk3[:, 0:4, :], bc(qn[0:n, :].unsqueeze(1), [n, 4, DH]), ALU.mult)
                dve.tensor_tensor(qk3[:, 4:8, :], qk3[:, 4:8, :], bc(kn[0:n, :].unsqueeze(1), [n, 4, DH]), ALU.mult
                                  ).then_inc(s["normed"], 1)
            dve.wait_ge(s["ki_in"], 16 * 21)
            for i in range(5):
                last = dve.tensor_scalar(wi[0:NT[i], i, :], wi[0:NT[i], i, :], float(HI * DI) ** -0.5, None, ALU.mult)
            last.then_inc(s["w_scaled"], 1)
            for i in range(5):
                n, tok = NT[i], slice(P * i, P * i + NT[i])
                for x, dst in enumerate((sb["qT"][:, :, tok], sb["kT"][:, :, tok], sb["kiT"][:, tok])):
                    c = 3 * i + x
                    dve.wait_ge(s["turned"], c + 1)
                    src = ps[c % 4][:, :, 0:n] if x < 2 else ps[c % 4][:, 0, 0:n]
                    dve.tensor_copy(dst, src).then_inc(s["out"], 1)

        @block.tensor
        def _(pe):
            pe.wait_ge(s["par_in"], 80)
            for x in range(8):
                if x >= 2:
                    pe.wait_ge(s["row_out"], x - 1)
                pe.matmul(row_ps[x % 2][:, :], bc(rb[:, x // 2:x // 2 + 1], [32, P]),
                          onehot[:, 384 * (x % 2):384 * (x % 2 + 1)], start=True, stop=True).then_inc(s["row"], 1)
            pe.wait_ge(s["ki_in"], 16 * 21)
            for i in range(5):
                n = NT[i]
                eye = sb["ident"][0:n, 0:n]
                pe.wait_ge(s["normed"], i + 1)
                for x in range(3):
                    c = 3 * i + x
                    if c >= 4:
                        pe.wait_ge(s["out"], c - 3)
                    if x < 2:
                        for h in range(HA):
                            last = pe.transpose(ps[c % 4][:, h, 0:n], qk[0:n, i, DA * x + DH * h:DA * x + DH * (h + 1)],
                                                eye)
                    else:
                        last = pe.transpose(ps[c % 4][:, 0, 0:n], ki2[0:n, i].rearrange("p x d -> p (x d)"), eye)
                    last.then_inc(s["turned"], 1)


def attend_prompt(nc, dram, sb):
    with ExitStack() as ctx:
        sem = lambda n: ctx.enter_context(nc.semaphore(f"ap_{n}"))
        sbuf = lambda n, s: ctx.enter_context(nc.sbuf_tensor(f"ap_{n}", s, F32))
        qT, kT, kiT, qiT, toe = (sb[n] for n in ("qT", "kT", "kiT", "qiT", "toe"))
        relu, sc = sbuf("relu", [P, 2, TP]), sbuf("sc", [P, 2, TP])
        best, bm, lg = sbuf("best", [P, 2, 8]), sbuf("bm", [P, 2, TP]), sbuf("lg", [P, 2, TP])
        mx, den = sbuf("mx", [P, 2]), sbuf("den", [P, 2])
        pT = sbuf("pT", [P, 2, 512])
        outT = sbuf("outT", [P, HA, TP])
        s_ps = [ctx.enter_context(nc.psum_tensor(f"ap_s{n}", [P, 1024], F32)) for n in range(2)]
        t_ps = [ctx.enter_context(nc.psum_tensor(f"ap_t{n}", [P, 512], F32)) for n in range(2)]
        o_ps = [ctx.enter_context(nc.psum_tensor(f"ap_o{n}", [P, 4, P], F32)) for n in range(2)]
        names = ("score", "relu_out", "acc", "chain", "mask_ready", "bm_ready", "qk", "lg_ready", "exp_ready", "p_ready",
                 "turned", "pT_out", "pv", "o_out", "saved", "lg_out")
        s = {n: sem(n) for n in names}
        rows = [P, P, P, P, TAILP]
        keys = [P * (i + 1) for i in range(4)] + [TP]
        order = [("h", 0, h) for h in range(HA)]
        for i in range(1, 5):
            order += [("i", i, h) for h in range(HI)] + [("h", i, h) for h in range(HA)]
        nth = {o: n for n, o in enumerate(order)}
        relus = lambda i, h: HI * (i - 1) + h
        blocks = lambda i: [(P * b, min(P, keys[i] - P * b)) for b in range(i + 1)]
        block = ctx.enter_context(nc.Block())

        def freed(eng, n):
            kind, i, h = order[n - 2]
            if kind == "i":
                eng.wait_ge(s["relu_out"], relus(i, h) + 1)
            else:
                eng.wait_ge(s["lg_out"], HA * i + h + 1)

        @block.tensor
        def _(pe):
            def head_out(i, h):
                c, n = HA * i + h, rows[i]
                pe.wait_ge(s["p_ready"], c + 1)
                if c >= 2:
                    pe.wait_ge(s["pT_out"], c - 1)
                for b, (k0, kn) in enumerate(blocks(i)):
                    last = pe.transpose(t_ps[c % 2][0:kn, n * b:n * (b + 1)], lg[0:n, c % 2, k0:k0 + kn],
                                        sb["ident"][0:n, 0:n])
                last.then_inc(s["turned"], 1)
                pe.wait_ge(s["pT_out"], c + 1)
                if h == 0 and i >= 2:
                    pe.wait_ge(s["o_out"], i - 1)
                for b, (k0, kn) in enumerate(blocks(i)):
                    last = pe.matmul(o_ps[i % 2][:, h, 0:n], sb["v_tok"][0:kn, b, DH * h:DH * (h + 1)],
                                     pT[0:kn, c % 2, n * b:n * (b + 1)], start=(b == 0), stop=(b == i))
                last.then_inc(s["pv"], 1)

            done = None
            for x, (kind, i, h) in enumerate(order):
                n = rows[i]
                q = slice(P * i, P * i + n)
                if x >= 2:
                    freed(pe, x)
                for k0, kn in ((0, min(512, keys[i])), (512, keys[i] - 512)):
                    if kn <= 0:
                        continue
                    if kind == "i":
                        half = slice(DI * (h % 2), DI * (h % 2 + 1))
                        last = pe.matmul(s_ps[x % 2][0:n, k0:k0 + kn], qiT[half, h // 2, q], kiT[half, k0:k0 + kn],
                                         start=True, stop=True)
                    else:
                        last = pe.matmul(s_ps[x % 2][0:n, k0:k0 + kn], qT[:, h, q], kT[:, h, k0:k0 + kn],
                                         start=True, stop=True)
                last.then_inc(s["score"], 1)
                if done:
                    head_out(*done)
                done = (i, h) if kind == "h" else None
            head_out(*done)

        @block.scalar
        def _(act):
            for i in range(5):
                n, L = rows[i], keys[i]
                if i:
                    for h in range(HI):
                        x = nth["i", i, h]
                        act.wait_ge(s["score"], x + 1)
                        if relus(i, h) >= 2:
                            act.wait_ge(s["acc"], relus(i, h) - 1)
                        act.activation(relu[0:n, h % 2, 0:L], s_ps[x % 2][0:n, 0:L], ACT.Relu).then_inc(s["relu_out"], 1)
                for h in range(HA):
                    c = HA * i + h
                    act.wait_ge(s["lg_ready"], c + 1)
                    act.activation(lg[0:n, c % 2, 0:L], lg[0:n, c % 2, 0:L], ACT.Exp, bias=mx[0:n, c % 2:c % 2 + 1],
                                   accum_out=den[0:n, c % 2:c % 2 + 1]).then_inc(s["exp_ready"], 1)
                    act.wait_ge(s["turned"], c + 1)
                    if c >= 2:
                        act.wait_ge(s["pv"], c - 1)
                    for b, (k0, kn) in enumerate(blocks(i)):
                        if kn == P and b:
                            continue
                        w = n * (i + 1) if kn == P and i < 4 else n * i if kn == P else n
                        at = 0 if kn == P else n * b
                        last = act.activation(pT[0:kn, c % 2, at:at + w], t_ps[c % 2][0:kn, at:at + w], ACT.Copy)
                    last.then_inc(s["pT_out"], 1)

        @block.gpsimd
        def _(pool):
            for i in range(5):
                n, L = rows[i], keys[i]
                pool.wait_ge(s["mask_ready"], i + 1)
                for h in range(HA):
                    c = HA * i + h
                    if c >= 2:
                        pool.wait_ge(s["lg_out"], c - 1)
                    pool.tensor_tensor(bm[0:n, c % 2, 0:L], toe[0:n, h, 512 - P * i:512 - P * i + L], sc[0:n, i % 2, 0:L],
                                       ALU.add).then_inc(s["bm_ready"], 1)

        @block.vector
        def _(dve):
            step = Chain(dve, s["chain"])

            def choose(i):
                n, L = rows[i], keys[i]
                x = sc[0:n, i % 2, 0:L]
                diag = sc[0:n, i % 2, P * i:L]
                causal = sb["causal"][0:n, 0:L - P * i]
                if i >= 2:
                    dve.wait_ge(s["bm_ready"], HA * (i - 1))
                if i == 0:
                    dve.tensor_copy(diag, causal).then_inc(s["mask_ready"], 1)
                    return
                for h in range(HI):
                    dve.wait_ge(s["relu_out"], relus(i, h) + 1)
                    if h == 0:
                        ins = dve.tensor_scalar(x, relu[0:n, 0, 0:L], sb["wi"][0:n, i, 0:1], None, ALU.mult)
                    else:
                        ins = dve.scalar_tensor_tensor(out=x, in0=relu[0:n, h % 2, 0:L], scalar=sb["wi"][0:n, i, h:h + 1],
                                                       in1=x, op0=ALU.mult, op1=ALU.add)
                    ins.then_inc(s["acc"], 1)
                    dve.wait_ge(s["acc"], relus(i, h) + 1)
                step(dve.tensor_tensor(diag, diag, causal, ALU.add))
                for r in range(TOPP // 8):
                    step(dve.max(best[0:n, r % 2, :], x))
                    step(dve.match_replace(x, best[0:n, r % 2, :], x, TAKEN))
                step(dve.tensor_scalar(x, x, TAKEN, NEG, ALU.not_equal, ALU.mult))
                dve.tensor_tensor(diag, diag, causal, ALU.add).then_inc(s["mask_ready"], 1)

            def soften(i):
                n, L = rows[i], keys[i]
                for h in range(HA):
                    c = HA * i + h
                    x = nth["h", i, h]
                    one = lg[0:n, c % 2, 0:L]
                    dve.wait_ge(s["bm_ready"], c + 1)
                    dve.wait_ge(s["score"], x + 1)
                    if c >= 2:
                        dve.wait_ge(s["turned"], c - 1)
                    dve.tensor_tensor(one, s_ps[x % 2][0:n, 0:L], bm[0:n, c % 2, 0:L], ALU.add).then_inc(s["lg_out"], 1)
                    dve.wait_ge(s["lg_out"], c + 1)
                    dve.tensor_reduce(mx[0:n, c % 2:c % 2 + 1], one, AX.X, ALU.max, negate=True).then_inc(s["lg_ready"], 1)
                    dve.wait_ge(s["exp_ready"], c + 1)
                    step(dve.reciprocal(den[0:n, c % 2:c % 2 + 1], den[0:n, c % 2:c % 2 + 1]))
                    dve.tensor_scalar(one, one, den[0:n, c % 2:c % 2 + 1], None, ALU.mult).then_inc(s["p_ready"], 1)
                dve.wait_ge(s["pv"], HA * (i + 1))
                dve.tensor_copy(outT[:, :, P * i:P * i + n], o_ps[i % 2][:, :, 0:n]).then_inc(s["o_out"], 1)

            for i in range(5):
                choose(i)
                soften(i)

        @block.sync
        def _(sp):
            sp.wait_ge(s["o_out"], 5)
            for h in range(HA):
                sp.dma_start(dram["mixT"][:, TOK * h:TOK * h + TP], outT[:, h, :]).then_inc(s["saved"], 16)
            sp.wait_ge(s["saved"], 16 * HA)


def clear_semaphores(nc, sb):
    with nc.Block() as block:
        @block.gpsimd
        def _(pool):
            pool.sem_clear(range(sb["const_in"].num, bass.NUM_HW_SEMAPHORES))


NROW = TS * HA
NSEL = TOPS + DT
SKEYS = PAST + DT
RING = 8
WINS = 8
ROUNDS_FIRST = 14
AT_SPREAD, AT_PLACES, AT_LOGITS, AT_SOFTMAX, AT_WEIGHTS, AT_VALUES, AT_OUT = 16, 18, 28, 28, 29, 30, 40


def sample_constants():
    r = np.arange(NROW)
    tok, h = r // HA, r % HA
    b, t = tok // DT, tok % DT
    own = (h[:, None, None] == np.arange(HA)[None, :, None]) & (b[:, None, None] == np.arange(TS)[None, None, :] // DT)
    rows = np.concatenate([(np.arange(P) % 32)[:, None], (PAST + t)[:, None], h[:, None] == np.arange(HA),
                           b[:, None] == np.arange(DB), own.reshape(NROW, NROW)], axis=1)
    j = np.arange(TS)
    toks = np.concatenate([j[:, None] == tok[None, :], np.where(np.arange(DT)[None, :] > j[:, None] % DT, NEG, 0.0),
                           np.broadcast_to(PAST + np.arange(DT), (TS, DT))], axis=1)
    return {"c_rows": rows.astype(np.float32), "c_toks": toks.astype(np.float32)}


R_MOD, R_QPOS, R_HEAD, R_BATCH, R_OWN = 0, 1, 2, 2 + HA, 2 + HA + DB
T_REP, T_CAUSAL, T_NEWPOS = 0, NROW, NROW + DT


def sample_scores(nc, dram, consts, sb):
    with ExitStack() as ctx:
        sem = lambda n: ctx.enter_context(nc.semaphore(f"ss_{n}"))
        sbuf = lambda n, s, t=F32: ctx.enter_context(nc.sbuf_tensor(f"ss_{n}", s, t))
        psum = lambda n, s: ctx.enter_context(nc.psum_tensor(f"ss_{n}", s, F32))
        GR, NG = 4, PAST // 512
        pt_i, ptf, offs = sbuf("pt_i", [P, DB * NG], I32), sbuf("ptf", [P, DB * NG]), sbuf("offs", [P, DB * NG], U32)
        raw, laid = sbuf("raw", [P, GR, 2, 4 * DI]), sbuf("laid", [P, 2, 4, 2, DI])
        qs, qbd = sbuf("qs", [P, HI, TS]), sbuf("qbd", [P, 4, 2, HI, DT])
        kn, wi = sbuf("kn", [DT, DB, DI]), sbuf("wi", [TS, HI])
        wt, w = sbuf("wt", [TS, DB, HI, DT]), sbuf("w", [P, 4, TS])
        kiT, knT, relu = sbuf("kiT", [P, 2, 512]), sbuf("knT", [P, 4, DT]), sbuf("relu", [P, 2, 512])
        t_ps, s_ps = [psum(f"t{n}", [P, 4, P]) for n in range(2)], [psum(f"s{n}", [P, 512]) for n in range(2)]
        c_ps = [psum(f"c{n}", [TS, 512]) for n in range(2)]
        names = ("par_in", "q_in", "chain", "offs_ready", "laid", "q_ready", "w_turned", "w_ready", "turned", "kiT_ready",
                 "scored", "relu_ready", "summed", "sc_out", "kn_turned")
        s = {n: sem(n) for n in names}
        keys_in = sb["gathered"][RING:]
        sc = sb["ssc"]
        units = [(g, p) for g in range(NG) for p in range(4)]
        block = ctx.enter_context(nc.Block())

        @block.sync
        def _(sp):
            for q in range(4):
                sp.dma_start(pt_i[32 * q:32 * (q + 1), :], dram["pages_q"][q].partition_broadcast(32)
                             ).then_inc(s["par_in"], 16)
            sp.dma_start(sb["c_rows"][:, :], consts["c_rows"]).then_inc(s["par_in"], 16)
            sp.dma_start(sb["c_toks"][:, :], consts["c_toks"]).then_inc(s["par_in"], 16)
            for x in range(2):
                src = dram["projT"][0:HI * DI, TP:TOK].rearrange("(h d) t -> d h t", d=DI)
                sp.dma_start(qs[64 * x:64 * (x + 1), :, :], src).then_inc(s["q_in"], 16)
            sp.dma_start(kn[:, :, :], dram["projN"][TP:TOK, N_KI:N_KI + DI].rearrange("(b s) d -> s b d", s=DT)
                         ).then_inc(s["q_in"], 16)
            sp.dma_start(wi[:, :], dram["projN"][TP:TOK, N_WI:N_WI + HI]).then_inc(s["q_in"], 16)

        @block.gpsimd
        def _(pool):
            pool.wait_ge(s["offs_ready"], 1)
            table = dram["cache_kidx"][0].rearrange("n (r x) d -> (n r) (x d)", x=4)
            for n, (g, p) in enumerate(units):
                if n >= GR:
                    pool.wait_ge(s["laid"], n - GR + 1)
                for x in range(2):
                    c = (2 * p + x) * NG + g
                    pool.indirect_dma_start(raw[:, n % GR, x, :], None, table,
                                            bass.IndirectOffsetOnAxis(ap=offs[:, c:c + 1], axis=0)
                                            ).then_inc(keys_in[n % GR], 16)

        @block.vector
        def _(dve):
            step = Chain(dve, s["chain"])
            dve.wait_ge(s["par_in"], 96)
            step(dve.tensor_copy(ptf[:, :], pt_i[:, :]))
            step(dve.tensor_scalar(ptf[:, :], ptf[:, :], 32.0, sb["c_rows"][:, R_MOD:R_MOD + 1], ALU.mult, ALU.add))
            dve.tensor_copy(offs[:, :], ptf[:, :]).then_inc(s["offs_ready"], 1)
            step(dve.memset(qbd[:, :, :, :, :], 0.0))
            dve.wait_ge(s["q_in"], 64)
            q5 = qs[:, :, :].rearrange("d h (p x t) -> d p x h t", x=2, t=DT)
            for x in range(2):
                half = slice(64 * x, 64 * (x + 1))
                for p in range(4):
                    last = dve.tensor_copy(qbd[half, p, x], q5[half, p, x])
            last.then_inc(s["q_ready"], 1)
            step(dve.tensor_scalar(wi[:, :], wi[:, :], float(HI * DI) ** -0.5, None, ALU.mult))
            eye = sb["ident"][0:TS, 0:TS].rearrange("p (b t) -> p b t", b=DB).unsqueeze(2)
            step(dve.tensor_copy(wt[:, :, :, :], bc(eye, [TS, DB, HI, DT])))
            for b in range(DB):
                last = dve.tensor_tensor(wt[:, b], wt[:, b], bc(wi[:, :].unsqueeze(2), [TS, HI, DT]), ALU.mult)
            last.then_inc(s["q_ready"], 1)
            dve.wait_ge(s["w_turned"], 1)
            dve.tensor_copy(w[:, :, :], t_ps[0][:, :, 0:TS]).then_inc(s["w_ready"], 1)
            dve.wait_ge(s["kn_turned"], 1)
            dve.tensor_copy(knT[:, :, :], t_ps[1][:, :, 0:DT]).then_inc(s["w_ready"], 1)

            def scores_out(g):
                dve.wait_ge(s["summed"], 4 * g + 4)
                dve.tensor_copy(sc[:, 512 * g:512 * (g + 1)], c_ps[g % 2][:, :]).then_inc(s["sc_out"], 1)

            for n, (g, p) in enumerate(units):
                dve.wait_ge(s["turned"], n + 1)
                if n >= 2:
                    dve.wait_ge(s["scored"], n - 1)
                dve.tensor_copy(kiT[:, n % 2, :].rearrange("p (q r) -> p q r", r=4),
                                t_ps[n % 2][:, :, :].rearrange("p r q -> p q r")).then_inc(s["kiT_ready"], 1)
                if g and p == 1:
                    scores_out(g - 1)
            scores_out(NG - 1)
            dve.wait_ge(s["summed"], len(units) + 1)
            dve.tensor_tensor(sc[:, PAST:], c_ps[0][:, 0:DT], sb["c_toks"][:, T_CAUSAL:T_CAUSAL + DT], ALU.add
                              ).then_inc(s["sc_out"], 1)

        @block.scalar
        def _(act):
            def lay(n):
                act.wait_ge(keys_in[n % GR], 32 * (n // GR + 1))
                if n >= 2:
                    act.wait_ge(s["turned"], n - 1)
                act.activation(laid[:, n % 2], raw[:, n % GR].rearrange("p x (r d) -> p r x d", r=4), ACT.Copy
                               ).then_inc(s["laid"], 1)

            lay(0)
            for n in range(len(units)):
                if n + 1 < len(units):
                    lay(n + 1)
                act.wait_ge(s["scored"], n + 1)
                if n >= 2:
                    act.wait_ge(s["summed"], n - 1)
                act.activation(relu[:, n % 2, :], s_ps[n % 2][:, :], ACT.Relu).then_inc(s["relu_ready"], 1)
            act.wait_ge(s["scored"], len(units) + 1)
            act.wait_ge(s["summed"], len(units))
            act.activation(relu[:, 0, 0:16], s_ps[0][:, 0:16], ACT.Relu).then_inc(s["relu_ready"], 1)

        @block.tensor
        def _(pe):
            eye = sb["ident"]
            pe.wait_ge(s["q_ready"], 2)
            for p in range(4):
                last = pe.transpose(t_ps[0][:, p, 0:TS], wt[:, 2 * p:2 * p + 2].rearrange("j x h t -> j (x h t)"),
                                    eye[0:TS, 0:TS])
            last.then_inc(s["w_turned"], 1)
            for p in range(4):
                last = pe.transpose(t_ps[1][:, p, 0:DT], kn[:, 2 * p:2 * p + 2].rearrange("s x d -> s (x d)"),
                                    eye[0:DT, 0:DT])
            last.then_inc(s["kn_turned"], 1)
            pe.wait_ge(s["w_ready"], 2)

            def turn(n):
                pe.wait_ge(s["laid"], n + 1)
                if n >= 2:
                    pe.wait_ge(s["kiT_ready"], n - 1)
                for r in range(4):
                    last = pe.transpose(t_ps[n % 2][:, r, :], laid[:, n % 2, r].rearrange("p x d -> p (x d)"), eye[:, :])
                last.then_inc(s["turned"], 1)

            def score(n, p):
                pe.wait_ge(s["kiT_ready"], n + 1)
                if n >= 2:
                    pe.wait_ge(s["relu_ready"], n - 1)
                pe.matmul(s_ps[n % 2][:, :], qbd[:, p].rearrange("d x h t -> d (x h t)"), kiT[:, n % 2, :],
                          start=True, stop=True).then_inc(s["scored"], 1)

            def add(n, g, p):
                pe.wait_ge(s["relu_ready"], n + 1)
                if g >= 2 and p == 0:
                    pe.wait_ge(s["sc_out"], g - 1)
                pe.matmul(c_ps[g % 2][:, :], w[:, p, :], relu[:, n % 2, :], start=(p == 0), stop=(p == 3)
                          ).then_inc(s["summed"], 1)

            turn(0)
            for n, (g, p) in enumerate(units):
                if n + 1 < len(units):
                    turn(n + 1)
                score(n, p)
                if n:
                    add(n - 1, *units[n - 1])
            add(n, *units[n])
            pe.wait_ge(s["relu_ready"], len(units))
            pe.wait_ge(s["sc_out"], NG - 1)
            for p in range(4):
                last = pe.matmul(s_ps[0][:, DT * p:DT * (p + 1)], qbd[:, p].rearrange("d x h t -> d (x h t)"),
                                 knT[:, p, :], start=True, stop=True)
            last.then_inc(s["scored"], 1)
            pe.wait_ge(s["relu_ready"], len(units) + 1)
            for p in range(4):
                last = pe.matmul(c_ps[0][:, 0:DT], w[:, p, :], relu[:, 0, DT * p:DT * (p + 1)], start=(p == 0),
                                 stop=(p == 3))
            last.then_inc(s["summed"], 1)


def sample_inputs(nc, dram, sb):
    with ExitStack() as ctx:
        sem = lambda n: ctx.enter_context(nc.semaphore(f"si_{n}"))
        sbuf = lambda n, s: ctx.enter_context(nc.sbuf_tensor(f"si_{n}", s, F32))
        gains, sq, ss = sbuf("gains", [TS, 2, DH]), sbuf("sq", [TS, 8, DH]), sbuf("ss", [TS, 8])
        ps = ctx.enter_context(nc.psum_tensor("si_ps", [P, 8, TS], F32))
        s = {n: sem(n) for n in ("in", "sq", "chain", "summed", "root", "normed", "turned", "out", "saved")}
        qkv = sb["s_qkv"]
        block = ctx.enter_context(nc.Block())

        @block.sync
        def _(sp):
            sp.dma_start(qkv[:, :], dram["projN"][TP:TOK, 0:3 * DA]).then_inc(s["in"], 16)
            for x, name in enumerate(("q_norm", "k_norm")):
                sp.dma_start(gains[:, x, :], dram[name][0].partition_broadcast(TS)).then_inc(s["in"], 16)
            sp.dma_start(sb["relh"][:, :], AP(tensor=dram["rel_bias_t"].tensor, offset=dram["rel_bias_t"].offset,
                                              ap=[[0, TS], [32, HA], [1, 32]])).then_inc(s["in"], 16)
            sp.dma_start(sb["pages"][:, :], AP(tensor=dram["page_table"].tensor, offset=dram["page_table"].offset,
                                               ap=[[PAGES, DB], [0, DT], [1, PAGES]])).then_inc(s["in"], 16)
            sp.wait_ge(s["normed"], 1)
            sp.dma_start(dram["q_rows"], qkv[:, 0:DA]).then_inc(s["saved"], 16)
            sp.wait_ge(s["saved"], 16)

        @block.scalar
        def _(act):
            act.wait_ge(s["in"], 80)
            act.activation(sq[:, :, :], qkv[:, 0:2 * DA].rearrange("p (h e) -> p h e", h=8), ACT.Square
                           ).then_inc(s["sq"], 1)
            act.wait_ge(s["summed"], 1)
            act.activation(ss[:, :], ss[:, :], ACT.Sqrt, bias=sb["eps"][0:TS, 0:1], scale=1.0 / DH
                           ).then_inc(s["root"], 1)

        @block.vector
        def _(dve):
            step = Chain(dve, s["chain"])
            dve.wait_ge(s["in"], 80)
            step(dve.tensor_scalar(gains[:, 0, :], gains[:, 0, :], float(DH) ** -0.5, None, ALU.mult))
            dve.wait_ge(s["sq"], 1)
            dve.tensor_reduce(ss[:, :], sq[:, :, :], AX.X, ALU.add).then_inc(s["summed"], 1)
            dve.wait_ge(s["root"], 1)
            step(dve.reciprocal(ss[:, :], ss[:, :]))
            qk3 = qkv[:, 0:2 * DA].rearrange("p (h e) -> p h e", h=8)
            step(dve.tensor_tensor(qk3, qk3, bc(ss[:, :].unsqueeze(2), [TS, 8, DH]), ALU.mult))
            for x in range(2):
                last = dve.tensor_tensor(qk3[:, 4 * x:4 * x + 4, :], qk3[:, 4 * x:4 * x + 4, :],
                                         bc(gains[:, x:x + 1, :], [TS, 4, DH]), ALU.mult)
            last.then_inc(s["normed"], 1)
            dve.wait_ge(s["turned"], 1)
            dve.tensor_copy(sb["s_qT"][:, :].rearrange("p (t h) -> p h t", h=HA), ps[:, 0:4, :])
            dve.tensor_copy(sb["s_kT"][:, :].rearrange("p (h t) -> p h t", h=HA), ps[:, 4:8, :])

        @block.tensor
        def _(pe):
            pe.wait_ge(s["normed"], 1)
            for x in range(8):
                last = pe.transpose(ps[:, x, :], qkv[:, DH * x:DH * (x + 1)], sb["ident"][0:TS, 0:TS])
            last.then_inc(s["turned"], 1)


class ChooseFirst:

    def __init__(self, nc, sb, rounds):
        self.nc, self.sb, self.rounds = nc, sb, rounds

    def enter(self, ctx):
        self.chain = ctx.enter_context(self.nc.semaphore("cf_chain"))

    def vector(self, dve):
        choose(Chain(dve, self.chain), dve, self.sb, range(self.rounds))

    def tensor(self, pe, strip):
        pass

    def scalar(self, act, strip):
        pass

    def gpsimd(self, pool):
        pass


def choose(step, dve, sb, rounds):
    sc, best, idx = sb["ssc"], sb["best"], sb["idx"]
    for r in rounds:
        step(dve.max(best[:, r % 2, :], sc[:, :]))
        step(dve.max_index(idx[:, 8 * r:8 * r + 8], best[:, r % 2, :], sc[:, :]))
        step(dve.match_replace(sc[:, :], best[:, r % 2, :], sc[:, :], TAKEN))


class AttendSample:

    def __init__(self, nc, dram, sb, first_round):
        self.nc, self.dram, self.sb, self.first_round = nc, dram, sb, first_round

    def enter(self, ctx):
        nc = self.nc
        sbuf = lambda n, s, t=F32: ctx.enter_context(nc.sbuf_tensor(f"as_{n}", s, t))
        psum = lambda n: ctx.enter_context(nc.psum_tensor(f"as_{n}", [P, 512], F32))
        self.pos, self.dead, self.phys, self.hit, self.capped = (
            sbuf(n, [TS, w]) for n, w in (("pos", NSEL), ("dead", NSEL), ("phys", TOPS), ("hit", TOPS), ("capped", TOPS)))
        self.jump, self.offs = sbuf("jump", [TS, PAGES]), sbuf("offs", [P, 2, TS], U32)
        self.drop, self.bias, self.near, self.dist = (
            sbuf(n, [P, w]) for n, w in (("drop", 32), ("bias", NSEL), ("near", NSEL), ("dist", NSEL)))
        self.rows, self.qb, self.prod = sbuf("rows", [P, RING, DA]), sbuf("qb", [P, 4, DA]), sbuf("prod", [P, 2, DA])
        self.lt, self.own, self.p_t = sbuf("lt", [P, 2, NROW]), sbuf("own", [P, NROW]), sbuf("p_t", [P, 2, NROW])
        self.p, self.mx, self.den = sbuf("p", [P, NSEL]), sbuf("mx", [P, 1]), sbuf("den", [P, 1])
        self.pn, self.pnT = sbuf("pn", [P, DB, DT]), sbuf("pnT", [TS, NROW])
        self.win = sbuf("win", [P, WINS, 2 * NROW - HA])
        self.o, self.oT = sbuf("o", [P, DH]), sbuf("oT", [P, HA, TS])
        small, pos_bank, dead_bank, self.o_ps = psum("small"), psum("pos_bank"), psum("dead_bank"), psum("o_bank")
        self.off_ps = small[:, 0:2 * TS].rearrange("p (x t) -> p x t", x=2)
        self.n_ps, self.t_ps = small[:, 128:256], small[:, 256:384]
        self.rep_ps, self.pT_ps = pos_bank[:, 0:NSEL], pos_bank[:, 0:3 * NROW].rearrange("p (x r) -> p x r", x=3)
        self.dead_ps, self.l_ps = dead_bank[:, 0:NSEL], dead_bank[:, 0:2 * NROW]
        names = ("chain", "phys_ready", "pos_ready", "off_turned", "spread", "offs_ready", "own_logits",
                 "multiplied", "reduced", "lt_turned", "mx_ready", "exp_ready", "p_ready", "p_turned", "pT_ready",
                 "win_zeroed", "win_ready", "pv", "o_ready", "o_turned", "oT_ready", "saved")
        self.s = {n: ctx.enter_context(nc.semaphore(f"as_{n}")) for n in names}
        self.rows_in, self.q_in = self.sb["gathered"][0:RING], self.sb["gathered"][RING + 4:RING + 8]
        self.units = [(j, x) for j in range(TS) for x in range(2)]
        self.N = len(self.units)

    def gpsimd(self, pool):
        s, N = self.s, self.N
        pool.memset(self.win[:, :, :], 0.0).then_inc(s["win_zeroed"], 1)
        pool.wait_ge(s["offs_ready"], 1)
        for n in range(2 * N):
            j, x = self.units[n % N]
            table = self.dram["cache_k" if n < N else "cache_v"][0].rearrange("n r h d -> (n r) (h d)")
            if n < N and x == 0:
                if j >= 4:
                    pool.wait_ge(s["multiplied"], 2 * (j - 3))
                pool.dma_start(self.qb[:, j % 4, :], self.dram["q_rows"][j].partition_broadcast(P)
                               ).then_inc(self.q_in[j % 4], 16)
            if RING <= n < N + RING:
                pool.wait_ge(s["multiplied"], n - RING + 1)
            elif n >= N + RING:
                pool.wait_ge(s["pv"], n - N - RING + 1)
            pool.indirect_dma_start(self.rows[:, n % RING, :], None, table,
                                    bass.IndirectOffsetOnAxis(ap=self.offs[:, x, j:j + 1], axis=0)
                                    ).then_inc(self.rows_in[n % RING], 16)
        pool.wait_ge(s["oT_ready"], 1)
        for h in range(HA):
            pool.dma_start(self.dram["mixT"][:, TOK * h + TP:TOK * (h + 1)], self.oT[:, h, :]).then_inc(
                self.sb["gathered"][RING + 8], 16)
        pool.wait_ge(self.sb["gathered"][RING + 8], 16 * HA)

    def vector(self, dve):
        s, N, sb = self.s, self.N, self.sb
        pos, dead, phys, hit, capped, jump = self.pos, self.dead, self.phys, self.hit, self.capped, self.jump
        bias, near, dist, drop, p, o, prod = self.bias, self.near, self.dist, self.drop, self.p, self.o, self.prod
        col = lambda at, n=1: sb["c_rows"][:, at:at + n]
        step = Chain(dve, s["chain"])
        step(dve.tensor_copy(jump[:, :], sb["pages"][:, :]))
        step(dve.tensor_copy(hit[:, 0:PAGES], jump[:, :]))
        step(dve.tensor_tensor(jump[:, 1:], hit[:, 1:PAGES], hit[:, 0:PAGES - 1], ALU.subtract))
        step(dve.tensor_scalar(jump[:, 1:], jump[:, 1:], -1.0, None, ALU.add))
        step(dve.tensor_scalar(jump[:, :], jump[:, :], float(PAGE), None, ALU.mult))
        choose(step, dve, sb, range(self.first_round, TOPS // 8))
        step(dve.tensor_copy(pos[:, 0:TOPS], sb["idx"][:, :]))
        step(dve.tensor_copy(pos[:, TOPS:], sb["c_toks"][:, T_NEWPOS:T_NEWPOS + DT]))
        step(dve.tensor_scalar(dead[:, 0:TOPS], pos[:, 0:TOPS], float(PAST), NEG, ALU.is_ge, ALU.mult))
        dve.tensor_scalar(dead[:, TOPS:], sb["ssc"][:, PAST:], TAKEN, NEG, ALU.not_equal, ALU.mult
                          ).then_inc(s["pos_ready"], 1)
        step(dve.tensor_scalar(capped[:, :], pos[:, 0:TOPS], float(PAST - 1), None, ALU.min))
        step(dve.tensor_scalar(phys[:, :], capped[:, :], jump[:, 0:1], None, ALU.add))
        for g in range(1, PAGES):
            step(dve.tensor_scalar(hit[:, :], capped[:, :], float(PAGE * g), jump[:, g:g + 1], ALU.is_ge, ALU.mult))
            step(dve.tensor_tensor(phys[:, :], phys[:, :], hit[:, :], ALU.add))
        dve.tensor_copy(hit[:, :], phys[:, :]).then_inc(s["phys_ready"], 1)
        dve.wait_ge(s["off_turned"], 1)
        dve.tensor_copy(self.offs[:, :, :], self.off_ps).then_inc(s["offs_ready"], 1)
        dve.wait_ge(s["spread"], 1)
        step(dve.tensor_scalar(dist[:, :], self.rep_ps, col(R_QPOS), -1.0, ALU.subtract, ALU.mult))
        step(dve.tensor_scalar(bias[:, :], self.dead_ps, sb["relh"][:, 31:32], None, ALU.add))
        step(dve.tensor_tensor(drop[:, 1:], sb["relh"][:, 0:31], sb["relh"][:, 1:32], ALU.subtract))
        for b in range(31, 0, -1):
            step(dve.tensor_scalar(near[:, :], dist[:, :], float(BUCKET_FROM[b]), drop[:, b:b + 1], ALU.is_lt,
                                   ALU.mult))
            step(dve.tensor_tensor(bias[:, :], bias[:, :], near[:, :], ALU.add))
        for n, (j, x) in enumerate(self.units):
            dve.wait_ge(self.rows_in[n % RING], 16 * (n // RING + 1))
            dve.wait_ge(self.q_in[j % 4], 16 * (j // 4 + 1))
            if n >= 2:
                dve.wait_ge(s["reduced"], n - 1)
            dve.tensor_tensor(prod[:, n % 2, :], self.rows[:, n % RING, :], self.qb[:, j % 4, :], ALU.mult
                              ).then_inc(s["multiplied"], 1)
            dve.wait_ge(s["multiplied"], n + 1)
            dve.tensor_reduce(self.lt[:, x, HA * j:HA * (j + 1)], prod[:, n % 2, :].rearrange("p (h e) -> p h e", h=HA),
                              AX.X, ALU.add).then_inc(s["reduced"], 1)
        dve.wait_ge(s["own_logits"], 1)
        own = self.own[:, :]
        step(dve.tensor_tensor(own, self.n_ps, col(R_OWN, NROW), ALU.mult))
        step(dve.tensor_reduce(p[:, TOPS:], own.rearrange("p (m s) -> p s m", s=DT), AX.X, ALU.add))
        step(dve.tensor_tensor(p[:, TOPS:], p[:, TOPS:], bias[:, TOPS:], ALU.add))
        dve.wait_ge(s["lt_turned"], 1)
        step(dve.tensor_tensor(p[:, 0:TOPS], self.l_ps, bias[:, 0:TOPS], ALU.add))
        dve.tensor_reduce(self.mx[:, :], p[:, :], AX.X, ALU.max, negate=True).then_inc(s["mx_ready"], 1)
        dve.wait_ge(s["exp_ready"], 1)
        step(dve.reciprocal(self.den[:, :], self.den[:, :]))
        step(dve.tensor_scalar(p[:, :], p[:, :], self.den[:, 0:1], None, ALU.mult))
        dve.tensor_tensor(self.pn[:, :, :], bc(p[:, TOPS:].unsqueeze(1), [P, DB, DT]),
                          bc(col(R_BATCH, DB).unsqueeze(2), [P, DB, DT]), ALU.mult).then_inc(s["p_ready"], 1)
        dve.wait_ge(s["p_turned"], 1)
        dve.tensor_copy(self.p_t[:, :, :], self.pT_ps[:, 0:2, :])
        dve.tensor_copy(self.pnT[:, :], self.pT_ps[0:TS, 2, :]).then_inc(s["pT_ready"], 1)
        dve.wait_ge(s["pv"], N)
        step(dve.tensor_scalar(o[:, :], self.o_ps[:, 0:DH], col(R_HEAD), None, ALU.mult))
        for h in range(1, HA):
            ins = dve.scalar_tensor_tensor(out=o[:, :], in0=self.o_ps[:, DH * h:DH * (h + 1)], scalar=col(R_HEAD + h),
                                           in1=o[:, :], op0=ALU.mult, op1=ALU.add)
            if h < HA - 1:
                step(ins)
            else:
                ins.then_inc(s["o_ready"], 1)
        dve.wait_ge(s["o_turned"], 1)
        dve.tensor_copy(self.oT[:, :, :], self.t_ps.rearrange("p (t h) -> p h t", h=HA)).then_inc(s["oT_ready"], 1)

    def scalar(self, act, strip):
        s = self.s
        if strip == AT_SOFTMAX:
            act.wait_ge(s["mx_ready"], 1)
            act.activation(self.p[:, :], self.p[:, :], ACT.Exp, bias=self.mx[:, 0:1], accum_out=self.den[:, 0:1]
                           ).then_inc(s["exp_ready"], 1)
        if AT_VALUES <= strip < AT_VALUES + self.N // WINS:
            act.wait_ge(s["pT_ready"], 1)
            act.wait_ge(s["win_zeroed"], 1)
            for n in range(WINS * (strip - AT_VALUES), WINS * (strip - AT_VALUES + 1)):
                j, x = self.units[n]
                if n >= WINS:
                    act.wait_ge(s["pv"], n - WINS + 1)
                act.activation(self.win[:, n % WINS, NROW - HA:NROW], self.p_t[:, x, HA * j:HA * (j + 1)], ACT.Copy
                               ).then_inc(s["win_ready"], 1)

    def tensor(self, pe, strip):
        s, sb, N, eye = self.s, self.sb, self.N, self.sb["ident"]
        if strip == AT_SPREAD:
            pe.matmul(self.n_ps, sb["s_qT"][:, :], sb["s_kT"][:, :], start=True, stop=True).then_inc(s["own_logits"], 1)
            pe.wait_ge(s["pos_ready"], 1)
            rep = sb["c_toks"][:, T_REP:T_REP + NROW]
            pe.matmul(self.rep_ps, rep, self.pos[:, :], start=True, stop=True)
            pe.matmul(self.dead_ps, rep, self.dead[:, :], start=True, stop=True).then_inc(s["spread"], 1)
        if strip == AT_PLACES:
            pe.wait_ge(s["phys_ready"], 1)
            for x in range(2):
                last = pe.transpose(self.off_ps[:, x, :], self.hit[:, P * x:P * (x + 1)], eye[0:TS, 0:TS])
            last.then_inc(s["off_turned"], 1)
        if strip == AT_LOGITS:
            pe.wait_ge(s["reduced"], N)
            for x in range(2):
                last = pe.transpose(self.l_ps[:, P * x:P * (x + 1)], self.lt[:, x, :], eye[:, :])
            last.then_inc(s["lt_turned"], 1)
        if strip == AT_WEIGHTS:
            pe.wait_ge(s["p_ready"], 1)
            for x in range(2):
                pe.transpose(self.pT_ps[:, x, :], self.p[:, P * x:P * (x + 1)], eye[:, :])
            pe.transpose(self.pT_ps[0:TS, 2, :], self.pn[:, :, :].rearrange("p b s -> p (b s)"), eye[:, :]
                         ).then_inc(s["p_turned"], 1)
        if strip == AT_VALUES + 1:
            pe.wait_ge(s["pT_ready"], 1)
            pe.matmul(self.o_ps[:, :], self.pnT[:, :], sb["s_qkv"][:, 2 * DA:], start=True, stop=False)
        if AT_VALUES < strip <= AT_VALUES + N // WINS:
            for n in range(WINS * (strip - AT_VALUES - 1), WINS * (strip - AT_VALUES)):
                j, x = self.units[n]
                m = N + n
                pe.wait_ge(s["win_ready"], n + 1)
                pe.wait_ge(self.rows_in[m % RING], 16 * (m // RING + 1))
                at = NROW - HA - HA * j
                pe.matmul(self.o_ps[:, :], self.win[:, n % WINS, at:at + NROW], self.rows[:, m % RING, :], start=False,
                          stop=(n == N - 1)).then_inc(s["pv"], 1)
        if strip == AT_OUT:
            pe.wait_ge(s["o_ready"], 1)
            pe.transpose(self.t_ps, self.o[:, :], eye[:, :]).then_inc(s["o_turned"], 1)


F32R = mybir.dt.float32r
BANKS = 8
GROUPS, GT = 8, FF // 8 // P
CHUNK_W = 2048
PER = GT * P // 128
NOUT = D // 128
PARTS = 2
HIGH = 0xFFFFF000


def output_and_mlp(nc, dram, sb):
    with ExitStack() as ctx:
        sem = lambda n: ctx.enter_context(nc.semaphore(f"om_{n}"))
        sbuf = lambda n, s: ctx.enter_context(nc.sbuf_tensor(f"om_{n}", s, F32))
        x, h, hid = sbuf("x", [P, KT, TOK]), sbuf("h", [P, 2, KT, TOK]), sbuf("hid", [P, 2, GT, TOK])
        ring, raw, relu = sbuf("ring", [P, 2, 2, CHUNK_W]), sbuf("raw", [P, PARTS, CHUNK_W // PARTS]), sbuf("relu", [P, 4, HALF])
        ps = [ctx.enter_context(nc.psum_tensor(f"om_ps{n}", [P, CH], F32)) for n in range(BANKS)]
        raw_in, hi_ready, split = ([sem(f"{n}{q}") for q in range(PARTS)] for n in ("raw_in", "hi_ready", "split"))
        product = [sem(f"product{b}") for b in range(BANKS)]
        evac = [sem(f"evac{b}") for b in range(BANKS)]
        relued = [sem(f"relued{b}") for b in range(BANKS)]
        masked_w = [sem(f"masked_w{q}") for q in range(PARTS)]
        x_in, masked, h_hi, h_lo, sq_ready, summed, root, rstd_ready, scaled, squared, masked_r = (
            sem(n) for n in ("x_in", "masked", "h_hi", "h_lo", "sq_ready", "summed", "root", "rstd_ready", "scaled",
                             "squared", "masked_r"))
        tm_turned, tm_out = sem("tm_turned"), sem("tm_out")
        mix_in = [sem(f"mix_in{q}") for q in range(2)]
        y_out = [sem(f"y_out{i}") for i in range(5)]
        mask, tile, mask_r = sbuf("mask", [P, PARTS, CHUNK_W // PARTS]), sbuf("tile", [P, 2, 2, TOK]), sbuf("mask_r", [P, 2, HALF])
        rstd = relu[:, 0:2, :].rearrange("p h t -> p (h t)")
        bits = lambda ap: ap.bitcast(U32)
        f32r = lambda ap: ap.bitcast(F32R)
        y_tok = lambda i: (raw if i % 2 else mask)[:, :, :].rearrange("p q n -> p (q n)")
        half_of = lambda q: slice(CHUNK_W // PARTS * q, CHUNK_W // PARTS * (q + 1))

        def bank0(c, down):
            return 4 * (c % 2) if down else 2 * (c % 4)

        def filled(base, c, down):
            return base + 2 + c // 2 if down else base + c // 4

        block = ctx.enter_context(nc.Block())

        @block.sync
        def _(sp):
            def load(n, part_of):
                for q in range(PARTS):
                    if not (isinstance(n, int) and n == 0):
                        sp.wait_ge(split[q], n)
                    src = part_of(q)
                    sp.dma_start(raw[:, q, :].rearrange("p (k w) -> p k w", k=src.shape[1]), src).then_inc(raw_in[q], 16)

            mix_t = dram["mixT"].rearrange("p (k t) -> p k t", k=KT)
            out = dram["w_out"][0].rearrange("(q k p) n -> q p k n", q=PARTS, p=P)
            up = dram["w_up"][0].rearrange("(q k p) n -> q p k n", q=PARTS, p=P)
            down = dram["w_down"][0].rearrange("(g q k p) n -> g q p k n", g=GROUPS, q=PARTS, p=P)
            load(0, lambda q: out[q][:, :, 0:128])
            for k in range(KT):
                if k >= 2:
                    sp.wait_ge(h_lo, k - 1)
                sp.dma_start(tile[:, 0, k % 2, :], mix_t[:, k, :]).then_inc(mix_in[k % 2], 16)
            for c in range(1, NOUT):
                load(c, lambda q: out[q][:, :, 128 * c:128 * (c + 1)])
            with sp.Fori(0, GROUPS) as g:
                for c in range(PER):
                    load(g * (2 * PER) + NOUT + c, lambda q: up[q][:, :, bass.ds(g * (GT * P) + 128 * c, 128)])
                for c in range(PER):
                    load(g * (2 * PER) + NOUT + PER + c, lambda q: down[bass.ds(g, 1), q].rearrange(
                        "g p k n -> (g p) k n")[:, :, 256 * c:256 * (c + 1)])

        @block.gpsimd
        def _(pool):
            def lows(n, s):
                for q in range(PARTS):
                    pool.wait_ge(hi_ready[q], n + 1)
                    pool.tensor_tensor(f32r(ring[:, s, 1, half_of(q)]), raw[:, q, :], mask[:, q, :], ALU.subtract
                                       ).then_inc(split[q], 1)

            def tile_lows(n):
                pool.wait_ge(masked, n + 1)
                pool.tensor_tensor(f32r(h[:, 1, n % KT, :]), tile[:, 0, n % 2, :], tile[:, 1, n % 2, :], ALU.subtract
                                   ).then_inc(h_lo, 1)

            lows(0, 0)
            for k in range(KT):
                tile_lows(k)
            for c in range(1, NOUT + 1):
                lows(c, c % 2)
            for k in range(KT):
                tile_lows(KT + k)
            for c in range(1, 2 * PER):
                lows(NOUT + c, c % 2)
            with pool.Fori(1, GROUPS) as g:
                for c in range(2 * PER):
                    lows(g * (2 * PER) + NOUT + c, c % 2)

        @block.tensor
        def _(pe):
            def chunk(n, s, src, kt, bank_a, before, wait=None):
                cols = CHUNK_W // kt
                for m in range(cols // P):
                    for k in range(kt):
                        if m == 0 and k % (kt // PARTS) == 0:
                            pe.wait_ge(split[k // (kt // PARTS)], n + 1)
                        if m == 0 and wait:
                            wait(k)
                        for a, b in ((0, 0), (0, 1), (1, 0)):
                            w = f32r(ring[:, s, a, cols * k + P * m:cols * k + P * (m + 1)])
                            for half in range(2):
                                bank = bank_a + 2 * m + half
                                first, last = k == 0 and a == b == 0, k == kt - 1 and a == 1
                                if first and not (isinstance(before, int) and before == 0):
                                    pe.wait_ge(evac[bank], before)
                                ins = pe.matmul(ps[bank][:, 0:HALF], w, f32r(src[:, b, k, two_halves(half)]),
                                                start=first, stop=last)
                                if last:
                                    ins.then_inc(product[bank], 1)

            def tile_split(n0):
                def wait(k):
                    pe.wait_ge(h_hi, n0 + k + 1)
                    pe.wait_ge(h_lo, n0 + k + 1)
                return wait

            for c in range(NOUT):
                chunk(c, c % 2, h, KT, bank0(c, False), filled(0, c, False), tile_split(0) if c == 0 else None)
            for half in range(2):
                pe.wait_ge(evac[half], NOUT // 4)
            for k in range(KT):
                pe.wait_ge(sq_ready, k + 1)
                for half in range(2):
                    last = pe.matmul(ps[half][:, 0:HALF], sb["ones"][:, :], tile[:, 0, k % 2, two_halves(half)],
                                     start=(k == 0), stop=(k == KT - 1))
                last.then_inc(summed, 1)
            pe.wait_ge(root, 2)
            with pe.Fori(0, GROUPS) as g:
                for c in range(PER):
                    chunk(g * (2 * PER) + NOUT + c, c % 2, h, KT, bank0(c, False), filled(g * 6 + 4, c, False),
                          tile_split(KT) if c == 0 else None)
                for b in range(BANKS):
                    pe.wait_ge(evac[b], g * 6 + 6)
                for c in range(PER):
                    chunk(g * (2 * PER) + NOUT + PER + c, c % 2, hid, GT, bank0(c, True), filled(g * 6 + 4, c, True))
            for b in range(BANKS):
                pe.wait_ge(evac[b], 4 + 6 * GROUPS)
            for n in range(20):
                i, c = n // 4, n % 4
                if n >= BANKS:
                    pe.wait_ge(tm_out, n - BANKS + 1)
                for j in range(4):
                    last = pe.transpose(ps[n % BANKS][0:NT[i], P * j:P * (j + 1)], x[:, 4 * c + j, P * i:P * i + NT[i]],
                                        sb["ident"][:, :])
                last.then_inc(tm_turned, 1)

        @block.vector
        def _(dve):
            def highs(n, s, buffer_free):
                if buffer_free:
                    dve.wait_ge(*buffer_free)
                for q in range(PARTS):
                    dve.wait_ge(raw_in[q], (n + 1) * 16)
                    dve.tensor_scalar(bits(mask[:, q, :]), bits(raw[:, q, :]), HIGH, None, ALU.bitwise_and
                                      ).then_inc(masked_w[q], 1)
                    dve.wait_ge(masked_w[q], n + 1)
                    dve.tensor_copy(f32r(ring[:, s, 0, half_of(q)]), mask[:, q, :]).then_inc(hi_ready[q], 1)

            def add_to_x(tiles, bank_a, before):
                for i, tile in enumerate(tiles):
                    for half in range(2):
                        b = bank_a + 2 * i + half
                        dst = x[:, tile, two_halves(half)]
                        dve.wait_ge(product[b], before + 1)
                        dve.tensor_tensor(dst, dst, ps[b][:, 0:HALF], ALU.add).then_inc(evac[b], 1)

            def hidden(g, c):
                for half in range(2):
                    b = bank0(c, False) + half
                    r, toks, done = relu[:, 2 * (c % 2) + half, :], two_halves(half), g * (2 * PER) + 2 * c + half + 1
                    dve.wait_ge(relued[b], g * 2 + c // 4 + 1)
                    dve.tensor_tensor(r, r, r, ALU.mult).then_inc(squared, 1)
                    dve.wait_ge(squared, done)
                    dve.tensor_scalar(bits(mask_r[:, half, :]), bits(r), HIGH, None, ALU.bitwise_and).then_inc(masked_r, 1)
                    dve.wait_ge(masked_r, done)
                    dve.tensor_copy(f32r(hid[:, 0, c, toks]), mask_r[:, half, :])
                    dve.tensor_tensor(f32r(hid[:, 1, c, toks]), r, mask_r[:, half, :], ALU.subtract
                                      ).then_inc(evac[b], 1)

            def group(g, last):
                base = g * 6 + 4
                for c in range(2 * PER):
                    n, down = g * (2 * PER) + NOUT + c + 1, c > PER
                    before = (7, base) if c == 0 else (bank0(c - 1, False) + 1, filled(base, c - 1, False) + 1) if not down \
                        else (bank0(c - 1 - PER, True) + 3, filled(base, c - 1 - PER, True) + 1)
                    if not (last and c == 2 * PER - 1):
                        highs(n, (c + 1) % 2, (product[before[0]], before[1]))
                    if c < PER:
                        hidden(g, c)
                    else:
                        d = c - PER
                        add_to_x((2 * d, 2 * d + 1), bank0(d, True), filled(base, d, True))

            def mask_tile(n):
                if n >= 2:
                    dve.wait_ge(h_hi, n - 1)
                    dve.wait_ge(h_lo, n - 1)
                dve.tensor_scalar(bits(tile[:, 1, n % 2, :]), bits(tile[:, 0, n % 2, :]), HIGH, None, ALU.bitwise_and
                                  ).then_inc(masked, 1)

            highs(0, 0, None)
            for k in range(KT):
                dve.wait_ge(mix_in[k % 2], 16 * (k // 2 + 1))
                mask_tile(k)
            dve.wait_ge(x_in, 16)
            for c in range(NOUT):
                highs(c + 1, (c + 1) % 2, (product[bank0(c - 1, False) + 1], filled(0, c - 1, False) + 1) if c else None)
                add_to_x((c,), bank0(c, False), filled(0, c, False))
            dve.wait_ge(root, 2)
            dve.reciprocal(rstd, rstd).then_inc(rstd_ready, 1)
            dve.wait_ge(rstd_ready, 1)
            for k in range(KT):
                if k >= 2:
                    dve.wait_ge(h_lo, KT + k - 1)
                dve.scalar_tensor_tensor(out=tile[:, 0, k % 2, :], in0=x[:, k, :], scalar=sb["g_mlp"][:, k:k + 1],
                                         in1=rstd, op0=ALU.mult, op1=ALU.mult).then_inc(scaled, 1)
                dve.wait_ge(scaled, k + 1)
                mask_tile(KT + k)
            with dve.Fori(0, GROUPS - 1) as g:
                group(g, False)
            group(GROUPS - 1, True)
            for n in range(20):
                i, c = n // 4, n % 4
                dve.wait_ge(tm_turned, n + 1)
                if c == 0 and i >= 2:
                    dve.wait_ge(y_out[i - 2], 16)
                dve.tensor_copy(y_tok(i)[0:NT[i], 512 * c:512 * (c + 1)], ps[n % BANKS][0:NT[i], :]).then_inc(tm_out, 1)

        @block.scalar
        def _(act):
            act.dma_start(x[:, :, :].rearrange("p k t -> p (k t)"), dram["xT"]).then_inc(x_in, 16)

            def tile_high(n):
                act.wait_ge(masked, n + 1)
                act.activation(f32r(h[:, 0, n % KT, :]), tile[:, 1, n % 2, :], ACT.Copy).then_inc(h_hi, 1)

            for k in range(KT):
                tile_high(k)
            act.wait_ge(h_lo, KT)
            for k in range(KT):
                for half in range(2):
                    act.wait_ge(evac[bank0(k, False) + half], k // 4 + 1)
                if k >= 2:
                    act.wait_ge(summed, k - 1)
                act.activation(tile[:, 0, k % 2, :], x[:, k, :], ACT.Square).then_inc(sq_ready, 1)
            act.wait_ge(summed, KT)
            for half in range(2):
                act.activation(rstd[:, two_halves(half)], ps[half][:, 0:HALF], ACT.Sqrt, bias=sb["eps"][:, 0:1],
                               scale=1.0 / D).then_inc(root, 1)
            for k in range(KT):
                tile_high(KT + k)
            with act.Fori(0, GROUPS) as g:
                for c in range(PER):
                    for half in range(2):
                        b, b2 = bank0(c, False) + half, bank0(c - 2, False) + half
                        act.wait_ge(evac[b2], filled(g * 6 + 4, c - 2, False) + 1)
                        act.wait_ge(product[b], filled(g * 6 + 4, c, False) + 1)
                        act.activation(relu[:, 2 * (c % 2) + half, :], ps[b][:, 0:HALF], ACT.Relu).then_inc(relued[b], 1)
            for i in range(5):
                act.wait_ge(tm_out, 4 * i + 4)
                yp, ys, rows = dram["y_prompt"][0], dram["y_sample"].rearrange("b t d -> (b t) d"), y_tok(i)
                if i == 0:
                    act.dma_start(yp[0:P - META, :], rows[META:, :]).then_inc(y_out[i], 16)
                elif i < 4:
                    act.dma_start(yp[P * i - META:P * (i + 1) - META, :], rows).then_inc(y_out[i], 16)
                else:
                    act.dma_start(yp[SEQ - TAILP:, :], rows[0:TAILP, :]).then_inc(y_out[i], 16)
                    act.dma_start(ys, rows[TAILP:TAIL, :]).then_inc(y_out[i], 16)
            for i in range(5):
                act.wait_ge(y_out[i], 32 if i == 4 else 16)


def build(nc, dram, consts):
    with ExitStack() as ctx:
        sbuf = lambda n, s, t=F32: ctx.enter_context(nc.sbuf_tensor(n, s, t))
        sb = {}
        for name, cols in (("ident", P), ("ones", P), ("eps", 1)):
            sb[name] = sbuf(name, [P, cols])
        sb["g_mix"], sb["g_mlp"] = sbuf("g_mix", [P, KT]), sbuf("g_mlp", [P, KT])
        sb["gathered"] = [ctx.enter_context(nc.semaphore(f"gathered{n}")) for n in range(RING + 9)]
        const_in = sb["const_in"] = ctx.enter_context(nc.semaphore("const_in"))
        sb["n_const"] = 4
        with nc.Block() as block:
            @block.sync
            def _(sp):
                sp.dma_start(sb["ident"][:, :], consts["c_ident"]).then_inc(const_in, 16)
                sp.dma_start(sb["ones"][:, :], consts["c_ones"]).then_inc(const_in, 16)
                sp.dma_start(sb["g_mix"][:, :], dram["norm_mix_t"]).then_inc(const_in, 16)
                sp.dma_start(sb["g_mlp"][:, :], dram["norm_mlp_t"]).then_inc(const_in, 16)

            @block.vector
            def _(dve):
                dve.memset(sb["eps"][:, :], EPS)

        with nc.sbuf_tensor("hT", [P, KT, TOK], F32) as hT:
            sb["hT"] = hT
            with nc.sbuf_tensor("xT", [P, KT, TOK], F32) as xT:
                sb["xT"] = xT
                load_and_norm(nc, dram, sb)
            with ExitStack() as sample:
                own = lambda n, s, t=F32: sample.enter_context(nc.sbuf_tensor(f"sm_{n}", s, t))
                for name, shape in (("ssc", [TS, SKEYS]), ("c_rows", [P, R_OWN + NROW]), ("c_toks", [TS, T_NEWPOS + DT]),
                                    ("s_qkv", [TS, 3 * DA]), ("s_qT", [P, NROW]), ("s_kT", [P, NROW]), ("relh", [P, 32]),
                                    ("best", [TS, 2, 8])):
                    sb[name] = own(name, shape)
                sb["pages"], sb["idx"] = own("pages", [TS, PAGES], I32), own("idx", [TS, TOPS], U32)
                sb["ring"] = own("w_ring", [P, 2, KT, CH])
                plan = chunk_plan()
                project_in(nc, dram, sb, plan[0:3], "pi")
                sample_scores(nc, dram, consts, sb)
                project_in(nc, dram, sb, plan[3:6], "pq", ChooseFirst(nc, sb, ROUNDS_FIRST))
                sample_inputs(nc, dram, sb)
                project_in(nc, dram, sb, plan[6:], "pm", AttendSample(nc, dram, sb, ROUNDS_FIRST))
        clear_semaphores(nc, sb)
        with ExitStack() as scans:
            own = lambda n, s: scans.enter_context(nc.sbuf_tensor(n, s, F32))
            sb["tm"] = own("tm", [P, 5, TM_COLS])
            for name, shape in (("g", [P, 5, 18]), ("dt", [P, 5, 12]), ("beta", [P, 5, 6]), ("cum", [P, 5, 36]),
                                ("eq", [P, 5, 18]), ("ecum", [P, 5, 18]), ("wend", [P, 5, 18]), ("el", [P, 13, 18]),
                                ("ssm_d", [P, 12]), ("upto", [P, 2 * P]), ("same", [P, 2 * P]), ("members", [P, 9]),
                                ("y_ssd", [P, 5, DBm]), ("y_gdn", [P, 5, DC])):
                sb[name] = own(name, shape)
            with nc.sbuf_tensor("bcT", [P, 4, TOK], F32) as bcT:
                sb["bcT"] = bcT
                convolve(nc, dram, sb)
                gates(nc, dram, consts, sb)
                ssd_scan(nc, dram, sb)
            with ExitStack() as delta:
                for name, shape in (("kbq", [P, HC, 2, TOK]), ("atT", [P, HC, TOK]), ("ttT", [P, HC, TOK]), ("rn", [P, 5, 12])):
                    sb[name] = delta.enter_context(nc.sbuf_tensor(name, shape, F32))
                gdn_prepare(nc, dram, consts, sb)
                gdn_scan(nc, dram, sb)
            clear_semaphores(nc, sb)
            gate_and_norm(nc, dram, sb)
        with ExitStack() as attention:
            own = lambda n, s: attention.enter_context(nc.sbuf_tensor(n, s, F32))
            for name, shape in (("qT", [P, HA, TOK]), ("kT", [P, HA, TOK]), ("kiT", [P, TOK]), ("qiT", [P, 8, TOK]),
                                ("v_tok", [P, 5, DA]), ("wi", [P, 5, HI]), ("toe", [P, HA, 640]), ("causal", [P, P])):
                sb[name] = own(name, shape)
            attention_inputs(nc, dram, consts, sb)
            attend_prompt(nc, dram, sb)
        clear_semaphores(nc, sb)
        output_and_mlp(nc, dram, sb)


_INS = ["x_prompt", "x_sample", "cache_k", "cache_v", "cache_kidx", "page_table", "state_ssm_conv", "state_ssm",
        "state_gdn_conv", "state_gdn", "meta_tokens", "rel_bias", "norm_mix", "w_in", "q_norm", "k_norm",
        "ssm_conv_w", "ssm_conv_b", "ssm_dt_bias", "ssm_A_log", "ssm_D", "ssm_norm", "gdn_conv_w", "gdn_dt_bias",
        "gdn_A_log", "gdn_norm", "w_out", "norm_mlp", "w_up", "w_down"]
_LAID_OUT = ("norm_mix", "norm_mlp", "ssm_conv_w", "ssm_conv_b", "gdn_conv_w", "state_ssm_conv", "state_gdn_conv")
_OUTS = [
    ("y_prompt", (1, SEQ, D)), ("y_sample", (DB, DT, D)),
    ("k_prompt", (1, 1, TP, HA, DH)), ("v_prompt", (1, 1, TP, HA, DH)), ("kidx_prompt", (1, 1, TP, DI)),
    ("k_sample", (1, DB, DT, HA, DH)), ("v_sample", (1, DB, DT, HA, DH)), ("kidx_sample", (1, DB, DT, DI)),
    ("ssm_conv_prompt", (1, 1, 3, CB)), ("ssm_prompt", (1, 1, HB, PB, NB)),
    ("ssm_conv_sample", (1, DB, 3, CB)), ("ssm_sample", (1, DB, HB, PB, NB)),
    ("gdn_conv_prompt", (1, 1, 3, CC)), ("gdn_prompt", (1, 1, HC, DK, DK)),
    ("gdn_conv_sample", (1, DB, 3, CC)), ("gdn_sample", (1, DB, HC, DK, DK)),
]


def kernel(**inputs):
    import numpy as _np
    import concourse.bacc as _bacc
    from concourse import mybir as _mybir
    from concourse.bass_utils import run_bass_kernel_spmd as _run

    nc = _bacc.Bacc("TRN2", target_bir_lowering=False, num_devices=1)
    arrays, dram, consts = {}, {}, {}

    def given(name, a):
        arrays[name] = a
        return nc.dram_tensor(name, a.shape, _mybir.dt.from_np(a.dtype), kind="ExternalInput").ap()

    for name in _INS:
        if name not in _LAID_OUT:
            dram[name] = given(f"in_{name}", _np.ascontiguousarray(inputs[name]))
    for name in ("norm_mix", "norm_mlp"):
        dram[f"{name}_t"] = given(f"in_{name}_t", _np.ascontiguousarray(inputs[name].reshape(KT, P).T))
    taps = _np.concatenate([inputs["ssm_conv_w"][0], inputs["gdn_conv_w"][0]], axis=1)
    bias = _np.concatenate([inputs["ssm_conv_b"][0], _np.zeros(CC, _np.float32)])
    conv = _np.concatenate([taps, bias[None]], axis=0).reshape(5, NCONV, P).transpose(2, 1, 0)
    dram["conv_par"] = given("in_conv_par", _np.ascontiguousarray(conv))
    state = _np.concatenate([inputs["state_ssm_conv"][0], inputs["state_gdn_conv"][0]], axis=2)
    state = state.reshape(DB, 3, NCONV, P).transpose(3, 2, 0, 1)
    dram["conv_state"] = given("in_conv_state", _np.ascontiguousarray(state))
    pages = inputs["page_table"].reshape(DB, PAGES // 4, 4).transpose(2, 0, 1)
    dram["pages_q"] = given("in_pages_q", _np.ascontiguousarray(pages.reshape(4, DB * PAGES // 4)))
    dram["rel_bias_t"] = given("in_rel_bias_t", _np.ascontiguousarray(inputs["rel_bias"].T))
    for name, a in {**constants(), **sample_constants()}.items():
        consts[name] = given(name, a)
    for name, shape in _OUTS:
        dram[name] = nc.dram_tensor(f"out_{name}", shape, F32, kind="ExternalOutput").ap()
    dram["projT"] = nc.dram_tensor("projT", (R_CONV + NCONV * P, TOK), F32).ap()
    dram["projN"] = nc.dram_tensor("projN", (TOK, NTM), F32).ap()
    dram["skew"] = nc.dram_tensor("skew", (HA, P * 768), F32).ap()
    dram["q_rows"] = nc.dram_tensor("q_rows", (TS, DA), F32).ap()
    dram["xT"] = nc.dram_tensor("xT_scratch", (P, KT * TOK), F32).ap()
    dram["mixT"] = nc.dram_tensor("mixT_scratch", (P, KT * TOK), F32).ap()
    build(nc, dram, consts)
    r = _run(nc, [arrays], core_ids=[0])
    return tuple(r.results[0][f"out_{name}"] for name, _ in _OUTS)
```
